# Optimizing a Trainium2 kernel written in Bass

```python
import math
import jax, jax.numpy as jnp
from jax import lax
import numpy as np

D_MODEL = 1024
BATCH = 1
SEQ = 512
DEPTH = 2

N_MEM = 256
DN_HEADS = 4
DN_DK = 128
DN_DV = 128
DN_CONV = 4
DN_CHUNK = 64
SWA_HEADS = 8
SWA_KV_HEADS = 2
SWA_DH = 64
WINDOW = 128
XA_HEADS = 4
XA_DH = 128
D_FF = 2816
N_BRANCH = 3
BRANCH_W = 512
DEEPNORM_ALPHA = (2 * DEPTH) ** 0.25
DEEPNORM_BETA = (8 * DEPTH) ** -0.25
LN_EPS = 1e-5
RMS_EPS = 1e-6
NEG_INF = -1e30
IN_SPLITS = (DN_HEADS * DN_DK, DN_HEADS * DN_DK, DN_HEADS * DN_DV, DN_HEADS, DN_HEADS,
             DN_HEADS * DN_DV, SWA_HEADS * SWA_DH, SWA_KV_HEADS * SWA_DH, SWA_KV_HEADS * SWA_DH,
             XA_HEADS * XA_DH, N_BRANCH * D_MODEL)
D_IN = sum(IN_SPLITS)
VALUE_SEGMENTS = (2, 8)


def layer_norm(x, g, b):
    xf = x.astype(jnp.float32)
    mu = xf.mean(-1, keepdims=True)
    var = jnp.square(xf - mu).mean(-1, keepdims=True)
    return ((xf - mu) * lax.rsqrt(var + LN_EPS) * g.astype(jnp.float32) + b.astype(jnp.float32)).astype(x.dtype)

def swiglu(x, w_gu, w_down):
    gate, up = jnp.split(x @ w_gu, 2, axis=-1)
    return (jax.nn.silu(gate) * up) @ w_down

def causal_depthwise_conv(x, w):
    K, C = w.shape
    return lax.conv_general_dilated(x, w[:, None, :].astype(x.dtype), window_strides=(1,),
                                    padding=[(K - 1, 0)], dimension_numbers=('NWC', 'WIO', 'NWC'),
                                    feature_group_count=C)

def gated_delta_rule(q, k, v, g, beta):
    f32 = jnp.float32
    B_, S_, H, dk = q.shape
    dv = v.shape[-1]
    C = DN_CHUNK
    N = S_ // C

    def chunks(t):
        t = t.astype(f32).reshape((B_, N, C, H) + t.shape[3:])
        return jnp.moveaxis(t, 3, 1)

    q = chunks(q) * (dk ** -0.5)
    k, v, beta, g = chunks(k), chunks(v), chunks(beta), chunks(g)
    g = jnp.cumsum(g, axis=-1)
    tril = jnp.tril(jnp.ones((C, C), bool))
    strict = jnp.tril(jnp.ones((C, C), bool), -1)
    decay = jnp.exp(jnp.where(tril, g[..., :, None] - g[..., None, :], NEG_INF))

    k_beta = k * beta[..., None]
    a = jnp.where(strict, jnp.einsum('bhncd,bhnsd->bhncs', k_beta, k) * decay, 0.0)
    t_mat = a + jnp.eye(C, dtype=f32)
    rhs = jnp.concatenate([v * beta[..., None], k_beta * jnp.exp(g)[..., None]], axis=-1)
    sol = lax.linalg.triangular_solve(t_mat, rhs, left_side=True, lower=True, unit_diagonal=True)
    u, w = sol[..., :dv], sol[..., dv:]

    qk = jnp.where(tril, jnp.einsum('bhncd,bhnsd->bhncs', q, k) * decay, 0.0)
    g_last = g[..., -1]
    k_tail = k * jnp.exp(g_last[..., None] - g)[..., None]
    q_dec = q * jnp.exp(g)[..., None]

    def step(S, xs):
        q_i, qk_i, u_i, w_i, kt_i, gl_i = xs
        v_new = u_i - jnp.einsum('bhcd,bhde->bhce', w_i, S)
        o = jnp.einsum('bhcd,bhde->bhce', q_i, S) + jnp.einsum('bhcs,bhse->bhce', qk_i, v_new)
        S = S * jnp.exp(gl_i)[..., None, None] + jnp.einsum('bhcd,bhce->bhde', kt_i, v_new)
        return S, o

    xs = tuple(jnp.moveaxis(t, 2, 0) for t in (q_dec, qk, u, w, k_tail, g_last))
    S0 = jnp.zeros((B_, H, dk, dv), f32)
    _, o = lax.scan(step, S0, xs)
    o = jnp.moveaxis(o, 0, 2)
    return jnp.moveaxis(o, 1, 3).reshape(B_, S_, H, dv)

def deltanet_branch(q, k, v, b, a, z, conv_w, a_log, dt_bias, norm_w):
    f32 = jnp.float32
    B_, S_, _ = q.shape
    qkv = jax.nn.silu(causal_depthwise_conv(jnp.concatenate([q, k, v], axis=-1), conv_w))
    q, k, v = jnp.split(qkv.astype(f32), 3, axis=-1)
    q = q.reshape(B_, S_, DN_HEADS, DN_DK)
    k = k.reshape(B_, S_, DN_HEADS, DN_DK)
    v = v.reshape(B_, S_, DN_HEADS, DN_DV)
    q = q * lax.rsqrt(jnp.sum(q * q, -1, keepdims=True) + RMS_EPS)
    k = k * lax.rsqrt(jnp.sum(k * k, -1, keepdims=True) + RMS_EPS)
    beta = jax.nn.sigmoid(b.astype(f32))
    g = -jnp.exp(a_log.astype(f32)) * jax.nn.softplus(a.astype(f32) + dt_bias.astype(f32))
    o = gated_delta_rule(q, k, v, g, beta)
    o = o * lax.rsqrt(jnp.mean(o * o, -1, keepdims=True) + RMS_EPS) * norm_w.astype(f32)
    o = o * jax.nn.silu(z.astype(f32).reshape(B_, S_, DN_HEADS, DN_DV))
    return o.reshape(B_, S_, DN_HEADS * DN_DV).astype(z.dtype)

def sliding_window_attention(q, k, v, sinks):
    f32 = jnp.float32
    B_, S_, _ = q.shape
    Hkv, G, dh, W = SWA_KV_HEADS, SWA_HEADS // SWA_KV_HEADS, SWA_DH, WINDOW
    nb = S_ // W
    qb = q.reshape(B_, nb, W, Hkv, G, dh)

    def band(t):
        tb = t.reshape(B_, nb, W, Hkv, dh)
        prev = jnp.pad(tb[:, :-1], ((0, 0), (1, 0), (0, 0), (0, 0), (0, 0)))
        return jnp.concatenate([prev, tb], axis=2)

    kb, vb = band(k), band(v)
    s = jnp.einsum('bnqhgd,bnkhd->bnhgqk', qb, kb).astype(f32) * (dh ** -0.5)
    q_pos = jnp.arange(nb)[:, None] * W + jnp.arange(W)[None, :]
    k_pos = jnp.arange(nb)[:, None] * W - W + jnp.arange(2 * W)[None, :]
    diff = q_pos[:, :, None] - k_pos[:, None, :]
    mask = (diff >= 0) & (diff < W) & (k_pos[:, None, :] >= 0)
    s = jnp.where(mask[None, :, None, None], s, NEG_INF)
    sink = sinks.astype(f32).reshape(Hkv, G)[None, None, :, :, None, None]
    m = jnp.maximum(s.max(-1, keepdims=True), sink)
    p = jnp.exp(s - m)
    p = p / (p.sum(-1, keepdims=True) + jnp.exp(sink - m))
    o = jnp.einsum('bnhgqk,bnkhd->bnqhgd', p.astype(v.dtype), vb)
    return o.reshape(B_, S_, SWA_HEADS * dh)

def memory_cross_attention(q, mem_n, w_mem_kv):
    B_, S_, _ = q.shape
    M = mem_n.shape[1]
    k, v = jnp.split(mem_n @ w_mem_kv, 2, axis=-1)
    k = k.reshape(B_, M, XA_HEADS, XA_DH)
    v = v.reshape(B_, M, XA_HEADS, XA_DH)
    q = q.reshape(B_, S_, XA_HEADS, XA_DH)
    s = jnp.einsum('bshd,bmhd->bhsm', q, k).astype(jnp.float32) * (XA_DH ** -0.5)
    p = jax.nn.softmax(s, axis=-1)
    o = jnp.einsum('bhsm,bmhd->bshd', p.astype(v.dtype), v)
    return o.reshape(B_, S_, XA_HEADS * XA_DH)

def hybrid_layer(x, mem_n, ln_g, ln_b, ffn1_w_gu, ffn1_w_down, w_in, dn_conv_w, dn_a_log,
                 dn_dt_bias, dn_norm_w, swa_sinks, w_mem_kv, w_branch, w_out, ffn2_w_gu, ffn2_w_down):
    B_, S_, D = x.shape
    h = layer_norm(DEEPNORM_ALPHA * x + 0.5 * swiglu(x, ffn1_w_gu, ffn1_w_down), ln_g[0], ln_b[0])
    split_idx = [int(i) for i in np.cumsum(IN_SPLITS)[:-1]]
    (dn_q, dn_k, dn_v, dn_b, dn_a, dn_z, sw_q, sw_k, sw_v, xa_q, gates) = jnp.split(h @ w_in, split_idx, axis=-1)
    o_dn = deltanet_branch(dn_q, dn_k, dn_v, dn_b, dn_a, dn_z, dn_conv_w, dn_a_log, dn_dt_bias, dn_norm_w)
    o_sw = sliding_window_attention(sw_q, sw_k, sw_v, swa_sinks)
    o_xa = memory_cross_attention(xa_q, mem_n, w_mem_kv)
    branches = jnp.stack([o_dn, o_sw, o_xa], axis=2)
    gates = jax.nn.sigmoid(gates.reshape(B_, S_, N_BRANCH, D))
    merged = jnp.sum(gates * jnp.einsum('bsnc,ncd->bsnd', branches, w_branch), axis=2)
    h = layer_norm(DEEPNORM_ALPHA * h + merged @ w_out, ln_g[1], ln_b[1])
    return layer_norm(DEEPNORM_ALPHA * h + 0.5 * swiglu(h, ffn2_w_gu, ffn2_w_down), ln_g[2], ln_b[2])

def first_inputs(seed: int = 0) -> dict:
    key = jax.random.key(seed)
    ks = jax.random.split(key, 20)
    f32 = jnp.float32
    nrm = lambda k, shape, s: jax.random.normal(k, shape, f32) * s
    col_scale = np.concatenate([np.full(n, DEEPNORM_BETA if i in VALUE_SEGMENTS else 1.0, np.float32)
                                for i, n in enumerate(IN_SPLITS)])
    kv_scale = np.concatenate([np.ones(XA_HEADS * XA_DH, np.float32),
                               np.full(XA_HEADS * XA_DH, DEEPNORM_BETA, np.float32)])
    dt = jnp.exp(jax.random.uniform(ks[9], (DEPTH, DN_HEADS), f32, math.log(1e-3), math.log(1e-1)))
    return {
        "x": nrm(ks[0], (BATCH, SEQ, D_MODEL), 1.0),
        "mem": nrm(ks[1], (BATCH, N_MEM, D_MODEL), 1.0),
        "mem_ln_g": 1.0 + nrm(ks[2], (D_MODEL,), 0.02),
        "mem_ln_b": nrm(ks[3], (D_MODEL,), 0.02),
        "ln_g": 1.0 + nrm(ks[4], (DEPTH, 3, D_MODEL), 0.02),
        "ln_b": nrm(ks[5], (DEPTH, 3, D_MODEL), 0.02),
        "ffn1_w_gu": nrm(ks[6], (DEPTH, D_MODEL, 2 * D_FF), DEEPNORM_BETA * D_MODEL ** -0.5),
        "ffn1_w_down": nrm(ks[7], (DEPTH, D_FF, D_MODEL), DEEPNORM_BETA * D_FF ** -0.5),
        "w_in": nrm(ks[8], (DEPTH, D_MODEL, D_IN), D_MODEL ** -0.5) * jnp.asarray(col_scale),
        "dn_conv_w": nrm(ks[10], (DEPTH, DN_CONV, 3 * DN_HEADS * DN_DK), DN_CONV ** -0.5),
        "dn_a_log": jnp.log(jax.random.uniform(ks[11], (DEPTH, DN_HEADS), f32, 1.0, 16.0)),
        "dn_dt_bias": dt + jnp.log(-jnp.expm1(-dt)),
        "dn_norm_w": 1.0 + nrm(ks[12], (DEPTH, DN_DV), 0.02),
        "swa_sinks": nrm(ks[13], (DEPTH, SWA_HEADS), 0.5),
        "w_mem_kv": nrm(ks[14], (DEPTH, D_MODEL, 2 * XA_HEADS * XA_DH), D_MODEL ** -0.5) * jnp.asarray(kv_scale),
        "w_branch": nrm(ks[15], (DEPTH, N_BRANCH, BRANCH_W, D_MODEL), DEEPNORM_BETA * BRANCH_W ** -0.5),
        "w_out": nrm(ks[16], (DEPTH, D_MODEL, D_MODEL), DEEPNORM_BETA * D_MODEL ** -0.5),
        "ffn2_w_gu": nrm(ks[17], (DEPTH, D_MODEL, 2 * D_FF), DEEPNORM_BETA * D_MODEL ** -0.5),
        "ffn2_w_down": nrm(ks[18], (DEPTH, D_FF, D_MODEL), DEEPNORM_BETA * D_FF ** -0.5),
    }

def first_block(x, mem, mem_ln_g, mem_ln_b, ln_g, ln_b, ffn1_w_gu, ffn1_w_down, w_in, dn_conv_w,
              dn_a_log, dn_dt_bias, dn_norm_w, swa_sinks, w_mem_kv, w_branch, w_out, ffn2_w_gu, ffn2_w_down):
    mem_n = layer_norm(mem, mem_ln_g, mem_ln_b)
    for l in range(DEPTH):
        x = hybrid_layer(x, mem_n, ln_g[l], ln_b[l], ffn1_w_gu[l], ffn1_w_down[l], w_in[l], dn_conv_w[l],
                         dn_a_log[l], dn_dt_bias[l], dn_norm_w[l], swa_sinks[l], w_mem_kv[l], w_branch[l],
                         w_out[l], ffn2_w_gu[l], ffn2_w_down[l])
    return x


DEPTH_2 = 1

HEAD_DIM = 64
N_SB = 4
N_MOBA = 4
N_FOX = 4
N_DSA = 4
BRANCH_W_2 = 4 * HEAD_DIM
N_BRANCH_2 = 4
Q_BLOCK = 128
MOBA_BLOCK = 256
MOBA_TOPK = 3
MOBA_Q_CHUNK = 32
DSA_TOPK = 256
IDX_HEADS = 8
IDX_DIM = 32
T5_BUCKETS = 32
T5_MAX_DIST = 128
CONV_W = 3
NEG_BIG = -1e30

IN_SIZES = (
    [BRANCH_W_2] * 3
    + [BRANCH_W_2] * 3
    + [BRANCH_W_2] * 3 + [N_FOX]
    + [BRANCH_W_2, HEAD_DIM, HEAD_DIM]
    + [IDX_HEADS * IDX_DIM, IDX_DIM, IDX_HEADS]
)
P_IN = int(sum(IN_SIZES))
IN_SPLITS_2 = tuple(int(v) for v in np.cumsum(IN_SIZES)[:-1])


def rmsnorm(x, g):
    xf = x.astype(jnp.float32)
    y = xf * lax.rsqrt(jnp.mean(xf * xf, axis=-1, keepdims=True) + RMS_EPS)
    return (y * g.astype(jnp.float32)).astype(x.dtype)

def to_heads(t, n):
    b, s, _ = t.shape
    return t.reshape(b, s, n, HEAD_DIM).transpose(0, 2, 1, 3)

def merge_heads(o):
    b, h, s, d = o.shape
    return o.transpose(0, 2, 1, 3).reshape(b, s, h * d)

def t5_bucket(n):
    n = jnp.maximum(n, 0)
    max_exact = T5_BUCKETS // 2
    nf = jnp.maximum(n, 1).astype(jnp.float32)
    large = max_exact + (jnp.log(nf / max_exact) / math.log(T5_MAX_DIST / max_exact)
                         * (T5_BUCKETS - max_exact)).astype(jnp.int32)
    large = jnp.minimum(large, T5_BUCKETS - 1)
    return jnp.where(n < max_exact, n, large)

def stick_breaking_attention(q, k, v):
    s_len = q.shape[2]
    scale = HEAD_DIM ** -0.5
    outs = []
    for i in range(s_len // Q_BLOCK):
        t0, t1 = i * Q_BLOCK, (i + 1) * Q_BLOCK
        z = jnp.einsum('bhqd,bhkd->bhqk', q[:, :, t0:t1], k[:, :, :t1]).astype(jnp.float32) * scale
        strict = jnp.arange(t1)[None, :] < jnp.arange(t0, t1)[:, None]
        log_neg = jnp.where(strict, jax.nn.log_sigmoid(-z), 0.0)
        excl = lax.cumsum(log_neg, axis=3, reverse=True) - log_neg
        w = jnp.where(strict, jnp.exp(jax.nn.log_sigmoid(z) + excl), 0.0)
        outs.append(jnp.einsum('bhqk,bhkd->bhqd', w.astype(v.dtype), v[:, :, :t1]))
    return jnp.concatenate(outs, axis=2)

def forgetting_attention(q, k, v, f_logit):
    s_len = q.shape[2]
    scale = HEAD_DIM ** -0.5
    c = jnp.cumsum(jax.nn.log_sigmoid(f_logit.astype(jnp.float32)), axis=1).transpose(0, 2, 1)
    outs = []
    for i in range(s_len // Q_BLOCK):
        t0, t1 = i * Q_BLOCK, (i + 1) * Q_BLOCK
        logits = jnp.einsum('bhqd,bhkd->bhqk', q[:, :, t0:t1], k[:, :, :t1]).astype(jnp.float32) * scale
        logits = logits + c[:, :, t0:t1, None] - c[:, :, None, :t1]
        causal = jnp.arange(t1)[None, :] <= jnp.arange(t0, t1)[:, None]
        p = jax.nn.softmax(jnp.where(causal, logits, NEG_BIG), axis=-1)
        outs.append(jnp.einsum('bhqk,bhkd->bhqd', p.astype(v.dtype), v[:, :, :t1]))
    return jnp.concatenate(outs, axis=2)

def moba_attention(q, k, v, bias_table):
    b, h, s_len, d = q.shape
    scale = HEAD_DIM ** -0.5
    nb = -(-s_len // MOBA_BLOCK)
    pad = nb * MOBA_BLOCK - s_len
    kp = jnp.pad(k, ((0, 0), (0, 0), (0, pad), (0, 0)))
    vp = jnp.pad(v, ((0, 0), (0, 0), (0, pad), (0, 0)))
    kb = kp.reshape(b, h, nb, MOBA_BLOCK, d)
    vb = vp.reshape(b, h, nb, MOBA_BLOCK, d)
    kmean = jnp.mean(kb.astype(jnp.float32), axis=3).astype(k.dtype)
    topk = min(MOBA_TOPK, nb)
    table_t = bias_table.T
    bi = jnp.arange(b)[:, None, None, None]
    hi = jnp.arange(h)[None, :, None, None]

    def chunk(ci):
        t0 = ci * MOBA_Q_CHUNK
        qc = lax.dynamic_slice_in_dim(q, t0, MOBA_Q_CHUNK, axis=2)
        tpos = t0 + jnp.arange(MOBA_Q_CHUNK)
        own = t0 // MOBA_BLOCK
        gate = jnp.einsum('bhqd,bhnd->bhqn', qc, kmean).astype(jnp.float32)
        past = jnp.arange(nb) < own
        gate = jnp.where(past, gate, -jnp.inf)
        _, gidx = lax.top_k(gate, topk)
        sel_valid = gidx < own
        ks = kb[bi, hi, gidx]
        vs = vb[bi, hi, gidx]
        s_sel = jnp.einsum('bhqd,bhqnkd->bhqnk', qc, ks).astype(jnp.float32) * scale
        kpos = gidx[..., None] * MOBA_BLOCK + jnp.arange(MOBA_BLOCK)
        bucket = t5_bucket(tpos[None, None, :, None, None] - kpos)
        s_sel = s_sel + table_t[hi[..., None], bucket].astype(jnp.float32)
        s_sel = jnp.where(sel_valid[..., None], s_sel, NEG_BIG)
        ko = lax.dynamic_slice_in_dim(kp, own * MOBA_BLOCK, MOBA_BLOCK, axis=2)
        vo = lax.dynamic_slice_in_dim(vp, own * MOBA_BLOCK, MOBA_BLOCK, axis=2)
        kpos_own = own * MOBA_BLOCK + jnp.arange(MOBA_BLOCK)
        dist_own = tpos[:, None] - kpos_own[None, :]
        s_own = jnp.einsum('bhqd,bhkd->bhqk', qc, ko).astype(jnp.float32) * scale
        s_own = s_own + table_t[:, t5_bucket(dist_own)].astype(jnp.float32)[None]
        s_own = jnp.where(dist_own >= 0, s_own, NEG_BIG)
        logits = jnp.concatenate([s_sel.reshape(b, h, MOBA_Q_CHUNK, topk * MOBA_BLOCK), s_own], axis=-1)
        p = jax.nn.softmax(logits, axis=-1).astype(v.dtype)
        p_sel = p[..., :topk * MOBA_BLOCK].reshape(b, h, MOBA_Q_CHUNK, topk, MOBA_BLOCK)
        p_own = p[..., topk * MOBA_BLOCK:]
        return (jnp.einsum('bhqnk,bhqnkd->bhqd', p_sel, vs)
                + jnp.einsum('bhqk,bhkd->bhqd', p_own, vo))

    out = lax.map(chunk, jnp.arange(s_len // MOBA_Q_CHUNK))
    return out.transpose(1, 2, 0, 3, 4).reshape(b, h, s_len, d)

def dsa_attention(q, k, v, q_idx, k_idx, w_idx, bias_table):
    b, h, s_len, d = q.shape
    scale = HEAD_DIM ** -0.5
    ksel = min(DSA_TOPK, s_len // 4)
    table_t = bias_table.T
    bi = jnp.arange(b)[:, None, None]
    outs = []
    for i in range(s_len // Q_BLOCK):
        t0, t1 = i * Q_BLOCK, (i + 1) * Q_BLOCK
        kk = min(ksel, t1)
        tpos = jnp.arange(t0, t1)
        isc = jax.nn.relu(jnp.einsum('bqhe,bke->bqhk', q_idx[:, t0:t1], k_idx[:, :t1]))
        isc = jnp.einsum('bqh,bqhk->bqk', w_idx[:, t0:t1], isc).astype(jnp.float32)
        admissible = jnp.arange(t1)[None, :] <= tpos[:, None]
        _, idx = lax.top_k(jnp.where(admissible, isc, -jnp.inf), kk)
        dist = tpos[None, :, None] - idx
        ks = k[bi, idx]
        vs = v[bi, idx]
        logits = jnp.einsum('bhqd,bqkd->bhqk', q[:, :, t0:t1], ks).astype(jnp.float32) * scale
        logits = logits + table_t[:, t5_bucket(dist)].transpose(1, 0, 2, 3).astype(jnp.float32)
        logits = jnp.where((dist >= 0)[:, None], logits, NEG_BIG)
        p = jax.nn.softmax(logits, axis=-1).astype(v.dtype)
        outs.append(jnp.einsum('bhqk,bqkd->bhqd', p, vs))
    return jnp.concatenate(outs, axis=2)

def token_mixer(xn, w_in, fox_b_f, t5_bias, w_gate, w_branch, w_out):
    b, s_len, _ = xn.shape
    proj = xn @ w_in
    (sb_q, sb_k, sb_v, mb_q, mb_k, mb_v, fx_q, fx_k, fx_v, fx_f,
     ds_q, ds_k, ds_v, ix_q, ix_k, ix_w) = jnp.split(proj, IN_SPLITS_2, axis=-1)
    o_sb = stick_breaking_attention(to_heads(sb_q, N_SB), to_heads(sb_k, N_SB), to_heads(sb_v, N_SB))
    o_mb = moba_attention(to_heads(mb_q, N_MOBA), to_heads(mb_k, N_MOBA), to_heads(mb_v, N_MOBA),
                          t5_bias[:, :N_MOBA])
    o_fx = forgetting_attention(to_heads(fx_q, N_FOX), to_heads(fx_k, N_FOX), to_heads(fx_v, N_FOX),
                                fx_f + fox_b_f)
    o_ds = dsa_attention(to_heads(ds_q, N_DSA), ds_k, ds_v,
                         ix_q.reshape(b, s_len, IDX_HEADS, IDX_DIM), ix_k, ix_w, t5_bias[:, N_MOBA:])
    branches = (o_sb, o_mb, o_fx, o_ds)
    mixed = None
    for i in range(N_BRANCH_2):
        y = jax.nn.sigmoid(xn @ w_gate[i]) * (merge_heads(branches[i]) @ w_branch[i])
        mixed = y if mixed is None else mixed + y
    return mixed @ w_out

def conv_ffn(xn, w_up, conv_w, conv_b, w_down):
    s_len = xn.shape[1]
    hdn = xn @ w_up
    hp = jnp.pad(hdn, ((0, 0), (CONV_W - 1, 0), (0, 0)))
    acc = conv_b
    for j in range(CONV_W):
        acc = acc + conv_w[j] * hp[:, j:j + s_len]
    g, u = jnp.split(acc, 2, axis=-1)
    return (jax.nn.gelu(g, approximate=False) * u) @ w_down

def second_inputs(seed: int = 0) -> dict:
    key = jax.random.key(seed)
    ks = jax.random.split(key, 14)
    nrm = jax.random.normal
    f32 = jnp.float32
    return {
        "x": nrm(ks[0], (BATCH, SEQ, D_MODEL), f32),
        "norm_mix_g": 1.0 + 0.02 * nrm(ks[1], (DEPTH_2, D_MODEL), f32),
        "norm_ffn_g": 1.0 + 0.02 * nrm(ks[2], (DEPTH_2, D_MODEL), f32),
        "norm_final_g": 1.0 + 0.02 * nrm(ks[3], (D_MODEL,), f32),
        "w_in": nrm(ks[4], (DEPTH_2, D_MODEL, P_IN), f32) * D_MODEL ** -0.5,
        "fox_b_f": 1.0 + 0.1 * nrm(ks[5], (DEPTH_2, N_FOX), f32),
        "t5_bias": 0.5 * nrm(ks[6], (T5_BUCKETS, N_MOBA + N_DSA), f32),
        "w_gate": nrm(ks[7], (DEPTH_2, N_BRANCH_2, D_MODEL, D_MODEL), f32) * D_MODEL ** -0.5,
        "w_branch": nrm(ks[8], (DEPTH_2, N_BRANCH_2, BRANCH_W_2, D_MODEL), f32) * BRANCH_W_2 ** -0.5,
        "w_out": nrm(ks[9], (DEPTH_2, D_MODEL, D_MODEL), f32) * D_MODEL ** -0.5,
        "w_up": nrm(ks[10], (DEPTH_2, D_MODEL, 2 * D_FF), f32) * D_MODEL ** -0.5,
        "conv_w": nrm(ks[11], (DEPTH_2, CONV_W, 2 * D_FF), f32) * CONV_W ** -0.5,
        "conv_b": 0.01 * nrm(ks[12], (DEPTH_2, 2 * D_FF), f32),
        "w_down": nrm(ks[13], (DEPTH_2, D_FF, D_MODEL), f32) * D_FF ** -0.5,
    }

def second_block(x, norm_mix_g, norm_ffn_g, norm_final_g, w_in, fox_b_f, t5_bias,
              w_gate, w_branch, w_out, w_up, conv_w, conv_b, w_down):
    for l in range(DEPTH_2):
        x = x + token_mixer(rmsnorm(x, norm_mix_g[l]), w_in[l], fox_b_f[l], t5_bias,
                            w_gate[l], w_branch[l], w_out[l])
        x = x + conv_ffn(rmsnorm(x, norm_ffn_g[l]), w_up[l], conv_w[l], conv_b[l], w_down[l])
    return rmsnorm(x, norm_final_g)


def setup_inputs(seed=0):
    out = dict(first_inputs(seed))
    for name, value in second_inputs(seed + 1).items():
        if name != "x":
            out[name + "_2"] = value
    return out


def reference(
    x, mem, mem_ln_g, mem_ln_b, ln_g, ln_b, ffn1_w_gu, ffn1_w_down, w_in, dn_conv_w, dn_a_log,
    dn_dt_bias, dn_norm_w, swa_sinks, w_mem_kv, w_branch, w_out, ffn2_w_gu, ffn2_w_down,
    norm_mix_g_2, norm_ffn_g_2, norm_final_g_2, w_in_2, fox_b_f_2, t5_bias_2, w_gate_2,
    w_branch_2, w_out_2, w_up_2, conv_w_2, conv_b_2, w_down_2,
):
    x = first_block(
        x, mem, mem_ln_g, mem_ln_b, ln_g, ln_b, ffn1_w_gu, ffn1_w_down, w_in, dn_conv_w,
        dn_a_log, dn_dt_bias, dn_norm_w, swa_sinks, w_mem_kv, w_branch, w_out, ffn2_w_gu,
        ffn2_w_down,
    )
    return second_block(
        x, norm_mix_g_2, norm_ffn_g_2, norm_final_g_2, w_in_2, fox_b_f_2, t5_bias_2, w_gate_2,
        w_branch_2, w_out_2, w_up_2, conv_w_2, conv_b_2, w_down_2,
    )


_drawn_inputs = setup_inputs


def setup_inputs(seed=0):
    import zlib

    import numpy as np

    out = dict(_drawn_inputs(seed))
    spreads = {}
    factors = {'mem': 5.15,
     'mem_ln_g': 8.0,
     'mem_ln_b': 8.0,
     'dn_norm_w': 8.0,
     'swa_sinks': 8.0,
     'w_mem_kv': 4.245,
     'norm_mix_g_2': 3.235,
     'norm_ffn_g_2': 3.954,
     'norm_final_g_2': 2.852,
     'fox_b_f_2': 7.109,
     'conv_b_2': 7.645}
    for name, (base, spread) in spreads.items():
        noise = np.random.default_rng([zlib.crc32(name.encode()), seed]).standard_normal(out[name].shape)
        drawn = base * np.exp(spread * noise) if base else spread * noise
        out[name] = __import__('jax').numpy.asarray(drawn.astype(out[name].dtype))
    for name, factor in factors.items():
        out[name] = (out[name] * factor).astype(out[name].dtype)
    return out
```

```python
import math
from contextlib import ExitStack

import numpy as np
import concourse.bass as bass
from concourse import mybir

F32 = mybir.dt.float32
F32R = mybir.dt.float32r
ALU = mybir.AluOpType
ACT = mybir.ActivationFunctionType
AX = mybir.AxisListType

P = 128
SEQ = 512
NT = SEQ // P
DM = 1024
DT = DM // P
FF = 2816
FT = FF // P
DEPTH = 2
NMEM = 256
ALPHA = (2 * DEPTH) ** 0.25
LN_EPS = 1e-5
RMS_EPS = 1e-6
NEG = -1e30
FILL = -3.0e38
TAKEN = -3.3e38

T5_BUCKETS = 32
T5_MAX_DIST = 128

NSLAB = 561
NRAW = 3
NSPLIT = 3
AHEAD = NSPLIT - 1
PAGES = 76



CONSTS = {}


def const_tables():
    p = np.arange(P)[:, None]
    c = np.arange(P)[None, :]
    t = {
        "ident": (p == c).astype(np.float32),
        "ones": np.ones((P, P), np.float32),
        "mean": np.full((P, P), 1.0 / DM, np.float32),
        "upto": (p <= c).astype(np.float32),
        "before": np.where(c < p, 0.0, NEG).astype(np.float32),
        "since": np.where(c >= p, 0.0, NEG).astype(np.float32),
        "causal": np.where(c <= p, 0.0, NEG).astype(np.float32),
        "later": (c > p).astype(np.float32),
        "ntri": np.where(p > c, -1.0, 0.0).astype(np.float32),
        "nones": np.full((P, P), -1.0, np.float32),
        "nblock8": np.where(p // 8 == c // 8, -1.0, 0.0).astype(np.float32),
    }
    for b in (8, 16, 32, 64):
        t[f"low{b}"] = ((c // b % 2 == 1) & (p // b == c // b - 1)).astype(np.float32)
    kk = np.arange(2 * P)[None, :]
    t["band"] = np.where((kk > p) & (kk <= p + P), 0.0, NEG).astype(np.float32)
    return t


def bucket_rows():
    d = 511 - np.arange(640)
    n = np.maximum(d, 0)
    nf = np.maximum(n, 1).astype(np.float32)
    half = T5_BUCKETS // 2
    large = half + (np.log(nf / half) / math.log(T5_MAX_DIST / half) * (T5_BUCKETS - half)).astype(np.int32)
    bucket = np.where(n < half, n, np.minimum(large, T5_BUCKETS - 1))
    out = np.zeros((33, 640), np.float32)
    out[np.where(d >= 0, bucket, 32), np.arange(640)] = 1.0
    return out


def layout(entries):
    at, out = 0, {}
    for name, n in entries:
        out[name] = (at, n)
        at += n
    return out, at


CONST_AT, NCONST = layout([(k, v.shape[1]) for k, v in const_tables().items()])
PARAM_AT, NPARAM = layout([
    ("mem_ln_g", 8), ("mem_ln_b", 8), ("ln_g", 48), ("ln_b", 48), ("conv", 96), ("dn_norm", 2),
    ("sinks", 16), ("a_log", 8), ("dt_bias", 8), ("norm_mix", 8), ("norm_ffn", 8), ("norm_final", 8),
    ("fox", 4), ("conv2", 132), ("conv2_b", 44),
])



class Line:

    def __init__(self, sem):
        self.sem, self.n, self.seen, self.ops = sem, 0, {}, []

    def wait(self, *tokens):
        for t in tokens:
            if t is None:
                continue
            if isinstance(t, list):
                self.wait(*t)
            elif self.seen.get(id(t[0]), 0) < t[1]:
                self.seen[id(t[0])] = t[1]
                self.ops.append(("wait", t[0], t[1]))

    def __call__(self, fn, *tokens, mark=True):
        self.wait(*tokens)
        if mark:
            self.n += 1
            self.ops.append(("run", fn, self.sem, 1))
            return (self.sem, self.n)
        self.ops.append(("run", fn, None, 0))
        return None

    def dma(self, dst, src, sem, value, *tokens):
        self.wait(*tokens)
        self.ops.append(("run", lambda e: e.dma_start(dst, src), sem, 16))
        return (sem, value)

    def emit(self, e):
        for op in self.ops:
            if op[0] == "wait":
                e.wait_ge(op[1], op[2])
            else:
                i = op[1](e)
                if op[2] is not None:
                    i.then_inc(op[2], op[3])


class Stock:

    def __init__(self, items):
        self.free = [(x, []) for x in items]

    def take(self):
        return self.free.pop(0)

    def give(self, x, *tokens):
        self.free.append((x, [t for t in tokens if t is not None]))


class Act:

    def __init__(self):
        self.hi, self.lo, self.tok, self.pages = [], [], [], []



def hybrid_then_mixer_program(nc, w, x_t, mem_t, consts, params, table, buckets, out):
    order = []
    ctx = ExitStack()
    with ctx:
        def sb(name, shape, dt=F32):
            return ctx.enter_context(nc.sbuf_tensor(name, shape, dt))

        def sem(name):
            return ctx.enter_context(nc.semaphore(name))

        raw = sb("raw", [P, NRAW, 1024])
        w_hi = sb("w_hi", [P, NSPLIT, 1024], F32R)
        w_lo = sb("w_lo", [P, NSPLIT, 1024], F32R)
        cst = sb("cst", [P, NCONST])
        par = sb("par", [P, NPARAM])
        alb = sb("alb", [P, 48])
        small = sb("small", [P, 2048])
        tab = sb("tab", [33, 8])
        page_f, page_r = [], []
        for i in range(PAGES):
            with nc.sbuf_tensor(f"page_r{i}", [P, 512], F32R) as r:
                page_r.append(r)
            page_f.append(sb(f"page_f{i}", [P, 512]))
        banks = [ctx.enter_context(nc.psum_tensor(f"bank{i}", [P, 512], F32)) for i in range(8)]
        scratch = nc.dram_tensor("bias_rows", (8, P, 640), F32, kind="Internal").ap()

        pe, act, dve, pool = Line(sem("s_pe")), Line(sem("s_act")), Line(sem("s_dve")), Line(sem("s_pool"))
        sp = Line(None)
        s_raw = [sem(f"s_raw{i}") for i in range(NRAW)]
        s_cst, s_par, s_tab = sem("s_cst"), sem("s_par"), sem("s_tab")
        s_x = [sem(f"s_x{i}") for i in range(8)]
        s_oh, s_out = sem("s_oh"), sem("s_out")
        s_bw = [sem(f"s_bw{i}") for i in range(8)]
        s_tb = [sem(f"s_tb{i}") for i in range(8)]

        ps = Stock(range(8))
        pg = Stock(range(PAGES))
        stat_at = [0]

        def stat(n):
            a = stat_at[0]
            stat_at[0] += n
            assert a + n <= 2048
            return small[:, a:a + n]

        def pf(i, n=512):
            return page_f[i][:, 0:n]

        def pr(i, n=512):
            return page_r[i][:, 0:n]

        def C(name):
            a, n = CONST_AT[name]
            return cst[:, a:a + n]

        def col(name, i):
            a, _ = PARAM_AT[name]
            return par[:, a + i:a + i + 1]

        t_cst = sp.dma(cst[:, :], consts, s_cst, 16)
        t_par = sp.dma(par[:, :], params, s_par, 16)
        act.wait(t_cst, t_par)
        dve.wait(t_cst, t_par)
        pe.wait(t_cst)

        def mm(o, l, r, start, stop, *tok, mark=False):
            return pe(lambda e: e.matmul(o, l, r, start=start, stop=stop), *tok, mark=mark)

        def tr(o, i, *tok, mark=False):
            idn = C("ident")
            return pe(lambda e: e.transpose(o, i, idn), *tok, mark=mark)

        def fn(o, i, f, *tok, bias=None, scale=1.0, acc=None):
            kw = {}
            if bias is not None:
                kw["bias"] = bias
            if acc is not None:
                kw["accum_out"] = acc
            return act(lambda e: e.activation(o, i, f, scale=scale, **kw), *tok)

        def tt(o, a, b, op, *tok, on=dve):
            return on(lambda e: e.tensor_tensor(o, a, b, op), *tok)

        def ts(o, a, s1, s2, op0, op1, *tok, on=dve):
            if op1 is None:
                return on(lambda e: e.tensor_scalar(o, a, s1, None, op0), *tok)
            return on(lambda e: e.tensor_scalar(o, a, s1, s2, op0, op1), *tok)

        def stt(o, a, s, b, op0, op1, *tok):
            return dve(lambda e: e.scalar_tensor_tensor(out=o, in0=a, scalar=s, in1=b, op0=op0, op1=op1), *tok)

        def rmax(o, a, *tok):
            return dve(lambda e: e.tensor_reduce(o, a, AX.X, ALU.max), *tok)

        def recip(o, a, *tok):
            return dve(lambda e: e.reciprocal(o, a), *tok)

        cb = stat(4)
        t_cb = []
        for i, v in enumerate((LN_EPS, RMS_EPS, 128 * RMS_EPS, 1.0)):
            t_cb.append(dve(lambda e, i=i, v=v: e.memset(cb[:, i:i + 1], v)))
        EPS_LN, EPS_RMS, EPS_Q, ONE = (cb[:, i:i + 1] for i in range(4))
        act.wait(t_cb[-1])
        a, n = PARAM_AT["ln_b"]
        t_alb = ts(alb[:, :], par[:, a:a + n], ALPHA, None, ALU.mult, None)
        act.wait(t_alb)

        t_hi, t_lo, freed, t_raw = {}, {}, {}, {}
        state = {"block": 0, "raw": 0, "split": 0}

        def load_slab(s):
            t_raw[s] = sp.dma(raw[:, s % NRAW, :], w[s], s_raw[s % NRAW], 16 * (s // NRAW + 1),
                              t_hi.get(s - NRAW), t_lo.get(s - NRAW))

        def split_slab(s):
            r, k = s % NRAW, s % NSPLIT
            t_hi[s] = fn(w_hi[:, k, :], raw[:, r, :], ACT.Copy, t_raw[s], freed.get(s - NSPLIT))
            t_lo[s] = tt(w_lo[:, k, :], raw[:, r, :], w_hi[:, k, :].bitcast(F32), ALU.subtract,
                         t_hi[s], freed.get(s - NSPLIT))

        def ahead(s):
            while state["split"] <= min(s + AHEAD, NSLAB - 1):
                while state["raw"] <= min(state["split"] + NRAW - 1, NSLAB - 1):
                    load_slab(state["raw"])
                    state["raw"] += 1
                split_slab(state["split"])
                state["split"] += 1

        def block(key):
            i = state["block"]
            state["block"] += 1
            order.append(key)
            s, j = divmod(i, 8)
            if j == 0:
                ahead(s)
            c = slice(j * P, j * P + P)
            return w_hi[:, s % NSPLIT, c], w_lo[:, s % NSPLIT, c], [t_hi[s], t_lo[s]], s, j

        def gemm_t(mat, mt, X, n=512):
            b, bf = ps.take()
            kts = len(X.hi)
            for kt in range(kts):
                wh, wl, wt, s, j = block((mat, mt, kt))
                o = banks[b][:, 0:n]
                mm(o, wh, X.hi[kt], kt == 0, False, bf, wt, X.tok[kt])
                mm(o, wh, X.lo[kt], False, False)
                t = mm(o, wl, X.hi[kt], False, kt == kts - 1, mark=(j == 7 or kt == kts - 1))
                if j == 7:
                    freed[s] = t
            return b, t

        def gemm_n(mat, mt, X, n=P, tiles=NT):
            b, bf = ps.take()
            kts = len(X.hi)
            assert state["block"] % 8 == 0 and kts == 8
            bl = [block((mat, mt, kt)) for kt in range(kts)]
            for i in range(tiles):
                o = banks[b][:, i * n:(i + 1) * n]
                c = slice(i * P, i * P + P)
                for kt, (wh, wl, wt, s, j) in enumerate(bl):
                    mm(o, X.hi[kt][:, c], wh[:, 0:n], kt == 0, False, bf, wt, X.tok[kt])
                    mm(o, X.lo[kt][:, c], wh[:, 0:n], False, False)
                    t = mm(o, X.hi[kt][:, c], wl[:, 0:n], False, kt == kts - 1,
                           mark=(i == tiles - 1 and kt == kts - 1))
            freed[s] = t
            return b, t

        def drop(X, *tok):
            for p in X.pages:
                pg.give(p, *tok)
            X.pages = []

        def split_into(X, src, *tok, n=512):
            h, hf = pg.take()
            l, lf = pg.take()
            t1 = fn(pr(h, n), src, ACT.Copy, hf, *tok)
            t2 = tt(pr(l, n), src, pr(h, n).bitcast(F32), ALU.subtract, lf, t1)
            X.hi.append(pr(h, n))
            X.lo.append(pr(l, n))
            X.tok.append([t1, t2])
            X.pages += [h, l]
            return [t1, t2]

        R = [pg.take()[0] for _ in range(8)]
        Rt = [None] * 8

        def first_load(alpha):
            X = Act()
            for m in range(8):
                t = sp.dma(pf(R[m]), x_t[m], s_x[m], 16)
                t2 = split_into(X, pf(R[m]), t)
                Rt[m] = fn(pf(R[m]), pf(R[m]), ACT.Copy, t2, scale=alpha)
            return X

        def add_up(b, t, m, scale):
            Rt[m] = stt(pf(R[m]), banks[b][:, :], scale, pf(R[m]), ALU.mult, ALU.add, t, Rt[m])
            ps.give(b, Rt[m])

        def layer_norm(tiles, toks, g, bcol, scaled, n=512, keep=1.0):
            s, sf = pg.take()
            ta = tt(pf(s, n), pf(tiles[0], n), pf(tiles[1], n), ALU.add, sf, toks[0], toks[1])
            for m in range(2, 8):
                ta = tt(pf(s, n), pf(s, n), pf(tiles[m], n), ALU.add, ta, toks[m])
            b, bf = ps.take()
            tm = mm(banks[b][:, 0:n], C("mean"), pf(s, n), True, True, bf, ta, mark=True)
            pg.give(s, tm)
            v, vf = ps.take()
            td = []
            for m in range(8):
                t = tt(pf(tiles[m], n), pf(tiles[m], n), banks[b][:, 0:n], ALU.subtract, tm, toks[m])
                td.append(t)
                q, qf = pg.take()
                t = fn(pf(q, n), pf(tiles[m], n), ACT.Square, t, qf)
                t = mm(banks[v][:, 0:n], C("mean"), pf(q, n), m == 0, m == 7, vf, t, mark=True)
                pg.give(q, t)
            ps.give(b, td[-1])
            r, rf = pg.take()
            t = fn(pf(r, n), banks[v][:, 0:n], ACT.Sqrt, t, rf, bias=EPS_LN)
            ps.give(v, t)
            tr_ = recip(pf(r, n), pf(r, n), t)
            X = Act()
            out_t = []

            def tail(m):
                h, l = X.pages[2 * m], X.pages[2 * m + 1]
                src = pf(tiles[m], n)
                t2 = stt(pr(l, n), src, bcol(m), pr(h, n).bitcast(F32), ALU.add, ALU.subtract, lfs[m], X.tok[m])
                X.tok[m] = [X.tok[m], t2]
                if keep is not None:
                    bb = scaled(m) if keep != 1.0 else bcol(m)
                    out_t.append(fn(src, src, ACT.Identity, t2, bias=bb, scale=keep))
                else:
                    pg.give(tiles[m], t2, X.tok[m][0])

            lfs = []
            for m in range(8):
                h, hf = pg.take()
                l, lf = pg.take()
                lfs.append(lf)
                src = pf(tiles[m], n)
                t1 = stt(src, src, g(m), pf(r, n), ALU.mult, ALU.mult, tr_, td[m])
                t1 = fn(pr(h, n), src, ACT.Identity, t1, hf, bias=bcol(m))
                X.hi.append(pr(h, n))
                X.lo.append(pr(l, n))
                X.tok.append(t1)
                X.pages += [h, l]
                if m >= 1:
                    tail(m - 1)
            tail(7)
            pg.give(r, X.tok[7][1])
            return X, out_t

        def rstd_of(srcs, toks, c, eps, scale=1.0, n=512):
            v, vf = ps.take()
            k = len(srcs)
            for m in range(k):
                q, qf = pg.take()
                t = fn(pf(q, n), srcs[m], ACT.Square, toks[m], qf)
                t = mm(banks[v][:, 0:n], c, pf(q, n), m == 0, m == k - 1, vf, t, mark=True)
                pg.give(q, t)
            r, rf = pg.take()
            t = fn(pf(r, n), banks[v][:, 0:n], ACT.Sqrt, t, rf, bias=eps, scale=scale)
            ps.give(v, t)
            return r, recip(pf(r, n), pf(r, n), t)

        def rms_norm(name):
            r, t = rstd_of([pf(x) for x in R], Rt, C("mean"), EPS_RMS)
            X = Act()
            for m in range(8):
                p, pfree = pg.take()
                t1 = stt(pf(p), pf(R[m]), col(name, m), pf(r), ALU.mult, ALU.mult, t, Rt[m], pfree)
                t2 = split_into(X, pf(p), t1)
                pg.give(p, *t2)
            pg.give(r, t1)
            return X

        def ffn(X, up, down, scale):
            H = Act()
            for j in range(FT):
                bg, tg = gemm_t(up, j, X)
                bu, tu = gemm_t(up, FT + j, X)
                s, sf = pg.take()
                t1 = fn(pf(s), banks[bg][:, :], ACT.Silu, tg, sf)
                ps.give(bg, t1)
                t2 = tt(pf(s), pf(s), banks[bu][:, :], ALU.mult, t1, tu)
                ps.give(bu, t2)
                if j == FT - 1:
                    drop(X, tu)
                t3 = split_into(H, pf(s), t2)
                pg.give(s, *t3)
            for m in range(8):
                b, t = gemm_t(down, m, H)
                add_up(b, t, m, scale)
            drop(H, t)

        def projected(mat, mt, X, n=512):
            b, t = gemm_t(mat, mt, X, n)
            p, f = pg.take()
            t2 = fn(pf(p, n), banks[b][:, 0:n], ACT.Copy, t, f)
            ps.give(b, t2)
            return p, t2

        def projected_n(mat, mt, X, n=P, tiles=NT):
            b, t = gemm_n(mat, mt, X, n, tiles)
            p, f = pg.take()
            t2 = fn(pf(p, n * tiles), banks[b][:, 0:n * tiles], ACT.Copy, t, f)
            ps.give(b, t2)
            return p, t2

        class Merge:
            def __init__(self, X, gate, branch, nb):
                self.X, self.gate, self.branch = X, gate, branch
                self.G, self.M, self.n, self.count, self.nb = [], [], -1, 0, nb
                self.last = None

            def open(self, n):
                self.n, self.G = n, []

            def fill(self, k=1):
                for _ in range(k):
                    if len(self.G) == 8:
                        return
                    b, t = gemm_t(self.gate, self.n * 8 + len(self.G), self.X)
                    p, f = pg.take()
                    t2 = fn(pf(p), banks[b][:, :], ACT.Sigmoid, t, f)
                    ps.give(b, t2)
                    self.G.append((p, t2))
                    self.last = t

            def close(self, O):
                self.fill(8)
                for m in range(8):
                    b, t = gemm_t(self.branch(self.n), m, O)
                    g, tg = self.G[m]
                    t2 = tt(pf(g), pf(g), banks[b][:, :], ALU.mult, t, tg)
                    ps.give(b, t2)
                    if self.count == 0:
                        self.M.append((g, t2))
                    else:
                        p, tp = self.M[m]
                        t3 = tt(pf(p), pf(p), pf(g), ALU.add, t2, tp)
                        pg.give(g, t3)
                        self.M[m] = (p, t3)
                drop(O, t)
                self.count += 1

            def result(self):
                Y = Act()
                for p, t in self.M:
                    t2 = split_into(Y, pf(p), t)
                    pg.give(p, *t2)
                return Y

        def weights_and_values(Ps, tP, L, vs, ob, i, of, last):
            for a, p in enumerate(Ps):
                b, bf = ps.take()
                nk = L // P
                for kb in range(nk):
                    t = tr(banks[b][:, kb * P:(kb + 1) * P], p[0][:, kb * P:(kb + 1) * P],
                           bf, tP[a], mark=(kb == nk - 1))
                q, qf = pg.take()
                t2 = fn(pf(q, L), banks[b][:, 0:L], ACT.Copy, t, qf)
                ps.give(b, t2)
                if p[1] is not None:
                    pg.give(p[1], t)
                for kb in range(nk):
                    v, tv, rows = vs(a, kb)
                    t3 = mm(banks[ob[a]][rows, i * P:(i + 1) * P], v, pf(q)[:, kb * P:(kb + 1) * P],
                            kb == 0, kb == nk - 1, t2, tv, of[a] if i == 0 else None, mark=(kb == nk - 1))
                pg.give(q, t3)
                last[a] = t3

        def softmax_rows(p, L, t, sink=None):
            mx, sm = stat(2), stat(2)
            t = rmax(mx[:, 0:1], pf(p, L), t)
            if sink is not None:
                t = tt(mx[:, 0:1], mx[:, 0:1], sink, ALU.max, t)
            t = ts(mx[:, 1:2], mx[:, 0:1], -1.0, None, ALU.mult, None, t)
            t2 = fn(pf(p, L), pf(p, L), ACT.Exp, t, bias=mx[:, 1:2], acc=sm[:, 0:1])
            if sink is not None:
                es = stat(1)
                t2 = fn(es, sink, ACT.Exp, bias=mx[:, 1:2])
                t2 = tt(sm[:, 0:1], sm[:, 0:1], es, ALU.add, t2)
            t2 = recip(sm[:, 1:2], sm[:, 0:1], t2)
            return ts(pf(p, L), pf(p, L), sm[:, 1:2], None, ALU.mult, None, t2)

        X = first_load(ALPHA)

        mt_, mtok = [], []
        s_m = [sem(f"s_m{i}") for i in range(8)]
        for m in range(8):
            p, _ = pg.take()
            mt_.append(p)
            mtok.append(sp.dma(pf(p, NMEM), mem_t[m], s_m[m], 16))
        MX, _ = layer_norm(mt_, mtok, lambda m: col("mem_ln_g", m), lambda m: col("mem_ln_b", m), None,
                           n=NMEM, keep=None)
        mem_k, mem_v = {}, {}
        for l in range(DEPTH):
            mem_k[l] = []
            for h2 in range(2):
                p, f = pg.take()
                tk = []
                for a in range(2):
                    b, t = gemm_t(("w_mem_kv", l), 2 * h2 + a, MX, NMEM)
                    t2 = fn(pf(p)[:, a * NMEM:(a + 1) * NMEM], banks[b][:, 0:NMEM], ACT.Copy, t, f)
                    ps.give(b, t2)
                mem_k[l].append((p, t2))
            mem_v[l] = []
            for h2 in range(2):
                p, f = pg.take()
                for a in range(2):
                    b, t = gemm_n(("w_mem_kv", l), 4 + 2 * h2 + a, MX, P, 2)
                    t2 = fn(pf(p)[:, a * 256:(a + 1) * 256], banks[b][:, 0:256], ACT.Copy, t, f)
                    ps.give(b, t2)
                mem_v[l].append((p, t2))
        drop(MX, t)

        def cross_attention(l, X, mg):
            qs = [projected(("w_in", l), 23 + h, X) for h in range(4)]
            O = Act()
            sc = P ** -0.5
            for hp in range(2):
                ob, of = zip(*[ps.take() for _ in range(2)])
                kp, tk = mem_k[l][hp]
                vp, tv = mem_v[l][hp]
                last = [None, None]
                for i in range(NT):
                    b, bf = ps.take()
                    for a in range(2):
                        q, tq = qs[2 * hp + a]
                        t = mm(banks[b][:, a * 256:(a + 1) * 256], pf(q)[:, i * P:(i + 1) * P],
                               pf(kp)[:, a * 256:(a + 1) * 256], True, True, bf, tq, tk, mark=(a == 1))
                    st = stat(8)
                    t = rmax(st[:, 0:2], banks[b][:, :].rearrange("p (a n) -> p a n", a=2), t)
                    t = ts(st[:, 2:4], st[:, 0:2], -sc, None, ALU.mult, None, t)
                    p, f = pg.take()
                    tp = []
                    for a in range(2):
                        c = slice(a * 256, (a + 1) * 256)
                        te = fn(pf(p)[:, c], banks[b][:, c], ACT.Exp, t, f, bias=st[:, 2 + a:3 + a],
                                scale=sc, acc=st[:, 4 + a:5 + a])
                    ps.give(b, te)
                    t = recip(st[:, 6:8], st[:, 4:6], te)
                    for a in range(2):
                        c = slice(a * 256, (a + 1) * 256)
                        tp.append(ts(pf(p)[:, c], pf(p)[:, c], st[:, 6 + a:7 + a], None, ALU.mult, None, t))
                    mg.fill(1)
                    weights_and_values(
                        [(pf(p)[:, 0:256], None), (pf(p)[:, 256:512], p)], tp, 256,
                        lambda a, kb: (pf(vp)[:, a * 256 + kb * P:a * 256 + (kb + 1) * P], tv, slice(0, P)),
                        ob, i, of, last)
                for a in range(2):
                    t = split_into(O, banks[ob[a]][:, :], last[a])
                    ps.give(ob[a], *t)
            for q, _ in qs:
                pg.give(q, last[1])
            return O

        def window_attention(l, X, mg):
            qs = [projected(("w_in", l), 17 + j, X) for j in range(4)]
            k, tk = projected(("w_in", l), 21, X)
            v, tv = projected_n(("w_in", l), 22, X)
            O = Act()
            sc = 64 ** -0.5
            for j in range(4):
                ob, of = ps.take()
                q, tq = qs[j]
                last = [None, None]
                for n in range(NT):
                    k0 = max(n - 1, 0) * P
                    L = (n + 1) * P - k0
                    tp, pgs = [], []
                    for a in range(2):
                        b, bf = ps.take()
                        rows = slice(64 * a, 64 * a + 64)
                        t = mm(banks[b][:, 0:L], pf(q)[rows, n * P:(n + 1) * P], pf(k)[rows, k0:k0 + L],
                               True, True, bf, tq, tk, mark=True)
                        p, f = pg.take()
                        t = stt(pf(p, L), banks[b][:, 0:L], sc, C("band")[:, 2 * P - L:2 * P],
                                ALU.mult, ALU.add, t, f)
                        ps.give(b, t)
                        tp.append(softmax_rows(p, L, t, sink=col("sinks", l * 8 + 2 * j + a)))
                        pgs.append((pf(p, L), p))
                    if n % 2 == 1:
                        mg.fill(1)
                    weights_and_values(
                        pgs, tp, L,
                        lambda a, kb: (pf(v)[:, (k0 // P + kb) * P + 64 * a:(k0 // P + kb) * P + 64 * a + 64],
                                       tv, slice(64 * a, 64 * a + 64)),
                        [ob, ob], n, [of, of], last)
                t = split_into(O, banks[ob][:, :], *last)
                ps.give(ob, *t)
            for q, _ in qs:
                pg.give(q, *last)
            pg.give(k, *last)
            pg.give(v, *last)
            return O

        def row_sums(gcols, tg, idx, prefix=False):
            b, bf = ps.take()
            s, sf = pg.take()
            tl = []
            for i in range(NT):
                g = gcols[:, idx(i):idx(i) + 1]
                tl.append(ts(pf(s)[:, i * P:(i + 1) * P], C("ones"), g, None, ALU.mult, None, sf, tg))
            for i in range(NT):
                o = banks[b][:, i * P:(i + 1) * P]
                pre = range(i) if prefix else ()
                t = mm(o, pf(s)[:, i * P:(i + 1) * P], C("upto"), True, not pre, bf, tl[i], mark=True)
                for j in pre:
                    t = mm(o, pf(s)[:, j * P:(j + 1) * P], C("ones"), False, j == i - 1, mark=True)
            pg.give(s, t)
            return b, t

        def softplus_of(v, n, scratch_cols, *tok):
            t = fn(scratch_cols, v, ACT.Abs, *tok)
            t = fn(scratch_cols, scratch_cols, ACT.Exp, t, scale=-1.0)
            t = fn(scratch_cols, scratch_cols, ACT.Ln, t, bias=ONE)
            return stt(v, v, 0.0, scratch_cols, ALU.max, ALU.add, t)

        def delta_branch(l, X, mg):
            b, t = gemm_n(("w_in", l), 12, X, 8)
            ba = stat(32)
            t = fn(ba, banks[b][:, 0:32], ACT.Copy, t)
            ps.give(b, t)
            ba3 = ba.rearrange("p (i c) -> p i c", c=8)
            be, g, ea, w1 = stat(16), stat(16), stat(4), stat(16)
            be3, g3 = be.rearrange("p (i h) -> p i h", h=4), g.rearrange("p (i h) -> p i h", h=4)
            t_be = fn(be3, ba3[:, :, 0:4], ACT.Sigmoid, t)
            for h in range(4):
                tg = ts(g3[:, :, h:h + 1], ba3[:, :, 4 + h:5 + h], col("dt_bias", 4 * l + h), None,
                        ALU.add, None, t)
            tg = softplus_of(g, 16, w1, tg)
            a0 = PARAM_AT["a_log"][0] + 4 * l
            te = fn(ea, par[:, a0:a0 + 4], ACT.Exp)
            te = ts(ea, ea, -1.0, None, ALU.mult, None, te)
            for h in range(4):
                tg = ts(g3[:, :, h:h + 1], g3[:, :, h:h + 1], ea[:, h:h + 1], None, ALU.mult, None, tg, te)
            b, bf = ps.take()
            t = mm(banks[b][:, 0:16], C("upto"), g, True, True, bf, tg, mark=True)
            gc, ngc, eg, beg, kt_ = stat(16), stat(16), stat(16), stat(16), stat(16)
            t_gc = fn(gc, banks[b][:, 0:16], ACT.Copy, t)
            t_eg = fn(eg, banks[b][:, 0:16], ACT.Exp)
            ps.give(b, t_eg)
            t_ngc = ts(ngc, gc, -1.0, None, ALU.mult, None, t_gc)
            t_beg = tt(beg, be, eg, ALU.mult, t_eg, t_be)

            qkv = []
            for m in range(12):
                b, t = gemm_t(("w_in", l), m, X)
                p, f = pg.take()
                w_ = lambda j: col("conv", (l * 4 + j) * 12 + m)
                t = fn(pf(p), banks[b][:, :], ACT.Copy, t, f, scale=w_(3))
                for sh in range(1, 4):
                    t = stt(pf(p)[:, sh:], banks[b][:, 0:SEQ - sh], w_(3 - sh), pf(p)[:, sh:],
                            ALU.mult, ALU.add, t)
                ps.give(b, t)
                t = fn(pf(p), pf(p), ACT.Silu, t)
                qkv.append((p, t))
            for m in range(8):
                p, t = qkv[m]
                if m < 4:
                    r, t2 = rstd_of([pf(p)], [t], C("ones"), EPS_Q, scale=float(P))
                else:
                    r, t2 = rstd_of([pf(p)], [t], C("ones"), EPS_RMS)
                t3 = tt(pf(p), pf(p), pf(r), ALU.mult, t2)
                pg.give(r, t3)
                qkv[m] = (p, t3)

            O = Act()
            ot = []

            def four(f, *tok):
                b, bf = ps.take()
                for i in range(NT):
                    prods = f(i)
                    for n_, (x, y) in enumerate(prods):
                        t = mm(banks[b][:, i * P:(i + 1) * P], x, y, n_ == 0, n_ == len(prods) - 1,
                               bf, *tok, mark=(i == NT - 1 and n_ == len(prods) - 1))
                return b, t

            def T(p, i):
                return pf(p)[:, i * P:(i + 1) * P]

            def v4(ap):
                return ap.rearrange("p (i c) -> p i c", i=4)

            def bc(c):
                return C(c).rearrange("p (o c) -> p o c", o=1).broadcast_to([P, 4, P])

            def percol(s16, h):
                return s16.rearrange("p (i h) -> p i h", h=4)[:, :, h:h + 1].broadcast_to([P, 4, P])

            for h in range(4):
                q, tq = qkv[h]
                k, tk = qkv[4 + h]
                vv, tv = qkv[8 + h]
                gb, tgb = row_sums(g, tg, lambda i: 4 * i + h)
                d1, f1 = pg.take()
                d2, f2 = pg.take()
                e_, f3 = pg.take()
                G4 = v4(banks[gb][:, :])
                t1 = tt(v4(pf(d1)), bc("before"), G4, ALU.subtract, tgb, f1)
                t2 = tt(v4(pf(d2)), G4, bc("since"), ALU.add, tgb, f2)
                gl = stat(4)
                tgl = dve(lambda e, gl=gl, G4=G4: e.tensor_copy(gl, G4[:, :, P - 1:P]), tgb)
                t3 = fn(pf(e_), banks[gb][:, :], ACT.Exp, tgb, f3, tgl, t2)
                ps.give(gb, t3)
                ktl, egl = stat(4), stat(4)
                for i in range(NT):
                    c = 4 * i + h
                    td1 = fn(T(d1, i), T(d1, i), ACT.Exp, t1, bias=gc[:, c:c + 1])
                    td2 = fn(T(d2, i), T(d2, i), ACT.Exp, t2, t_ngc, bias=ngc[:, c:c + 1])
                    tkt = fn(ktl[:, i:i + 1], gl[:, i:i + 1], ACT.Exp, tgl, bias=ngc[:, c:c + 1])
                tegl = fn(egl, gl, ACT.Exp)
                b, bf = ps.take()
                for i in range(NT):
                    t = tr(banks[b][:, i * P:(i + 1) * P], T(k, i), bf, tk, mark=(i == 3))
                kbe, f1 = pg.take()
                tke, f2 = pg.take()
                vb, f3 = pg.take()
                t4 = tt(v4(pf(kbe)), v4(banks[b][:, :]), percol(beg, h), ALU.mult, t, f1, t_beg)
                kt3 = ktl.rearrange("p (i o) -> p i o", o=1).broadcast_to([P, 4, P])
                t5 = tt(v4(pf(tke)), v4(banks[b][:, :]), kt3, ALU.mult, f2, tkt)
                ps.give(b, t5)
                b, bf = ps.take()
                for i in range(NT):
                    t = tr(banks[b][:, i * P:(i + 1) * P], T(vv, i), bf, tv, mark=(i == 3))
                t6 = tt(v4(pf(vb)), v4(banks[b][:, :]), percol(be, h), ALU.mult, t, f3, t_be)
                ps.give(b, t6)
                pg.give(vv, t)
                b, t = four(lambda i: [(T(k, i), T(k, i))])
                t = tt(pf(d1), pf(d1), banks[b][:, :], ALU.mult, t, td1)
                ps.give(b, t)
                tA = tt(v4(pf(d1)), v4(pf(d1)), percol(be, h), ALU.mult, t)
                b, t = four(lambda i: [(T(k, i), T(q, i))], tq, tk)
                tQ = tt(pf(d2), pf(d2), banks[b][:, :], ALU.mult, t, td2)
                ps.give(b, tQ)
                pg.give(k, t)
                tqd = tt(pf(q), pf(q), pf(e_), ALU.mult, t, t3)
                pg.give(e_, tqd)
                mg.fill(1)
                b, bf = ps.take()
                for i in range(NT):
                    t = tr(banks[b][:, i * P:(i + 1) * P], T(d1, i), bf, tA, mark=(i == 3))
                at, f = pg.take()
                tAT = fn(pf(at), banks[b][:, :], ACT.Copy, t, f)
                ps.give(b, tAT)
                n1, f1 = pg.take()
                n1t, f2 = pg.take()
                ta = tt(v4(pf(n1)), v4(pf(d1)), bc("nblock8"), ALU.mult, tA, f1)
                pg.give(d1, ta, tAT)
                tb = tt(v4(pf(n1t)), v4(pf(at)), bc("nblock8"), ALU.mult, tAT, f2)
                x, f3 = pg.take()
                xt, f4 = pg.take()
                tx = tt(v4(pf(x)), v4(pf(n1)), bc("ident"), ALU.add, ta, f3)
                txt = tt(v4(pf(xt)), v4(pf(n1t)), bc("ident"), ALU.add, tb, f4)
                tn = [ta, tb]
                for lev in range(2):
                    b1, u1 = four(lambda i: [(T(n1t, i), T(n1, i))], tn)
                    b2, u2 = four(lambda i: [(T(n1, i), T(n1t, i))])
                    ta = fn(pf(n1), banks[b1][:, :], ACT.Copy, u1, u2, tx)
                    tb = dve(lambda e, b2=b2, n1t=n1t: e.tensor_copy(pf(n1t), banks[b2][:, :]), u2, u1, txt)
                    ps.give(b1, ta)
                    ps.give(b2, tb)
                    tn = [ta, tb]
                    b1, u1 = four(lambda i: [(T(xt, i), T(n1, i))], tn, txt)
                    b2, u2 = four(lambda i: [(T(n1, i), T(xt, i))])
                    tx = tt(pf(x), pf(x), banks[b1][:, :], ALU.add, u1, tx)
                    txt = tt(pf(xt), pf(xt), banks[b2][:, :], ALU.add, u2, txt)
                    ps.give(b1, tx)
                    ps.give(b2, txt)
                low, prod = n1, n1t
                tlast = u2
                mg.fill(1)
                for size in (8, 16, 32, 64):
                    t = tt(v4(pf(low)), v4(pf(at)), bc(f"low{size}"), ALU.mult, tlast, tAT)
                    b1, u1 = four(lambda i: [(T(low, i), T(x, i))], t, tx)
                    t = fn(pf(prod), banks[b1][:, :], ACT.Copy, u1, tlast)
                    ps.give(b1, t)
                    if size < 64:
                        b1, u1 = four(lambda i: [(T(xt, i), T(prod, i))], t, txt)
                    b2, u2 = four(lambda i: [(T(prod, i), T(xt, i))], t, txt)
                    if size < 64:
                        tx = tt(pf(x), pf(x), banks[b1][:, :], ALU.subtract, u1, tx)
                        ps.give(b1, tx)
                    txt = tt(pf(xt), pf(xt), banks[b2][:, :], ALU.subtract, u2, txt)
                    ps.give(b2, txt)
                    tlast = u2
                pg.give(n1t, tlast)
                pg.give(at, tlast)
                pg.give(x, tlast)
                wt, f = n1, None
                b, t = four(lambda i: [(T(kbe, i), T(xt, i))], t4, txt)
                twt = fn(pf(wt), banks[b][:, :], ACT.Copy, t, tlast, scale=-1.0)
                ps.give(b, twt)
                pg.give(kbe, t)
                S, f = pg.take()
                vn, f2 = pg.take()
                ob, of = ps.take()
                tS = None
                for i in range(NT):
                    b, bf = ps.take()
                    o = banks[b][:, 0:P]
                    t = mm(o, T(xt, i), T(vb, i), True, i == 0, bf, txt, t6, mark=True)
                    if i:
                        t = mm(o, T(wt, i), pf(S, P), False, True, twt, tS, mark=True)
                    tv_ = fn(T(vn, i), o, ACT.Copy, t, f2)
                    ps.give(b, tv_)
                    oo = banks[ob][:, i * P:(i + 1) * P]
                    if i:
                        mm(oo, pf(S, P), T(q, i), True, False, of, tqd, tS)
                    to = mm(oo, T(vn, i), T(d2, i), i == 0, True, of, tv_, tQ, mark=True)
                    if i < NT - 1:
                        b, bf = ps.take()
                        o = banks[b][:, 0:P]
                        t = mm(o, T(tke, i), T(vn, i), True, True, bf, t5, mark=True)
                        if i == 0:
                            tS = dve(lambda e, o=o, S=S: e.tensor_copy(pf(S, P), o), t, f)
                        else:
                            tS = stt(pf(S, P), pf(S, P), egl[:, i:i + 1], o, ALU.mult, ALU.add, t, to, tegl)
                        ps.give(b, tS)
                for z in (S, vn, xt, wt, vb, tke, d2, q):
                    pg.give(z, to, tS)
                o_, f = pg.take()
                t = fn(pf(o_), banks[ob][:, :], ACT.Copy, to, f)
                ps.give(ob, t)
                ot.append((o_, t))
            for h in range(4):
                o_, t = ot[h]
                r, t2 = rstd_of([pf(o_)], [t], C("ones"), EPS_RMS, scale=1.0 / P)
                t2 = stt(pf(o_), pf(o_), col("dn_norm", l), pf(r), ALU.mult, ALU.mult, t2)
                b, t = gemm_t(("w_in", l), 13 + h, X)
                z, f = pg.take()
                t3 = fn(pf(z), banks[b][:, :], ACT.Silu, t, f)
                ps.give(b, t3)
                t = tt(pf(o_), pf(o_), pf(z), ALU.mult, t2, t3)
                pg.give(z, t)
                pg.give(r, t)
                t = split_into(O, pf(o_), t)
                pg.give(o_, *t)
            return O

        for l in range(DEPTH):
            ffn(X, ("ffn1_gu", l), ("ffn1_down", l), 0.5)
            lng = lambda n: (lambda m: col("ln_g", (l * 3 + n) * 8 + m), lambda m: col("ln_b", (l * 3 + n) * 8 + m),
                             lambda m: alb[:, (l * 3 + n) * 8 + m:(l * 3 + n) * 8 + m + 1])
            X, Rt[:] = layer_norm(R, Rt, *lng(0), keep=ALPHA)
            mg = Merge(X, ("gates", l), lambda n: ("w_branch", l, n), 3)
            mg.open(2)
            O = cross_attention(l, X, mg)
            for p, t in mem_k[l] + mem_v[l]:
                pg.give(p, (pe.sem, pe.n))
            mg.close(O)
            mg.open(1)
            O = window_attention(l, X, mg)
            mg.close(O)
            mg.open(0)
            O = delta_branch(l, X, mg)
            mg.fill(8)
            drop(X, mg.last)
            mg.close(O)
            Y = mg.result()
            for m in range(8):
                b, t = gemm_t(("w_out", l), m, Y)
                add_up(b, t, m, 1.0)
            drop(Y, t)
            X, Rt[:] = layer_norm(R, Rt, *lng(1), keep=ALPHA)
            ffn(X, ("ffn2_gu", l), ("ffn2_down", l), 0.5)
            X, Rt[:] = layer_norm(R, Rt, *lng(2), keep=ALPHA if l < DEPTH - 1 else 1.0)
        drop(X)

        X = rms_norm("norm_mix")

        t = dve(lambda e: e.memset(tab[:, :], NEG))
        t_tab = sp.dma(tab[0:32, :], table, s_tab, 16, t)
        oh0, f0 = pg.take()
        oh1, f1 = pg.take()
        t_oh = sp.dma(pf(oh0)[0:33, :], buckets[:, 0:512], s_oh, 16, f0)
        t_oh = sp.dma(pf(oh1)[0:33, 0:128], buckets[:, 512:640], s_oh, 32, f1)
        t_bw = []
        for h in range(8):
            th, f = pg.take()
            t1 = ts(pf(th)[0:33, 0:P], C("ones")[0:33, :], tab[:, h:h + 1], None, ALU.mult, None, f, t, t_tab)
            b, bf = ps.take()
            b2, bf2 = ps.take()
            mm(banks[b][:, :], pf(th)[0:33, 0:P], pf(oh0)[0:33, :], True, True, bf, bf2, t1, t_oh)
            t1 = mm(banks[b2][:, 0:P], pf(th)[0:33, 0:P], pf(oh1)[0:33, 0:P], True, True, mark=True)
            pg.give(th, t1)
            bb, f2 = pg.take()
            bb2, f3 = pg.take()
            t2 = fn(pf(bb), banks[b][:, :], ACT.Copy, t1, f2)
            t3 = fn(pf(bb2, P), banks[b2][:, 0:P], ACT.Copy, t1, f3)
            ps.give(b, t2)
            ps.give(b2, t3)
            sp.dma(scratch[h, :, 0:512], pf(bb), s_bw[h], 16, t2)
            t_bw.append(sp.dma(scratch[h, :, 512:640], pf(bb2, P), s_bw[h], 32, t3))
            pg.give(bb, t_bw[h])
            pg.give(bb2, t_bw[h])
        pg.give(oh0, t1)
        pg.give(oh1, t1)

        def bias_tiles(hs):
            out_ = {}
            for h in hs:
                p, f = pg.take()
                src = bass.AP(tensor=scratch.tensor, offset=h * 640 * P + 127, ap=[[639, P], [1, 512]])
                out_[h] = (p, sp.dma(pf(p), src, s_tb[h], 16, t_bw[h], f))
            return out_

        sc = 64 ** -0.5
        mg = Merge(X, "w_gate_2", lambda n: ("w_branch_2", n), 4)

        def stick_breaking():
            qs = [projected("w_in_2", m, X) for m in (0, 1)]
            ks = [projected("w_in_2", m, X) for m in (2, 3)]
            vs = [projected_n("w_in_2", m, X) for m in (4, 5)]
            O = Act()
            for jt in range(2):
                q, tq = qs[jt]
                k, tk = ks[jt]
                v, tv = vs[jt]
                ob, of = ps.take()
                last = []
                for a in range(2):
                    rows = slice(64 * a, 64 * a + 64)
                    zp, ap_, tz, ta_ = [], [], [], []
                    for i in range(NT):
                        W = SEQ - i * P
                        b, bf = ps.take()
                        t = mm(banks[b][:, 0:W], pf(k)[rows, i * P:(i + 1) * P], pf(q)[rows, i * P:SEQ],
                               True, True, bf, tq, tk, mark=True)
                        z, fz = pg.take()
                        s, fs = pg.take()
                        t1 = ts(pf(z, W), banks[b][:, 0:W], sc, None, ALU.mult, None, t, fz)
                        ps.give(b, t1)
                        t = fn(pf(s, W), pf(z, W), ACT.Abs, t1, fs)
                        t = fn(pf(s, W), pf(s, W), ACT.Exp, t, scale=-1.0)
                        t = fn(pf(s, W), pf(s, W), ACT.Ln, t, bias=ONE)
                        t = stt(pf(s, W), pf(z, W), 0.0, pf(s, W), ALU.max, ALU.add, t)
                        t1 = tt(pf(z, W), pf(z, W), pf(s, W), ALU.subtract, t)
                        t = tt(pf(s, P), pf(s, P), C("later"), ALU.mult, t1)
                        zp.append(z)
                        ap_.append(s)
                        tz.append(t1)
                        ta_.append(t)
                    mg.fill(1)
                    for i in range(NT):
                        W = SEQ - i * P
                        b, bf = ps.take()
                        t = mm(banks[b][:, 0:W], C("ntri"), pf(ap_[i], W), True, i == NT - 1, bf, ta_, mark=True)
                        for j in range(i + 1, NT):
                            t = mm(banks[b][:, (j - i) * P:W], C("nones"), pf(ap_[j], SEQ - j * P),
                                   False, j == NT - 1, mark=True)
                        t = tt(pf(zp[i], W), pf(zp[i], W), banks[b][:, 0:W], ALU.add, t, tz[i])
                        ps.give(b, t)
                        t = fn(pf(zp[i], W), pf(zp[i], W), ACT.Exp, t)
                        tz[i] = tt(pf(zp[i], P), pf(zp[i], P), C("later"), ALU.mult, t)
                    for i in range(NT):
                        W = SEQ - i * P
                        t = mm(banks[ob][rows, i * P:SEQ], pf(v)[:, i * P + 64 * a:i * P + 64 * a + 64],
                               pf(zp[i], W), i == 0, i == NT - 1, of, tz[i], tv, mark=True)
                    for i in range(NT):
                        pg.give(zp[i], t)
                        pg.give(ap_[i], t)
                    last.append(t)
                t = split_into(O, banks[ob][:, :], last)
                ps.give(ob, *t)
            for p, _ in qs + ks + vs:
                pg.give(p, *last)
            return O

        def causal_softmax(qs, kof, vof, bias, extra=()):
            O = Act()
            for jt in range(2):
                q, tq = qs[jt]
                ob, of = ps.take()
                last = [None, None]
                for i in range(NT):
                    L = (i + 1) * P
                    tp, pgs = [], []
                    for a in range(2):
                        rows = slice(64 * a, 64 * a + 64)
                        k, tk = kof(jt)
                        b, bf = ps.take()
                        t = mm(banks[b][:, 0:L], pf(q)[rows, i * P:(i + 1) * P], pf(k)[rows, 0:L],
                               True, True, bf, tq, tk, mark=True)
                        p, f = pg.take()
                        adds, after = bias(2 * jt + a, i, L)
                        t = stt(pf(p, L), banks[b][:, 0:L], sc, adds[0][0], ALU.mult, ALU.add, t, f, adds[0][1])
                        ps.give(b, t)
                        for ap_, tok in adds[1:]:
                            t = tt(pf(p, L), pf(p, L), ap_, ALU.add, t, tok)
                        after(t)
                        tp.append(softmax_rows(p, L, t))
                        pgs.append((pf(p, L), p))
                    mg.fill(1)
                    weights_and_values(pgs, tp, L, lambda a, kb: vof(2 * jt + a, kb),
                                       [ob, ob], i, [of, of], last)
                t = split_into(O, banks[ob][:, :], *last)
                ps.give(ob, *t)
            return O, last

        nar, t_nar = projected_n("w_in_2", 23, X)

        def narrow(i, c0, n):
            return pf(nar)[:, i * P + c0:i * P + c0 + n]

        mg.open(0)
        O = stick_breaking()
        mg.close(O)

        mg.open(1)
        tbs = bias_tiles(range(4))
        qs = [projected("w_in_2", m, X) for m in (6, 7)]
        ks = [projected("w_in_2", m, X) for m in (8, 9)]
        vs = [projected_n("w_in_2", m, X) for m in (10, 11)]

        def v_of(vs):
            def f(h, kb):
                v, tv = vs[h // 2]
                a = h % 2
                return pf(v)[:, kb * P + 64 * a:kb * P + 64 * a + 64], tv, slice(64 * a, 64 * a + 64)
            return f

        def t5(tbs, h0):
            def f(h, i, L):
                p, t = tbs[h0 + h]
                return [(pf(p)[:, 384 - P * i:384 - P * i + L], t)], lambda t: None
            return f

        O, last = causal_softmax(qs, lambda jt: ks[jt], v_of(vs), t5(tbs, 0))
        for p, _ in qs + ks + vs + list(tbs.values()):
            pg.give(p, *last, (dve.sem, dve.n))
        mg.close(O)

        mg.open(2)
        qs = [projected("w_in_2", m, X) for m in (12, 13)]
        ks = [projected("w_in_2", m, X) for m in (14, 15)]
        vs = [projected_n("w_in_2", m, X) for m in (16, 17)]
        fl, w1, cc = stat(16), stat(16), stat(16)
        fl3 = fl.rearrange("p (i h) -> p i h", h=4)
        for i in range(NT):
            a0 = PARAM_AT["fox"][0]
            t = tt(fl3[:, i, :], narrow(i, 64, 4), par[:, a0:a0 + 4], ALU.add, t_nar)
        t = ts(fl, fl, -1.0, None, ALU.mult, None, t)
        t = softplus_of(fl, 16, w1, t)
        b, bf = ps.take()
        for i in range(NT):
            o = banks[b][:, 4 * i:4 * i + 4]
            tc = mm(o, C("upto"), fl[:, 4 * i:4 * i + 4], True, i == 0, bf, t, mark=True)
            for j in range(i):
                tc = mm(o, C("ones"), fl[:, 4 * j:4 * j + 4], False, j == i - 1, mark=True)
        t_cc = fn(cc, banks[b][:, 0:16], ACT.Copy, tc, scale=-1.0)
        ps.give(b, t_cc)
        crow = []
        for h in range(4):
            b, tb = row_sums(fl, t, lambda i: 4 * i + h, prefix=True)
            p, f = pg.take()
            tb = fn(pf(p), banks[b][:, :], ACT.Copy, tb, f)
            ps.give(b, tb)
            crow.append((p, tb))

        def fox(h, i, L):
            p, t = crow[h]
            q, f = pg.take()
            t = ts(pf(q, L), pf(p, L), cc[:, 4 * i + h:4 * i + h + 1], None, ALU.add, None, t, t_cc, f)
            d = pf(q)[:, L - P:L]
            t = tt(d, d, C("causal"), ALU.add, t)
            return [(pf(q, L), t)], lambda t: pg.give(q, t)

        O, last = causal_softmax(qs, lambda jt: ks[jt], v_of(vs), fox)
        for p, _ in qs + ks + vs + crow:
            pg.give(p, *last, (dve.sem, dve.n))
        mg.close(O)

        mg.open(3)
        ixq = [projected("w_in_2", m, X) for m in (20, 21)]
        ixk, t_ixk = projected("w_in_2", 22, X)
        pen = [None]
        for i in range(1, NT):
            L = (i + 1) * P
            s, fs = pg.take()
            for h in range(8):
                rows = slice(32 * (h % 4), 32 * (h % 4) + 32)
                q, tq = ixq[h // 4]
                b, bf = ps.take()
                t = mm(banks[b][:, 0:L], pf(q)[rows, i * P:(i + 1) * P], pf(ixk)[rows, 0:L],
                       True, True, bf, tq, t_ixk, mark=True)
                r, fr = pg.take()
                tr1 = fn(pf(r, L), banks[b][:, 0:L], ACT.Relu, t, fr)
                ps.give(b, tr1)
                wc = narrow(i, 68 + h, 1)
                if h == 0:
                    t2 = ts(pf(s, L), pf(r, L), wc, 0.0, ALU.mult, ALU.add, tr1, fs, t_nar)
                else:
                    t2 = stt(pf(s, L), pf(r, L), wc, pf(s, L), ALU.mult, ALU.add, tr1, t2)
                pg.give(r, t2)
            d = pf(s)[:, L - P:L]
            t2 = tt(d, d, C("causal"), ALU.add, t2)
            t8 = stat(8)
            for _ in range(16):
                t3 = dve(lambda e, s=s, L=L, t8=t8: e.max(t8, pf(s, L)), t2)
                t2 = dve(lambda e, s=s, L=L, t8=t8: e.match_replace(pf(s, L), t8, pf(s, L), TAKEN), t3)
            t2 = ts(pf(s, L), pf(s, L), TAKEN, NEG, ALU.not_equal, ALU.mult, t2)
            pen.append((s, t2))
            mg.fill(2)
        for p, _ in ixq + [(ixk, None)]:
            pg.give(p, t)
        tbs = bias_tiles(range(4, 8))
        qs = [projected("w_in_2", m, X) for m in (18, 19)]
        dk = projected("w_in_2", 24, X)

        def dsa(h, i, L):
            adds, _ = t5(tbs, 4)(h, i, L)
            if i:
                adds.append((pf(pen[i][0], L), pen[i][1]))
            return adds, lambda t: None

        O, last = causal_softmax(
            qs, lambda jt: dk, lambda h, kb: (narrow(kb, 0, 64), t_nar, slice(64 * (h % 2), 64 * (h % 2) + 64)), dsa)
        for p, _ in qs + [dk] + pen[1:] + list(tbs.values()):
            pg.give(p, *last, (dve.sem, dve.n))
        pg.give(nar, *last, (dve.sem, dve.n))
        mg.fill(8)
        drop(X, mg.last)
        mg.close(O)
        Y = mg.result()
        for m in range(8):
            b, t = gemm_t("w_out_2", m, Y)
            add_up(b, t, m, 1.0)
        drop(Y, t)

        X = rms_norm("norm_ffn")
        H = Act()
        for j in range(FT):
            parts = []
            for m in (j, FT + j):
                b, t = gemm_t("w_up_2", m, X)
                p, f = pg.take()
                w_ = lambda jj: col("conv2", jj * 2 * FT + m)
                t = fn(pf(p), banks[b][:, :], ACT.Identity, t, f, scale=w_(2), bias=col("conv2_b", m))
                for sh in (1, 2):
                    t = stt(pf(p)[:, sh:], banks[b][:, 0:SEQ - sh], w_(2 - sh), pf(p)[:, sh:],
                            ALU.mult, ALU.add, t)
                ps.give(b, t)
                parts.append((p, t))
            if j == FT - 1:
                drop(X, (pe.sem, pe.n))
            (g_, tg), (u_, tu) = parts
            t = fn(pf(g_), pf(g_), ACT.Gelu, tg)
            t = tt(pf(g_), pf(g_), pf(u_), ALU.mult, t, tu)
            pg.give(u_, t)
            t = split_into(H, pf(g_), t)
            pg.give(g_, *t)
        for m in range(8):
            b, t = gemm_t("w_down_2", m, H)
            add_up(b, t, m, 1.0)
        drop(H, t)
        r, t = rstd_of([pf(x) for x in R], Rt, C("mean"), EPS_RMS)
        for m in range(8):
            t1 = stt(pf(R[m]), pf(R[m]), col("norm_final", m), pf(r), ALU.mult, ALU.mult, t, Rt[m])
            t_out = sp.dma(out[m], pf(R[m]), s_out, 16 * (m + 1), t1)
        sp.wait(t_out)

        assert state["block"] <= 8 * NSLAB and state["block"] > 8 * (NSLAB - 1), state

        block_ = ctx.enter_context(nc.Block())
        for name, line in (("sync", sp), ("tensor", pe), ("scalar", act), ("vector", dve), ("gpsimd", pool)):
            if line.ops:
                on_engine(block_, name)(line.emit)
    return order


def on_engine(block_, name):
    return {"sync": block_.sync, "tensor": block_.tensor, "scalar": block_.scalar,
            "vector": block_.vector, "gpsimd": block_.gpsimd}[name]



def pad_cols(a, n):
    return np.concatenate([a, np.zeros((a.shape[0], n - a.shape[1]), a.dtype)], axis=1)


def matrices(inp):
    m = {}
    pairs = np.concatenate([np.r_[64 * j:64 * j + 64, 64 * (j + 4):64 * (j + 4) + 64] for j in range(4)])
    for l in range(DEPTH):
        m[("ffn1_gu", l)] = inp["ffn1_w_gu"][l]
        m[("ffn2_gu", l)] = inp["ffn2_w_gu"][l]
        m[("ffn1_down", l)] = inp["ffn1_w_down"][l]
        m[("ffn2_down", l)] = inp["ffn2_w_down"][l]
        w = inp["w_in"][l]
        m[("w_in", l)] = np.concatenate([
            w[:, 0:1536], pad_cols(w[:, 1536:1544], P), w[:, 1544:2056], w[:, 2056:2568][:, pairs],
            w[:, 2568:2824], w[:, 2824:3336]], axis=1)
        m[("gates", l)] = w[:, 3336:6408]
        m[("w_mem_kv", l)] = inp["w_mem_kv"][l]
        for n in range(3):
            b = inp["w_branch"][l, n]
            m[("w_branch", l, n)] = b[pairs] if n == 1 else b
        m[("w_out", l)] = inp["w_out"][l]
    w = inp["w_in_2"][0]
    sb, mb, fx, ds = w[:, 0:768], w[:, 768:1536], w[:, 1536:2308], w[:, 2308:]
    m["w_in_2"] = np.concatenate([
        sb, mb, fx[:, 0:768], ds[:, 0:256], ds[:, 384:640],
        ds[:, 640:672], ds[:, 640:672], ds[:, 640:672], ds[:, 640:672],
        pad_cols(np.concatenate([ds[:, 320:384], fx[:, 768:772], ds[:, 672:680]], axis=1), P),
        ds[:, 256:320], ds[:, 256:320]], axis=1)
    m["w_gate_2"] = np.concatenate([inp["w_gate_2"][0, n] for n in range(4)], axis=1)
    for n in range(4):
        m[("w_branch_2", n)] = inp["w_branch_2"][0, n]
    m["w_out_2"] = inp["w_out_2"][0]
    m["w_up_2"] = inp["w_up_2"][0]
    m["w_down_2"] = inp["w_down_2"][0]
    return m


def cols(a):
    return np.ascontiguousarray(a.reshape(-1, P).T)


def over_rows(a):
    return np.broadcast_to(a.reshape(1, -1), (P, a.size))


def kernel(**inputs):
    import concourse.bacc as _bacc
    from concourse.bass_utils import run_bass_kernel_spmd as _run

    inp = {k: np.ascontiguousarray(v) for k, v in inputs.items()}
    nc = _bacc.Bacc("TRN2", target_bir_lowering=False, num_devices=1)

    def dram(name, shape, kind="ExternalInput"):
        return nc.dram_tensor(name, shape, F32, kind=kind).ap()

    args = [
        dram("weights", (NSLAB, P, 1024)), dram("x_t", (8, P, SEQ)), dram("mem_t", (8, P, NMEM)),
        dram("consts", (P, NCONST)), dram("params", (P, NPARAM)), dram("table", (32, 8)),
        dram("buckets", (33, 640)), dram("out_t", (8, P, SEQ), "ExternalOutput"),
    ]
    order = hybrid_then_mixer_program(nc, *args)

    mats = matrices(inp)
    weights = np.zeros((NSLAB, P, 8, P), np.float32)
    for n, (mat, mt, kt) in enumerate(order):
        weights[n // 8, :, n % 8, :] = mats[mat][kt * P:(kt + 1) * P, mt * P:(mt + 1) * P]
    sinks = inp["swa_sinks"].reshape(DEPTH, 2, 4).transpose(0, 2, 1)
    params = np.concatenate([
        cols(inp["mem_ln_g"]), cols(inp["mem_ln_b"]), cols(inp["ln_g"]), cols(inp["ln_b"]),
        cols(inp["dn_conv_w"]), cols(inp["dn_norm_w"]), over_rows(sinks), over_rows(inp["dn_a_log"]),
        over_rows(inp["dn_dt_bias"]), cols(inp["norm_mix_g_2"]), cols(inp["norm_ffn_g_2"]),
        cols(inp["norm_final_g_2"]), over_rows(inp["fox_b_f_2"]), cols(inp["conv_w_2"]), cols(inp["conv_b_2"]),
    ], axis=1)
    arrays = {
        "weights": weights.reshape(NSLAB, P, 1024),
        "x_t": np.ascontiguousarray(inp["x"][0].T).reshape(8, P, SEQ),
        "mem_t": np.ascontiguousarray(inp["mem"][0].T).reshape(8, P, NMEM),
        "consts": np.concatenate(list(const_tables().values()), axis=1),
        "params": np.ascontiguousarray(params),
        "table": inp["t5_bias_2"],
        "buckets": bucket_rows(),
    }
    r = _run(nc, [arrays], core_ids=[0])
    got = r.results[0]["out_t"]
    return np.ascontiguousarray(got.reshape(DM, SEQ).T).reshape(1, SEQ, DM)
```

```python
import math
from contextlib import ExitStack

import numpy as np
import concourse.bass as bass
from concourse import mybir

F32 = mybir.dt.float32
F32R = mybir.dt.float32r
ALU = mybir.AluOpType
ACT = mybir.ActivationFunctionType
AX = mybir.AxisListType

P = 128
SEQ = 512
NT = SEQ // P
DM = 1024
DT = DM // P
FF = 2816
FT = FF // P
DEPTH = 2
NMEM = 256
ALPHA = (2 * DEPTH) ** 0.25
LN_EPS = 1e-5
RMS_EPS = 1e-6
NEG = -1e30
FILL = -3.0e38
TAKEN = -3.3e38

T5_BUCKETS = 32
T5_MAX_DIST = 128

NSLAB = 561
NRAW = 3
NSPLIT = 3
AHEAD = NSPLIT - 1
PAGES = 76



CONSTS = {}


def const_tables():
    p = np.arange(P)[:, None]
    c = np.arange(P)[None, :]
    t = {
        "ident": (p == c).astype(np.float32),
        "ones": np.ones((P, P), np.float32),
        "mean": np.full((P, P), 1.0 / DM, np.float32),
        "upto": (p <= c).astype(np.float32),
        "before": np.where(c < p, 0.0, NEG).astype(np.float32),
        "since": np.where(c >= p, 0.0, NEG).astype(np.float32),
        "causal": np.where(c <= p, 0.0, NEG).astype(np.float32),
        "later": (c > p).astype(np.float32),
        "ntri": np.where(p > c, -1.0, 0.0).astype(np.float32),
        "nones": np.full((P, P), -1.0, np.float32),
        "nblock8": np.where(p // 8 == c // 8, -1.0, 0.0).astype(np.float32),
    }
    for b in (8, 16, 32, 64):
        t[f"low{b}"] = ((c // b % 2 == 1) & (p // b == c // b - 1)).astype(np.float32)
    kk = np.arange(2 * P)[None, :]
    t["band"] = np.where((kk > p) & (kk <= p + P), 0.0, NEG).astype(np.float32)
    return t


def bucket_rows():
    d = 511 - np.arange(640)
    n = np.maximum(d, 0)
    nf = np.maximum(n, 1).astype(np.float32)
    half = T5_BUCKETS // 2
    large = half + (np.log(nf / half) / math.log(T5_MAX_DIST / half) * (T5_BUCKETS - half)).astype(np.int32)
    bucket = np.where(n < half, n, np.minimum(large, T5_BUCKETS - 1))
    out = np.zeros((33, 640), np.float32)
    out[np.where(d >= 0, bucket, 32), np.arange(640)] = 1.0
    return out


def layout(entries):
    at, out = 0, {}
    for name, n in entries:
        out[name] = (at, n)
        at += n
    return out, at


CONST_AT, NCONST = layout([(k, v.shape[1]) for k, v in const_tables().items()])
PARAM_AT, NPARAM = layout([
    ("mem_ln_g", 8), ("mem_ln_b", 8), ("ln_g", 48), ("ln_b", 48), ("conv", 96), ("dn_norm", 2),
    ("sinks", 16), ("a_log", 8), ("dt_bias", 8), ("norm_mix", 8), ("norm_ffn", 8), ("norm_final", 8),
    ("fox", 4), ("conv2", 132), ("conv2_b", 44),
])



class Line:

    def __init__(self, sem):
        self.sem, self.n, self.seen, self.ops = sem, 0, {}, []

    def wait(self, *tokens):
        for t in tokens:
            if t is None:
                continue
            if isinstance(t, list):
                self.wait(*t)
            elif self.seen.get(id(t[0]), 0) < t[1]:
                self.seen[id(t[0])] = t[1]
                self.ops.append(("wait", t[0], t[1]))

    def __call__(self, fn, *tokens, mark=True):
        self.wait(*tokens)
        if mark:
            self.n += 1
            self.ops.append(("run", fn, self.sem, 1))
            return (self.sem, self.n)
        self.ops.append(("run", fn, None, 0))
        return None

    def dma(self, dst, src, sem, value, *tokens):
        self.wait(*tokens)
        self.ops.append(("run", lambda e: e.dma_start(dst, src), sem, 16))
        return (sem, value)

    def emit(self, e):
        for op in self.ops:
            if op[0] == "wait":
                e.wait_ge(op[1], op[2])
            else:
                i = op[1](e)
                if op[2] is not None:
                    i.then_inc(op[2], op[3])


class Stock:

    def __init__(self, items):
        self.free = [(x, []) for x in items]

    def take(self):
        return self.free.pop(0)

    def give(self, x, *tokens):
        self.free.append((x, [t for t in tokens if t is not None]))


class Act:

    def __init__(self):
        self.hi, self.lo, self.tok, self.pages = [], [], [], []


def go(gen):
    while True:
        try:
            next(gen)
        except StopIteration as s:
            return s.value


class Later:

    def __init__(self, gen):
        self.gen, self.value, self.done = gen, None, False

    def step(self):
        try:
            next(self.gen)
        except StopIteration as s:
            self.value, self.done = s.value, True


class Background:

    def __init__(self):
        self.queue = []

    def add(self, gen):
        w = Later(gen)
        self.queue.append(w)
        return w

    def steps(self, n):
        while n > 0 and self.queue:
            self.queue[0].step()
            n -= 1
            if self.queue[0].done:
                self.queue.pop(0)

    def get(self, w):
        while not w.done:
            self.steps(1)
        return w.value

    def weave(self, gens, n):
        gens = list(gens)
        while gens:
            for g in list(gens):
                try:
                    next(g)
                except StopIteration:
                    gens.remove(g)
                self.steps(n)



def hybrid_then_mixer_program(nc, w, x_t, mem_t, consts, params, table, buckets, out):
    order = []
    ctx = ExitStack()
    with ctx:
        def sb(name, shape, dt=F32):
            return ctx.enter_context(nc.sbuf_tensor(name, shape, dt))

        def sem(name):
            return ctx.enter_context(nc.semaphore(name))

        raw = sb("raw", [P, NRAW, 1024])
        w_hi = sb("w_hi", [P, NSPLIT, 1024], F32R)
        w_lo = sb("w_lo", [P, NSPLIT, 1024], F32R)
        cst = sb("cst", [P, NCONST])
        par = sb("par", [P, NPARAM])
        alb = sb("alb", [P, 48])
        small = sb("small", [P, 2048])
        tab = sb("tab", [33, 8])
        page_f, page_r = [], []
        for i in range(PAGES):
            with nc.sbuf_tensor(f"page_r{i}", [P, 512], F32R) as r:
                page_r.append(r)
            page_f.append(sb(f"page_f{i}", [P, 512]))
        banks = [ctx.enter_context(nc.psum_tensor(f"bank{i}", [P, 512], F32)) for i in range(8)]
        scratch = nc.dram_tensor("bias_rows", (8, P, 640), F32, kind="Internal").ap()

        pe, act, dve, pool = Line(sem("s_pe")), Line(sem("s_act")), Line(sem("s_dve")), Line(sem("s_pool"))
        sp = Line(None)
        s_raw = [sem(f"s_raw{i}") for i in range(NRAW)]
        s_cst, s_par, s_tab = sem("s_cst"), sem("s_par"), sem("s_tab")
        s_x = [sem(f"s_x{i}") for i in range(8)]
        s_oh, s_out = sem("s_oh"), sem("s_out")
        s_bw = [sem(f"s_bw{i}") for i in range(8)]
        s_tb = [sem(f"s_tb{i}") for i in range(8)]

        ps = Stock(range(8))
        pg = Stock(range(PAGES))
        stat_at = [0]

        def stat(n):
            a = stat_at[0]
            stat_at[0] += n
            assert a + n <= 2048
            return small[:, a:a + n]

        def pf(i, n=512):
            return page_f[i][:, 0:n]

        def pr(i, n=512):
            return page_r[i][:, 0:n]

        def C(name):
            a, n = CONST_AT[name]
            return cst[:, a:a + n]

        def col(name, i):
            a, _ = PARAM_AT[name]
            return par[:, a + i:a + i + 1]

        t_cst = sp.dma(cst[:, :], consts, s_cst, 16)
        t_par = sp.dma(par[:, :], params, s_par, 16)
        act.wait(t_cst, t_par)
        dve.wait(t_cst, t_par)
        pe.wait(t_cst)

        def mm(o, l, r, start, stop, *tok, mark=False):
            return pe(lambda e: e.matmul(o, l, r, start=start, stop=stop), *tok, mark=mark)

        def tr(o, i, *tok, mark=False):
            idn = C("ident")
            return pe(lambda e: e.transpose(o, i, idn), *tok, mark=mark)

        def fn(o, i, f, *tok, bias=None, scale=1.0, acc=None):
            kw = {}
            if bias is not None:
                kw["bias"] = bias
            if acc is not None:
                kw["accum_out"] = acc
            return act(lambda e: e.activation(o, i, f, scale=scale, **kw), *tok)

        def tt(o, a, b, op, *tok, on=dve):
            return on(lambda e: e.tensor_tensor(o, a, b, op), *tok)

        def ts(o, a, s1, s2, op0, op1, *tok, on=dve):
            if op1 is None:
                return on(lambda e: e.tensor_scalar(o, a, s1, None, op0), *tok)
            return on(lambda e: e.tensor_scalar(o, a, s1, s2, op0, op1), *tok)

        def stt(o, a, s, b, op0, op1, *tok):
            return dve(lambda e: e.scalar_tensor_tensor(out=o, in0=a, scalar=s, in1=b, op0=op0, op1=op1), *tok)

        def rmax(o, a, *tok):
            return dve(lambda e: e.tensor_reduce(o, a, AX.X, ALU.max), *tok)

        def recip(o, a, *tok):
            return dve(lambda e: e.reciprocal(o, a), *tok)

        cb = stat(4)
        t_cb = []
        for i, v in enumerate((LN_EPS, RMS_EPS, 128 * RMS_EPS, 1.0)):
            t_cb.append(dve(lambda e, i=i, v=v: e.memset(cb[:, i:i + 1], v)))
        EPS_LN, EPS_RMS, EPS_Q, ONE = (cb[:, i:i + 1] for i in range(4))
        act.wait(t_cb[-1])
        a, n = PARAM_AT["ln_b"]
        t_alb = ts(alb[:, :], par[:, a:a + n], ALPHA, None, ALU.mult, None)
        act.wait(t_alb)

        t_hi, t_lo, freed, t_raw = {}, {}, {}, {}
        state = {"block": 0, "raw": 0, "split": 0}

        def load_slab(s):
            t_raw[s] = sp.dma(raw[:, s % NRAW, :], w[s], s_raw[s % NRAW], 16 * (s // NRAW + 1),
                              t_hi.get(s - NRAW), t_lo.get(s - NRAW))

        def split_slab(s):
            r, k = s % NRAW, s % NSPLIT
            t_hi[s] = fn(w_hi[:, k, :], raw[:, r, :], ACT.Copy, t_raw[s], freed.get(s - NSPLIT))
            t_lo[s] = tt(w_lo[:, k, :], raw[:, r, :], w_hi[:, k, :].bitcast(F32), ALU.subtract,
                         t_hi[s], freed.get(s - NSPLIT))

        def ahead(s):
            while state["split"] <= min(s + AHEAD, NSLAB - 1):
                while state["raw"] <= min(state["split"] + NRAW - 1, NSLAB - 1):
                    load_slab(state["raw"])
                    state["raw"] += 1
                split_slab(state["split"])
                state["split"] += 1

        def block(key):
            i = state["block"]
            state["block"] += 1
            order.append(key)
            s, j = divmod(i, 8)
            if j == 0:
                ahead(s)
            c = slice(j * P, j * P + P)
            return w_hi[:, s % NSPLIT, c], w_lo[:, s % NSPLIT, c], [t_hi[s], t_lo[s]], s, j

        bg = Background()

        def product(mat, mt, X, n=512):
            b, bf = ps.take()
            kts = len(X.hi)
            for kt in range(kts):
                wh, wl, wt, s, j = block((mat, mt, kt))
                o = banks[b][:, 0:n]
                mm(o, wh, X.hi[kt], kt == 0, False, bf, wt, X.tok[kt])
                mm(o, wh, X.lo[kt], False, False)
                t = mm(o, wl, X.hi[kt], False, kt == kts - 1, mark=(j == 7 or kt == kts - 1))
                if j == 7:
                    freed[s] = t
                yield
            return b, t

        def gemm_t(mat, mt, X, n=512):
            return go(product(mat, mt, X, n))

        def drop(X, *tok):
            for p in X.pages:
                pg.give(p, *tok)
            X.pages = []

        def split_pair(src, *tok, n=512):
            h, hf = pg.take()
            l, lf = pg.take()
            t1 = fn(pr(h, n), src, ACT.Copy, hf, *tok)
            t2 = tt(pr(l, n), src, pr(h, n).bitcast(F32), ALU.subtract, lf, t1)
            return h, l, [t1, t2]

        def join(X, parts, n=512):
            h, l, t = parts
            X.hi.append(pr(h, n))
            X.lo.append(pr(l, n))
            X.tok.append(t)
            X.pages += [h, l]
            return t

        def split_into(X, src, *tok, n=512):
            return join(X, split_pair(src, *tok, n=n), n)

        def joined(O):
            X = Act()
            for i in sorted(O):
                join(X, O[i])
            return X

        R = [pg.take()[0] for _ in range(8)]
        Rt = [None] * 8

        def first_load(alpha):
            X = Act()
            for m in range(8):
                t = sp.dma(pf(R[m]), x_t[m], s_x[m], 16)
                t2 = split_into(X, pf(R[m]), t)
                Rt[m] = fn(pf(R[m]), pf(R[m]), ACT.Copy, t2, scale=alpha)
            return X

        def add_up(b, t, m, scale):
            Rt[m] = stt(pf(R[m]), banks[b][:, :], scale, pf(R[m]), ALU.mult, ALU.add, t, Rt[m])
            ps.give(b, Rt[m])

        def layer_norm(tiles, toks, g, bcol, scaled, n=512, keep=1.0):
            s, sf = pg.take()
            ta = tt(pf(s, n), pf(tiles[0], n), pf(tiles[1], n), ALU.add, sf, toks[0], toks[1])
            for m in range(2, 8):
                ta = tt(pf(s, n), pf(s, n), pf(tiles[m], n), ALU.add, ta, toks[m])
            b, bf = ps.take()
            tm = mm(banks[b][:, 0:n], C("mean"), pf(s, n), True, True, bf, ta, mark=True)
            pg.give(s, tm)
            v, vf = ps.take()
            td = []
            for m in range(8):
                t = tt(pf(tiles[m], n), pf(tiles[m], n), banks[b][:, 0:n], ALU.subtract, tm, toks[m])
                td.append(t)
                q, qf = pg.take()
                t = fn(pf(q, n), pf(tiles[m], n), ACT.Square, t, qf)
                t = mm(banks[v][:, 0:n], C("mean"), pf(q, n), m == 0, m == 7, vf, t, mark=True)
                pg.give(q, t)
            ps.give(b, td[-1])
            r, rf = pg.take()
            t = fn(pf(r, n), banks[v][:, 0:n], ACT.Sqrt, t, rf, bias=EPS_LN)
            ps.give(v, t)
            tr_ = recip(pf(r, n), pf(r, n), t)
            X = Act()
            out_t = []

            def tail(m):
                h, l = X.pages[2 * m], X.pages[2 * m + 1]
                src = pf(tiles[m], n)
                t2 = stt(pr(l, n), src, bcol(m), pr(h, n).bitcast(F32), ALU.add, ALU.subtract, lfs[m], X.tok[m])
                X.tok[m] = [X.tok[m], t2]
                if keep is not None:
                    bb = scaled(m) if keep != 1.0 else bcol(m)
                    out_t.append(fn(src, src, ACT.Identity, t2, bias=bb, scale=keep))
                else:
                    pg.give(tiles[m], t2, X.tok[m][0])

            lfs = []
            for m in range(8):
                h, hf = pg.take()
                l, lf = pg.take()
                lfs.append(lf)
                src = pf(tiles[m], n)
                t1 = stt(src, src, g(m), pf(r, n), ALU.mult, ALU.mult, tr_, td[m])
                t1 = fn(pr(h, n), src, ACT.Identity, t1, hf, bias=bcol(m))
                X.hi.append(pr(h, n))
                X.lo.append(pr(l, n))
                X.tok.append(t1)
                X.pages += [h, l]
                if m >= 1:
                    tail(m - 1)
            tail(7)
            pg.give(r, X.tok[7][1])
            return X, out_t

        def rstd_of(srcs, toks, c, eps, scale=1.0, n=512):
            v, vf = ps.take()
            k = len(srcs)
            for m in range(k):
                q, qf = pg.take()
                t = fn(pf(q, n), srcs[m], ACT.Square, toks[m], qf)
                t = mm(banks[v][:, 0:n], c, pf(q, n), m == 0, m == k - 1, vf, t, mark=True)
                pg.give(q, t)
            r, rf = pg.take()
            t = fn(pf(r, n), banks[v][:, 0:n], ACT.Sqrt, t, rf, bias=eps, scale=scale)
            ps.give(v, t)
            return r, recip(pf(r, n), pf(r, n), t)

        def rms_norm(name):
            r, t = rstd_of([pf(x) for x in R], Rt, C("mean"), EPS_RMS)
            X = Act()
            for m in range(8):
                p, pfree = pg.take()
                t1 = stt(pf(p), pf(R[m]), col(name, m), pf(r), ALU.mult, ALU.mult, t, Rt[m], pfree)
                t2 = split_into(X, pf(p), t1)
                pg.give(p, *t2)
            pg.give(r, t1)
            return X

        def ffn(X, up, down, scale, beside=None):
            H = Act()
            for j in range(FT):
                b1, tg = gemm_t(up, j, X)
                bu, tu = gemm_t(up, FT + j, X)
                s, sf = pg.take()
                t1 = fn(pf(s), banks[b1][:, :], ACT.Silu, tg, sf)
                ps.give(b1, t1)
                t2 = tt(pf(s), pf(s), banks[bu][:, :], ALU.mult, t1, tu)
                ps.give(bu, t2)
                if j == FT - 1:
                    drop(X, tu)
                t3 = split_into(H, pf(s), t2)
                pg.give(s, *t3)
                if beside is not None:
                    bg.steps(beside)
            for m in range(8):
                b, t = gemm_t(down, m, H)
                add_up(b, t, m, scale)
            drop(H, t)

        def project(mat, mt, X, n=512):
            b, t = yield from product(mat, mt, X, n)
            p, f = pg.take()
            t2 = fn(pf(p, n), banks[b][:, 0:n], ACT.Copy, t, f)
            ps.give(b, t2)
            return p, t2

        def project_n(mat, mt, X, cols=P, tiles=NT):
            q, t = yield from project(mat, mt, X, tiles * P)
            b, bf = ps.take()
            for i in range(tiles):
                t = tr(banks[b][:, i * P:(i + 1) * P], pf(q)[:, i * P:(i + 1) * P], bf, t, mark=True)
            p, f = pg.take()
            src = banks[b][:, 0:tiles * P].rearrange("p (i c) -> p i c", i=tiles)[:, :, 0:cols]
            dst = pf(p, tiles * cols).rearrange("p (i c) -> p i c", i=tiles)
            t2 = fn(dst, src, ACT.Copy, t, f)
            ps.give(b, t2)
            pg.give(q, t)
            return p, t2

        class Merge:
            def __init__(self, X, gate, branch):
                self.X, self.gate, self.branch, self.M, self.last = X, gate, branch, {}, None

            def add(self, n, O):
                for m in range(8):
                    b, t = yield from product(self.gate, n * 8 + m, self.X)
                    g, f = pg.take()
                    tg = fn(pf(g), banks[b][:, :], ACT.Sigmoid, t, f)
                    ps.give(b, tg)
                    b, t = yield from product(self.branch(n), m, O)
                    t2 = tt(pf(g), pf(g), banks[b][:, :], ALU.mult, t, tg)
                    ps.give(b, t2)
                    if m not in self.M:
                        self.M[m] = (g, t2)
                    else:
                        p, tp = self.M[m]
                        t3 = tt(pf(p), pf(p), pf(g), ALU.add, t2, tp)
                        pg.give(g, t3)
                        self.M[m] = (p, t3)
                drop(O, t)

            def result(self):
                Y = Act()
                for m in range(8):
                    p, t = self.M[m]
                    t2 = split_into(Y, pf(p), t)
                    pg.give(p, *t2)
                return Y

        def weights_and_values(Ps, tP, L, vs, ob, i, of, last):
            qs_ = []
            for a, p in enumerate(Ps):
                b, bf = ps.take()
                nk = L // P
                for kb in range(nk):
                    t = tr(banks[b][:, kb * P:(kb + 1) * P], p[0][:, kb * P:(kb + 1) * P],
                           bf, tP[a], mark=(kb == nk - 1))
                q, qf = pg.take()
                t2 = fn(pf(q, L), banks[b][:, 0:L], ACT.Copy, t, qf)
                ps.give(b, t2)
                if p[1] is not None:
                    pg.give(p[1], t)
                qs_.append((q, t2))
            yield
            for a, (q, t2) in enumerate(qs_):
                for kb in range(nk):
                    v, tv, rows = vs(a, kb)
                    t3 = mm(banks[ob[a]][rows, i * P:(i + 1) * P], v, pf(q)[:, kb * P:(kb + 1) * P],
                            kb == 0, kb == nk - 1, t2, tv, of[a] if i == 0 else None, mark=(kb == nk - 1))
                pg.give(q, t3)
                last[a] = t3

        def softmax_rows(p, L, t, sink=None):
            mx, sm = stat(2), stat(2)
            t = rmax(mx[:, 0:1], pf(p, L), t)
            if sink is not None:
                t = tt(mx[:, 0:1], mx[:, 0:1], sink, ALU.max, t)
            t = ts(mx[:, 1:2], mx[:, 0:1], -1.0, None, ALU.mult, None, t)
            t2 = fn(pf(p, L), pf(p, L), ACT.Exp, t, bias=mx[:, 1:2], acc=sm[:, 0:1])
            if sink is not None:
                es = stat(1)
                t2 = fn(es, sink, ACT.Exp, bias=mx[:, 1:2])
                t2 = tt(sm[:, 0:1], sm[:, 0:1], es, ALU.add, t2)
            t2 = recip(sm[:, 1:2], sm[:, 0:1], t2)
            return ts(pf(p, L), pf(p, L), sm[:, 1:2], None, ALU.mult, None, t2)

        s_m = [sem(f"s_m{i}") for i in range(8)]
        X = first_load(ALPHA)

        mem_k, mem_v = {}, {}

        def prepare_memory():
            mt_, mtok = [], []
            for m in range(8):
                p, f = pg.take()
                mt_.append(p)
                mtok.append(sp.dma(pf(p, NMEM), mem_t[m], s_m[m], 16, f))
            yield
            MX, _ = layer_norm(mt_, mtok, lambda m: col("mem_ln_g", m), lambda m: col("mem_ln_b", m), None,
                               n=NMEM, keep=None)
            yield
            for l in range(DEPTH):
                for kv, store in ((0, mem_k), (4, mem_v)):
                    store[l] = []
                    for h2 in range(2):
                        p, f = pg.take()
                        for a in range(2):
                            half = pf(p)[:, a * NMEM:(a + 1) * NMEM]
                            b, t = yield from product(("w_mem_kv", l), kv + 2 * h2 + a, MX, NMEM)
                            if kv == 0:
                                t2 = fn(half, banks[b][:, 0:NMEM], ACT.Copy, t, f)
                                ps.give(b, t2)
                                continue
                            q, qf = pg.take()
                            t2 = fn(pf(q, NMEM), banks[b][:, 0:NMEM], ACT.Copy, t, qf)
                            ps.give(b, t2)
                            yield
                            b, bf = ps.take()
                            for i in range(2):
                                t3 = tr(banks[b][:, i * P:(i + 1) * P], pf(q)[:, i * P:(i + 1) * P], bf, t2,
                                        mark=True)
                            pg.give(q, t3)
                            t2 = fn(half, banks[b][:, 0:NMEM], ACT.Copy, t3, f)
                            ps.give(b, t2)
                            yield
                        store[l].append((p, t2))
            drop(MX, t)

        def cross_head(l, h, q, O):
            sc = P ** -0.5
            ob, of = ps.take()
            kp, tk = mem_k[l][h // 2]
            vp, tv = mem_v[l][h // 2]
            half = slice(h % 2 * 256, h % 2 * 256 + 256)
            q, tq = q
            last = [None]
            for i in range(NT):
                b, bf = ps.take()
                s_ = banks[b][:, 0:256]
                t = mm(s_, pf(q)[:, i * P:(i + 1) * P], pf(kp)[:, half], True, True, bf, tq, tk, mark=True)
                st = stat(4)
                p, f = pg.take()
                t = rmax(st[:, 0:1], s_, t)
                t = ts(st[:, 1:2], st[:, 0:1], -sc, None, ALU.mult, None, t)
                t = fn(pf(p, 256), s_, ACT.Exp, t, f, bias=st[:, 1:2], scale=sc, acc=st[:, 2:3])
                ps.give(b, t)
                t = recip(st[:, 3:4], st[:, 2:3], t)
                t = ts(pf(p, 256), pf(p, 256), st[:, 3:4], None, ALU.mult, None, t)
                yield
                yield from weights_and_values(
                    [(pf(p, 256), p)], [t], 256,
                    lambda a, kb: (pf(vp)[:, half][:, kb * P:(kb + 1) * P], tv, slice(0, P)),
                    [ob], i, [of], last)
                yield
            pg.give(q, last[0])
            O[h] = split_pair(banks[ob][:, :], last[0])
            ps.give(ob, *O[h][2])

        def window_pair(l, j, q, k, v, O):
            sc = 64 ** -0.5
            (q, tq), (k, tk), (v, tv) = q, k, v
            ob, of = ps.take()
            last = [None, None]
            for n in range(NT):
                k0 = max(n - 1, 0) * P
                L = (n + 1) * P - k0
                tp, pgs = [], []
                for a in range(2):
                    b, bf = ps.take()
                    rows = slice(64 * a, 64 * a + 64)
                    t = mm(banks[b][:, 0:L], pf(q)[rows, n * P:(n + 1) * P], pf(k)[rows, k0:k0 + L],
                           True, True, bf, tq, tk, mark=True)
                    p, f = pg.take()
                    t = stt(pf(p, L), banks[b][:, 0:L], sc, C("band")[:, 2 * P - L:2 * P],
                            ALU.mult, ALU.add, t, f)
                    ps.give(b, t)
                    tp.append(softmax_rows(p, L, t, sink=col("sinks", l * 8 + 2 * j + a)))
                    pgs.append((pf(p, L), p))
                yield
                yield from weights_and_values(
                    pgs, tp, L,
                    lambda a, kb: (pf(v)[:, (k0 // P + kb) * P + 64 * a:(k0 // P + kb) * P + 64 * a + 64],
                                   tv, slice(64 * a, 64 * a + 64)),
                    [ob, ob], n, [of, of], last)
                yield
            pg.give(q, *last)
            O[j] = split_pair(banks[ob][:, :], *last)
            ps.give(ob, *O[j][2])

        def row_sums(gcols, tg, idx, prefix=False):
            b, bf = ps.take()
            s, sf = pg.take()
            tl = []
            for i in range(NT):
                g = gcols[:, idx(i):idx(i) + 1]
                tl.append(ts(pf(s)[:, i * P:(i + 1) * P], C("ones"), g, None, ALU.mult, None, sf, tg))
            for i in range(NT):
                o = banks[b][:, i * P:(i + 1) * P]
                pre = range(i) if prefix else ()
                t = mm(o, pf(s)[:, i * P:(i + 1) * P], C("upto"), True, not pre, bf, tl[i], mark=True)
                for j in pre:
                    t = mm(o, pf(s)[:, j * P:(j + 1) * P], C("ones"), False, j == i - 1, mark=True)
            pg.give(s, t)
            return b, t

        def softplus_of(v, n, scratch_cols, *tok):
            t = fn(scratch_cols, v, ACT.Abs, *tok)
            t = fn(scratch_cols, scratch_cols, ACT.Exp, t, scale=-1.0)
            t = fn(scratch_cols, scratch_cols, ACT.Ln, t, bias=ONE)
            return stt(v, v, 0.0, scratch_cols, ALU.max, ALU.add, t)

        def delta_branch(l, X, later):
            ba, t = go(project_n(("w_in", l), 12, X, 8))
            ba3 = pf(ba, 32).rearrange("p (i c) -> p i c", c=8)
            be, g, ea, w1 = stat(16), stat(16), stat(4), stat(16)
            be3, g3 = be.rearrange("p (i h) -> p i h", h=4), g.rearrange("p (i h) -> p i h", h=4)
            t_be = fn(be3, ba3[:, :, 0:4], ACT.Sigmoid, t)
            for h in range(4):
                tg = ts(g3[:, :, h:h + 1], ba3[:, :, 4 + h:5 + h], col("dt_bias", 4 * l + h), None,
                        ALU.add, None, t)
            pg.give(ba, t_be, tg)
            tg = softplus_of(g, 16, w1, tg)
            a0 = PARAM_AT["a_log"][0] + 4 * l
            te = fn(ea, par[:, a0:a0 + 4], ACT.Exp)
            te = ts(ea, ea, -1.0, None, ALU.mult, None, te)
            for h in range(4):
                tg = ts(g3[:, :, h:h + 1], g3[:, :, h:h + 1], ea[:, h:h + 1], None, ALU.mult, None, tg, te)

            def conv(m):
                b, t = yield from product(("w_in", l), m, X)
                p, f = pg.take()
                w_ = lambda j: col("conv", (l * 4 + j) * 12 + m)
                t = fn(pf(p), banks[b][:, :], ACT.Copy, t, f, scale=w_(3))
                for sh in range(1, 4):
                    t = stt(pf(p)[:, sh:], banks[b][:, 0:SEQ - sh], w_(3 - sh), pf(p)[:, sh:],
                            ALU.mult, ALU.add, t)
                ps.give(b, t)
                t = fn(pf(p), pf(p), ACT.Silu, t)
                return p, t

            qkv = [None] * 12
            for m in (0, 4, 8, 1, 5, 9):
                qkv[m] = go(conv(m))
            for m in (2, 6, 10, 3, 7, 11):
                qkv[m] = bg.add(conv(m))

            b, bf = ps.take()
            t = mm(banks[b][:, 0:16], C("upto"), g, True, True, bf, tg, mark=True)
            gc, ngc, eg, beg, kt_ = stat(16), stat(16), stat(16), stat(16), stat(16)
            t_gc = fn(gc, banks[b][:, 0:16], ACT.Copy, t)
            t_eg = fn(eg, banks[b][:, 0:16], ACT.Exp)
            ps.give(b, t_eg)
            t_ngc = ts(ngc, gc, -1.0, None, ALU.mult, None, t_gc)
            t_beg = tt(beg, be, eg, ALU.mult, t_eg, t_be)
            later()

            def unit_length(m):
                if isinstance(qkv[m], Later):
                    qkv[m] = bg.get(qkv[m])
                p, t = qkv[m]
                if m < 4:
                    r, t2 = rstd_of([pf(p)], [t], C("ones"), EPS_Q, scale=float(P))
                else:
                    r, t2 = rstd_of([pf(p)], [t], C("ones"), EPS_RMS)
                t3 = tt(pf(p), pf(p), pf(r), ALU.mult, t2)
                pg.give(r, t3)
                return p, t3

            ot = {}

            def four(f, *tok):
                b, bf = ps.take()
                for i in range(NT):
                    prods = f(i)
                    for n_, (x, y) in enumerate(prods):
                        t = mm(banks[b][:, i * P:(i + 1) * P], x, y, n_ == 0, n_ == len(prods) - 1,
                               bf, *tok, mark=(i == NT - 1 and n_ == len(prods) - 1))
                return b, t

            def T(p, i):
                return pf(p)[:, i * P:(i + 1) * P]

            def v4(ap):
                return ap.rearrange("p (i c) -> p i c", i=4)

            def bc(c):
                return C(c).rearrange("p (o c) -> p o c", o=1).broadcast_to([P, 4, P])

            def percol(s16, h):
                return s16.rearrange("p (i h) -> p i h", h=4)[:, :, h:h + 1].broadcast_to([P, 4, P])

            def head(h):
                q, tq = unit_length(h)
                k, tk = unit_length(4 + h)
                yield
                if isinstance(qkv[8 + h], Later):
                    qkv[8 + h] = bg.get(qkv[8 + h])
                vv, tv = qkv[8 + h]
                gb, tgb = row_sums(g, tg, lambda i: 4 * i + h)
                d1, f1 = pg.take()
                d2, f2 = pg.take()
                e_, f3 = pg.take()
                G4 = v4(banks[gb][:, :])
                t1 = tt(v4(pf(d1)), bc("before"), G4, ALU.subtract, tgb, f1)
                t2 = tt(v4(pf(d2)), G4, bc("since"), ALU.add, tgb, f2)
                gl = stat(4)
                tgl = dve(lambda e, gl=gl, G4=G4: e.tensor_copy(gl, G4[:, :, P - 1:P]), tgb)
                t3 = fn(pf(e_), banks[gb][:, :], ACT.Exp, tgb, f3, tgl, t2)
                ps.give(gb, t3)
                ktl, egl = stat(4), stat(4)
                for i in range(NT):
                    c = 4 * i + h
                    td1 = fn(T(d1, i), T(d1, i), ACT.Exp, t1, bias=gc[:, c:c + 1])
                    td2 = fn(T(d2, i), T(d2, i), ACT.Exp, t2, t_ngc, bias=ngc[:, c:c + 1])
                    tkt = fn(ktl[:, i:i + 1], gl[:, i:i + 1], ACT.Exp, tgl, bias=ngc[:, c:c + 1])
                tegl = fn(egl, gl, ACT.Exp)
                yield
                b, bf = ps.take()
                for i in range(NT):
                    t = tr(banks[b][:, i * P:(i + 1) * P], T(k, i), bf, tk, mark=(i == 3))
                kbe, f1 = pg.take()
                tke, f2 = pg.take()
                vb, f3 = pg.take()
                t4 = tt(v4(pf(kbe)), v4(banks[b][:, :]), percol(beg, h), ALU.mult, t, f1, t_beg)
                kt3 = ktl.rearrange("p (i o) -> p i o", o=1).broadcast_to([P, 4, P])
                t5 = tt(v4(pf(tke)), v4(banks[b][:, :]), kt3, ALU.mult, f2, tkt)
                ps.give(b, t5)
                b, bf = ps.take()
                for i in range(NT):
                    t = tr(banks[b][:, i * P:(i + 1) * P], T(vv, i), bf, tv, mark=(i == 3))
                t6 = tt(v4(pf(vb)), v4(banks[b][:, :]), percol(be, h), ALU.mult, t, f3, t_be)
                ps.give(b, t6)
                pg.give(vv, t)
                yield
                b, t = four(lambda i: [(T(k, i), T(k, i))])
                t = tt(pf(d1), pf(d1), banks[b][:, :], ALU.mult, t, td1)
                ps.give(b, t)
                tA = tt(v4(pf(d1)), v4(pf(d1)), percol(be, h), ALU.mult, t)
                b, t = four(lambda i: [(T(k, i), T(q, i))], tq, tk)
                tQ = tt(pf(d2), pf(d2), banks[b][:, :], ALU.mult, t, td2)
                ps.give(b, tQ)
                pg.give(k, t)
                tqd = tt(pf(q), pf(q), pf(e_), ALU.mult, t, t3)
                pg.give(e_, tqd)
                yield
                b, bf = ps.take()
                for i in range(NT):
                    t = tr(banks[b][:, i * P:(i + 1) * P], T(d1, i), bf, tA, mark=(i == 3))
                at, f = pg.take()
                tAT = fn(pf(at), banks[b][:, :], ACT.Copy, t, f)
                ps.give(b, tAT)
                n1, f1 = pg.take()
                n1t, f2 = pg.take()
                ta = tt(v4(pf(n1)), v4(pf(d1)), bc("nblock8"), ALU.mult, tA, f1)
                pg.give(d1, ta, tAT)
                tb = tt(v4(pf(n1t)), v4(pf(at)), bc("nblock8"), ALU.mult, tAT, f2)
                x, f3 = pg.take()
                xt, f4 = pg.take()
                tx = tt(v4(pf(x)), v4(pf(n1)), bc("ident"), ALU.add, ta, f3)
                txt = tt(v4(pf(xt)), v4(pf(n1t)), bc("ident"), ALU.add, tb, f4)
                yield
                tn = [ta, tb]
                for lev in range(2):
                    b1, u1 = four(lambda i: [(T(n1t, i), T(n1, i))], tn)
                    if lev == 0:
                        b2, u2 = four(lambda i: [(T(n1, i), T(n1t, i))])
                        tb = dve(lambda e, b2=b2, n1t=n1t: e.tensor_copy(pf(n1t), banks[b2][:, :]), u2, u1, txt)
                        ps.give(b2, tb)
                    ta = fn(pf(n1), banks[b1][:, :], ACT.Copy, u1, u2, tx)
                    ps.give(b1, ta)
                    yield
                    tn = [ta, tb]
                    b1, u1 = four(lambda i: [(T(xt, i), T(n1, i))], tn, txt)
                    b2, u2 = four(lambda i: [(T(n1, i), T(xt, i))])
                    tx = tt(pf(x), pf(x), banks[b1][:, :], ALU.add, u1, tx)
                    txt = tt(pf(xt), pf(xt), banks[b2][:, :], ALU.add, u2, txt)
                    ps.give(b1, tx)
                    ps.give(b2, txt)
                    if lev == 0:
                        yield
                low, prod = n1, n1t
                tlast = u2
                t = tt(v4(pf(low)), v4(pf(at)), bc("low8"), ALU.mult, tlast, tAT)
                yield
                for size in (8, 16, 32, 64):
                    b1, u1 = four(lambda i: [(T(low, i), T(x, i))], t, tx)
                    tp = fn(pf(prod), banks[b1][:, :], ACT.Copy, u1, tlast)
                    ps.give(b1, tp)
                    if size < 64:
                        t = tt(v4(pf(low)), v4(pf(at)), bc(f"low{2 * size}"), ALU.mult, u1)
                    yield
                    b2, u2 = four(lambda i: [(T(prod, i), T(xt, i))], tp, txt)
                    if size < 64:
                        b1, u1 = four(lambda i: [(T(xt, i), T(prod, i))])
                        tx = tt(pf(x), pf(x), banks[b1][:, :], ALU.subtract, u1, tx)
                        ps.give(b1, tx)
                        u2 = u1
                    txt = tt(pf(xt), pf(xt), banks[b2][:, :], ALU.subtract, u2, txt)
                    ps.give(b2, txt)
                    tlast = u2
                    yield
                pg.give(n1t, tlast)
                pg.give(at, tlast)
                pg.give(x, tlast)
                wt, f = n1, None
                b, t = four(lambda i: [(T(kbe, i), T(xt, i))], t4, txt)
                twt = fn(pf(wt), banks[b][:, :], ACT.Copy, t, tlast, scale=-1.0)
                ps.give(b, twt)
                pg.give(kbe, t)
                yield
                S, f = pg.take()
                vn, f2 = pg.take()
                ob, of = ps.take()
                tS = None
                for i in range(NT):
                    b, bf = ps.take()
                    o = banks[b][:, 0:P]
                    t = mm(o, T(xt, i), T(vb, i), True, i == 0, bf, txt, t6, mark=True)
                    if i:
                        t = mm(o, T(wt, i), pf(S, P), False, True, twt, tS, mark=True)
                    tv_ = fn(T(vn, i), o, ACT.Copy, t, f2)
                    ps.give(b, tv_)
                    yield
                    oo = banks[ob][:, i * P:(i + 1) * P]
                    if i:
                        mm(oo, pf(S, P), T(q, i), True, False, of, tqd, tS)
                    to = mm(oo, T(vn, i), T(d2, i), i == 0, True, of, tv_, tQ, mark=True)
                    if i < NT - 1:
                        b, bf = ps.take()
                        o = banks[b][:, 0:P]
                        t = mm(o, T(tke, i), T(vn, i), True, True, bf, t5, mark=True)
                        if i == 0:
                            tS = dve(lambda e, o=o, S=S: e.tensor_copy(pf(S, P), o), t, f)
                        else:
                            tS = stt(pf(S, P), pf(S, P), egl[:, i:i + 1], o, ALU.mult, ALU.add, t, to, tegl)
                        ps.give(b, tS)
                        yield
                for z in (S, vn, xt, wt, vb, tke, d2, q):
                    pg.give(z, to, tS)
                o_, f = pg.take()
                t = fn(pf(o_), banks[ob][:, :], ACT.Copy, to, f)
                ps.give(ob, t)
                ot[h] = (o_, t)

            bg.weave([head(0), head(1)], 1)
            bg.weave([head(2), head(3)], 1)

            def finish():
                O = {}
                for h in range(4):
                    o_, t = ot[h]
                    r, t2 = rstd_of([pf(o_)], [t], C("ones"), EPS_RMS, scale=1.0 / P)
                    t2 = stt(pf(o_), pf(o_), col("dn_norm", l), pf(r), ALU.mult, ALU.mult, t2)
                    pg.give(r, t2)
                    b, t = yield from product(("w_in", l), 13 + h, X)
                    z, f = pg.take()
                    t3 = fn(pf(z), banks[b][:, :], ACT.Silu, t, f)
                    ps.give(b, t3)
                    t = tt(pf(o_), pf(o_), pf(z), ALU.mult, t2, t3)
                    pg.give(z, t)
                    O[h] = split_pair(pf(o_), t)
                    pg.give(o_, *O[h][2])
                return joined(O)

            return finish

        for l in range(DEPTH):
            if l == 0:
                mem = bg.add(prepare_memory())
                ffn(X, ("ffn1_gu", l), ("ffn1_down", l), 0.5, beside=12)
                bg.get(mem)
            else:
                ffn(X, ("ffn1_gu", l), ("ffn1_down", l), 0.5)
            lng = lambda n: (lambda m: col("ln_g", (l * 3 + n) * 8 + m), lambda m: col("ln_b", (l * 3 + n) * 8 + m),
                             lambda m: alb[:, (l * 3 + n) * 8 + m:(l * 3 + n) * 8 + m + 1])
            X, Rt[:] = layer_norm(R, Rt, *lng(0), keep=ALPHA)
            mg = Merge(X, ("gates", l), lambda n: ("w_branch", l, n))
            ahead_ = {}

            def attention_projections():
                for h in range(4):
                    ahead_["x", h] = bg.add(project(("w_in", l), 23 + h, X))
                for j in range(4):
                    ahead_["s", j] = bg.add(project(("w_in", l), 17 + j, X))
                ahead_["k"] = bg.add(project(("w_in", l), 21, X))
                ahead_["v"] = bg.add(project_n(("w_in", l), 22, X))

            finish = delta_branch(l, X, attention_projections)
            got = {k: bg.get(v) for k, v in ahead_.items()}

            def first_branch():
                O = yield from finish()
                yield from mg.add(0, O)

            merge0 = bg.add(first_branch())
            OX, OS = {}, {}

            def crosses(h0):
                for h in (h0, h0 + 1):
                    yield from cross_head(l, h, got["x", h], OX)

            def windows(j0):
                for j in (j0, j0 + 1):
                    yield from window_pair(l, j, got["s", j], got["k"], got["v"], OS)

            bg.weave([crosses(0), windows(0), crosses(2), windows(2)], 2)
            for p, t in mem_k[l] + mem_v[l] + [got["k"], got["v"]]:
                pg.give(p, (pe.sem, pe.n))
            bg.get(merge0)
            go(mg.add(2, joined(OX)))
            go(mg.add(1, joined(OS)))
            drop(X, (pe.sem, pe.n))
            Y = mg.result()
            for m in range(8):
                b, t = gemm_t(("w_out", l), m, Y)
                add_up(b, t, m, 1.0)
            drop(Y, t)
            X, Rt[:] = layer_norm(R, Rt, *lng(1), keep=ALPHA)
            ffn(X, ("ffn2_gu", l), ("ffn2_down", l), 0.5)
            X, Rt[:] = layer_norm(R, Rt, *lng(2), keep=ALPHA if l < DEPTH - 1 else 1.0)
        drop(X)

        X = rms_norm("norm_mix")

        t = dve(lambda e: e.memset(tab[:, :], NEG))
        t_tab = sp.dma(tab[0:32, :], table, s_tab, 16, t)
        oh0, f0 = pg.take()
        oh1, f1 = pg.take()
        t_oh = sp.dma(pf(oh0)[0:33, :], buckets[:, 0:512], s_oh, 16, f0)
        t_oh = sp.dma(pf(oh1)[0:33, 0:128], buckets[:, 512:640], s_oh, 32, f1)
        t_bw = []
        for h in range(8):
            th, f = pg.take()
            t1 = ts(pf(th)[0:33, 0:P], C("ones")[0:33, :], tab[:, h:h + 1], None, ALU.mult, None, f, t, t_tab)
            b, bf = ps.take()
            b2, bf2 = ps.take()
            mm(banks[b][:, :], pf(th)[0:33, 0:P], pf(oh0)[0:33, :], True, True, bf, bf2, t1, t_oh)
            t1 = mm(banks[b2][:, 0:P], pf(th)[0:33, 0:P], pf(oh1)[0:33, 0:P], True, True, mark=True)
            pg.give(th, t1)
            bb, f2 = pg.take()
            bb2, f3 = pg.take()
            t2 = fn(pf(bb), banks[b][:, :], ACT.Copy, t1, f2)
            t3 = fn(pf(bb2, P), banks[b2][:, 0:P], ACT.Copy, t1, f3)
            ps.give(b, t2)
            ps.give(b2, t3)
            sp.dma(scratch[h, :, 0:512], pf(bb), s_bw[h], 16, t2)
            t_bw.append(sp.dma(scratch[h, :, 512:640], pf(bb2, P), s_bw[h], 32, t3))
            pg.give(bb, t_bw[h])
            pg.give(bb2, t_bw[h])
        pg.give(oh0, t1)
        pg.give(oh1, t1)

        def bias_tiles(hs):
            out_ = {}
            for h in hs:
                p, f = pg.take()
                src = bass.AP(tensor=scratch.tensor, offset=h * 640 * P + 127, ap=[[639, P], [1, 512]])
                out_[h] = (p, sp.dma(pf(p), src, s_tb[h], 16, t_bw[h], f))
            return out_

        sc = 64 ** -0.5
        mg = Merge(X, "w_gate_2", lambda n: ("w_branch_2", n))

        def stick_breaking(jt, q, k, v, O):
            (q, tq), (k, tk), (v, tv) = q, k, v
            ob, of = ps.take()
            last = []
            for a in range(2):
                rows = slice(64 * a, 64 * a + 64)
                zp, ap_, tz, ta_ = [], [], [], []
                for i in range(NT):
                    W = SEQ - i * P
                    b, bf = ps.take()
                    t = mm(banks[b][:, 0:W], pf(k)[rows, i * P:(i + 1) * P], pf(q)[rows, i * P:SEQ],
                           True, True, bf, tq, tk, mark=True)
                    z, fz = pg.take()
                    s, fs = pg.take()
                    t1 = ts(pf(z, W), banks[b][:, 0:W], sc, None, ALU.mult, None, t, fz)
                    ps.give(b, t1)
                    t = fn(pf(s, W), pf(z, W), ACT.Abs, t1, fs)
                    t = fn(pf(s, W), pf(s, W), ACT.Exp, t, scale=-1.0)
                    t = fn(pf(s, W), pf(s, W), ACT.Ln, t, bias=ONE)
                    t = stt(pf(s, W), pf(z, W), 0.0, pf(s, W), ALU.max, ALU.add, t)
                    t1 = tt(pf(z, W), pf(z, W), pf(s, W), ALU.subtract, t)
                    t = tt(pf(s, P), pf(s, P), C("later"), ALU.mult, t1)
                    zp.append(z)
                    ap_.append(s)
                    tz.append(t1)
                    ta_.append(t)
                    yield
                for i in range(NT):
                    W = SEQ - i * P
                    b, bf = ps.take()
                    t = mm(banks[b][:, 0:W], C("ntri"), pf(ap_[i], W), True, i == NT - 1, bf, ta_, mark=True)
                    for j in range(i + 1, NT):
                        t = mm(banks[b][:, (j - i) * P:W], C("nones"), pf(ap_[j], SEQ - j * P),
                               False, j == NT - 1, mark=True)
                    t = tt(pf(zp[i], W), pf(zp[i], W), banks[b][:, 0:W], ALU.add, t, tz[i])
                    ps.give(b, t)
                    t = fn(pf(zp[i], W), pf(zp[i], W), ACT.Exp, t)
                    tz[i] = tt(pf(zp[i], P), pf(zp[i], P), C("later"), ALU.mult, t)
                    yield
                for i in range(NT):
                    W = SEQ - i * P
                    t = mm(banks[ob][rows, i * P:SEQ], pf(v)[:, i * P + 64 * a:i * P + 64 * a + 64],
                           pf(zp[i], W), i == 0, i == NT - 1, of, tz[i], tv, mark=True)
                for i in range(NT):
                    pg.give(zp[i], t)
                    pg.give(ap_[i], t)
                last.append(t)
                yield
            O[jt] = split_pair(banks[ob][:, :], last)
            ps.give(ob, *O[jt][2])
            for p in (q, k, v):
                pg.give(p, *last)

        def causal_softmax(jt, q, k, vof, bias, O):
            (q, tq), (k, tk) = q, k
            ob, of = ps.take()
            last = [None, None]
            for i in range(NT):
                L = (i + 1) * P
                tp, pgs = [], []
                for a in range(2):
                    rows = slice(64 * a, 64 * a + 64)
                    b, bf = ps.take()
                    t = mm(banks[b][:, 0:L], pf(q)[rows, i * P:(i + 1) * P], pf(k)[rows, 0:L],
                           True, True, bf, tq, tk, mark=True)
                    p, f = pg.take()
                    adds, after = bias(2 * jt + a, i, L)
                    t = stt(pf(p, L), banks[b][:, 0:L], sc, adds[0][0], ALU.mult, ALU.add, t, f, adds[0][1])
                    ps.give(b, t)
                    for ap_, tok in adds[1:]:
                        t = tt(pf(p, L), pf(p, L), ap_, ALU.add, t, tok)
                    after(t)
                    tp.append(softmax_rows(p, L, t))
                    pgs.append((pf(p, L), p))
                yield
                yield from weights_and_values(pgs, tp, L, lambda a, kb: vof(2 * jt + a, kb),
                                              [ob, ob], i, [of, of], last)
                yield
            O[jt] = split_pair(banks[ob][:, :], *last)
            ps.give(ob, *O[jt][2])
            pg.give(q, *last)

        def proj(m):
            return project("w_in_2", m, X)

        nar, t_nar = go(project_n("w_in_2", 23, X))

        def narrow(i, c0, n):
            return pf(nar)[:, i * P + c0:i * P + c0 + n]

        ixq = [go(proj(m)) for m in (20, 21)]
        ixk, t_ixk = go(proj(22))
        pen = [None]

        def best_keys():
            for i in range(1, NT):
                L = (i + 1) * P
                s, fs = pg.take()
                for h in range(8):
                    rows = slice(32 * (h % 4), 32 * (h % 4) + 32)
                    q, tq = ixq[h // 4]
                    b, bf = ps.take()
                    t = mm(banks[b][:, 0:L], pf(q)[rows, i * P:(i + 1) * P], pf(ixk)[rows, 0:L],
                           True, True, bf, tq, t_ixk, mark=True)
                    r, fr = pg.take()
                    tr1 = fn(pf(r, L), banks[b][:, 0:L], ACT.Relu, t, fr)
                    ps.give(b, tr1)
                    wc = narrow(i, 68 + h, 1)
                    if h == 0:
                        t2 = ts(pf(s, L), pf(r, L), wc, 0.0, ALU.mult, ALU.add, tr1, fs, t_nar)
                    else:
                        t2 = stt(pf(s, L), pf(r, L), wc, pf(s, L), ALU.mult, ALU.add, tr1, t2)
                    pg.give(r, t2)
                    if h % 2:
                        yield
                d = pf(s)[:, L - P:L]
                t2 = tt(d, d, C("causal"), ALU.add, t2)
                t8 = stat(8)
                for r_ in range(16):
                    t3 = dve(lambda e, s=s, L=L, t8=t8: e.max(t8, pf(s, L)), t2)
                    t2 = dve(lambda e, s=s, L=L, t8=t8: e.match_replace(pf(s, L), t8, pf(s, L), TAKEN), t3)
                    if r_ % 2:
                        yield
                t2 = ts(pf(s, L), pf(s, L), TAKEN, NEG, ALU.not_equal, ALU.mult, t2)
                pen.append((s, t2))
            for p in [x[0] for x in ixq] + [ixk]:
                pg.give(p, t)

        sq = [go(proj(m)) for m in (0, 1)]
        sk = [go(proj(m)) for m in (2, 3)]
        sv = [go(project_n("w_in_2", m, X)) for m in (4, 5)]
        OSB = {}
        mq = [bg.add(proj(m)) for m in (6, 7)]
        mk = [bg.add(proj(m)) for m in (8, 9)]
        mv = [bg.add(project_n("w_in_2", m, X)) for m in (10, 11)]
        fq = [bg.add(proj(m)) for m in (12, 13)]
        fk = [bg.add(proj(m)) for m in (14, 15)]
        fv = [bg.add(project_n("w_in_2", m, X)) for m in (16, 17)]
        bg.weave([stick_breaking(0, sq[0], sk[0], sv[0], OSB), stick_breaking(1, sq[1], sk[1], sv[1], OSB),
                  best_keys()], 1)
        mq, mk, mv, fq, fk, fv = ([bg.get(x) for x in y] for y in (mq, mk, mv, fq, fk, fv))
        dq = [bg.add(proj(m)) for m in (18, 19)]
        dk = bg.add(proj(24))
        merges = [bg.add(mg.add(0, joined(OSB)))]
        tbs = bias_tiles(range(4))

        def v_of(vs):
            def f(h, kb):
                v, tv = vs[h // 2]
                a = h % 2
                return pf(v)[:, kb * P + 64 * a:kb * P + 64 * a + 64], tv, slice(64 * a, 64 * a + 64)
            return f

        def t5(tbs, h0):
            def f(h, i, L):
                p, t = tbs[h0 + h]
                return [(pf(p)[:, 384 - P * i:384 - P * i + L], t)], lambda t: None
            return f

        fl, w1, cc = stat(16), stat(16), stat(16)
        fl3 = fl.rearrange("p (i h) -> p i h", h=4)
        for i in range(NT):
            a0 = PARAM_AT["fox"][0]
            t = tt(fl3[:, i, :], narrow(i, 64, 4), par[:, a0:a0 + 4], ALU.add, t_nar)
        t = ts(fl, fl, -1.0, None, ALU.mult, None, t)
        t = softplus_of(fl, 16, w1, t)
        b, bf = ps.take()
        for i in range(NT):
            o = banks[b][:, 4 * i:4 * i + 4]
            tc = mm(o, C("upto"), fl[:, 4 * i:4 * i + 4], True, i == 0, bf, t, mark=True)
            for j in range(i):
                tc = mm(o, C("ones"), fl[:, 4 * j:4 * j + 4], False, j == i - 1, mark=True)
        t_cc = fn(cc, banks[b][:, 0:16], ACT.Copy, tc, scale=-1.0)
        ps.give(b, t_cc)
        crow = []
        for h in range(4):
            b, tb = row_sums(fl, t, lambda i: 4 * i + h, prefix=True)
            p, f = pg.take()
            tb = fn(pf(p), banks[b][:, :], ACT.Copy, tb, f)
            ps.give(b, tb)
            crow.append((p, tb))
            bg.steps(4)

        def fox(h, i, L):
            p, t = crow[h]
            q, f = pg.take()
            t = ts(pf(q, L), pf(p, L), cc[:, 4 * i + h:4 * i + h + 1], None, ALU.add, None, t, t_cc, f)
            d = pf(q)[:, L - P:L]
            t = tt(d, d, C("causal"), ALU.add, t)
            return [(pf(q, L), t)], lambda t: pg.give(q, t)

        def dsa(tbs):
            def f(h, i, L):
                adds, _ = t5(tbs, 4)(h, i, L)
                if i:
                    adds.append((pf(pen[i][0], L), pen[i][1]))
                return adds, lambda t: None
            return f

        OMB, OFX, ODS = {}, {}, {}

        def moba():
            for jt in range(2):
                yield from causal_softmax(jt, mq[jt], mk[jt], v_of(mv), t5(tbs, 0), OMB)
            for p, _ in mk + mv + list(tbs.values()):
                pg.give(p, (pe.sem, pe.n), (dve.sem, dve.n))
            merges.append(bg.add(mg.add(1, joined(OMB))))

        def forgetting():
            for jt in range(2):
                yield from causal_softmax(jt, fq[jt], fk[jt], v_of(fv), fox, OFX)
            for p, _ in fk + fv + crow:
                pg.give(p, (pe.sem, pe.n), (dve.sem, dve.n))
            merges.append(bg.add(mg.add(2, joined(OFX))))

        bg.weave([moba(), forgetting()], 2)
        tbs = bias_tiles(range(4, 8))
        dq, dk = [bg.get(x) for x in dq], bg.get(dk)
        f_ = dsa(tbs)
        vd = lambda h, kb: (narrow(kb, 0, 64), t_nar, slice(64 * (h % 2), 64 * (h % 2) + 64))
        bg.weave([causal_softmax(jt, dq[jt], dk, vd, f_, ODS) for jt in range(2)], 3)
        for p, _ in [dk] + pen[1:] + list(tbs.values()):
            pg.give(p, (pe.sem, pe.n), (dve.sem, dve.n))
        pg.give(nar, (pe.sem, pe.n), (dve.sem, dve.n))
        for m_ in merges:
            bg.get(m_)
        go(mg.add(3, joined(ODS)))
        drop(X, (pe.sem, pe.n))
        Y = mg.result()
        for m in range(8):
            b, t = gemm_t("w_out_2", m, Y)
            add_up(b, t, m, 1.0)
        drop(Y, t)

        X = rms_norm("norm_ffn")
        H = Act()
        for j in range(FT):
            parts = []
            for m in (j, FT + j):
                b, t = gemm_t("w_up_2", m, X)
                p, f = pg.take()
                w_ = lambda jj: col("conv2", jj * 2 * FT + m)
                t = fn(pf(p), banks[b][:, :], ACT.Identity, t, f, scale=w_(2), bias=col("conv2_b", m))
                for sh in (1, 2):
                    t = stt(pf(p)[:, sh:], banks[b][:, 0:SEQ - sh], w_(2 - sh), pf(p)[:, sh:],
                            ALU.mult, ALU.add, t)
                ps.give(b, t)
                parts.append((p, t))
            if j == FT - 1:
                drop(X, (pe.sem, pe.n))
            (g_, tg), (u_, tu) = parts
            t = fn(pf(g_), pf(g_), ACT.Gelu, tg)
            t = tt(pf(g_), pf(g_), pf(u_), ALU.mult, t, tu)
            pg.give(u_, t)
            t = split_into(H, pf(g_), t)
            pg.give(g_, *t)
        for m in range(8):
            b, t = gemm_t("w_down_2", m, H)
            add_up(b, t, m, 1.0)
        drop(H, t)
        r, t = rstd_of([pf(x) for x in R], Rt, C("mean"), EPS_RMS)
        for m in range(8):
            t1 = stt(pf(R[m]), pf(R[m]), col("norm_final", m), pf(r), ALU.mult, ALU.mult, t, Rt[m])
            t_out = sp.dma(out[m], pf(R[m]), s_out, 16 * (m + 1), t1)
        sp.wait(t_out)

        assert state["block"] <= 8 * NSLAB and state["block"] > 8 * (NSLAB - 1), state

        block_ = ctx.enter_context(nc.Block())
        for name, line in (("sync", sp), ("tensor", pe), ("scalar", act), ("vector", dve), ("gpsimd", pool)):
            if line.ops:
                on_engine(block_, name)(line.emit)
    return order


def on_engine(block_, name):
    return {"sync": block_.sync, "tensor": block_.tensor, "scalar": block_.scalar,
            "vector": block_.vector, "gpsimd": block_.gpsimd}[name]



def pad_cols(a, n):
    return np.concatenate([a, np.zeros((a.shape[0], n - a.shape[1]), a.dtype)], axis=1)


def matrices(inp):
    m = {}
    pairs = np.concatenate([np.r_[64 * j:64 * j + 64, 64 * (j + 4):64 * (j + 4) + 64] for j in range(4)])
    for l in range(DEPTH):
        m[("ffn1_gu", l)] = inp["ffn1_w_gu"][l]
        m[("ffn2_gu", l)] = inp["ffn2_w_gu"][l]
        m[("ffn1_down", l)] = inp["ffn1_w_down"][l]
        m[("ffn2_down", l)] = inp["ffn2_w_down"][l]
        w = inp["w_in"][l]
        m[("w_in", l)] = np.concatenate([
            w[:, 0:1536], pad_cols(w[:, 1536:1544], P), w[:, 1544:2056], w[:, 2056:2568][:, pairs],
            w[:, 2568:2824], w[:, 2824:3336]], axis=1)
        m[("gates", l)] = w[:, 3336:6408]
        m[("w_mem_kv", l)] = inp["w_mem_kv"][l]
        for n in range(3):
            b = inp["w_branch"][l, n]
            m[("w_branch", l, n)] = b[pairs] if n == 1 else b
        m[("w_out", l)] = inp["w_out"][l]
    w = inp["w_in_2"][0]
    sb, mb, fx, ds = w[:, 0:768], w[:, 768:1536], w[:, 1536:2308], w[:, 2308:]
    m["w_in_2"] = np.concatenate([
        sb, mb, fx[:, 0:768], ds[:, 0:256], ds[:, 384:640],
        ds[:, 640:672], ds[:, 640:672], ds[:, 640:672], ds[:, 640:672],
        pad_cols(np.concatenate([ds[:, 320:384], fx[:, 768:772], ds[:, 672:680]], axis=1), P),
        ds[:, 256:320], ds[:, 256:320]], axis=1)
    m["w_gate_2"] = np.concatenate([inp["w_gate_2"][0, n] for n in range(4)], axis=1)
    for n in range(4):
        m[("w_branch_2", n)] = inp["w_branch_2"][0, n]
    m["w_out_2"] = inp["w_out_2"][0]
    m["w_up_2"] = inp["w_up_2"][0]
    m["w_down_2"] = inp["w_down_2"][0]
    return m


def cols(a):
    return np.ascontiguousarray(a.reshape(-1, P).T)


def over_rows(a):
    return np.broadcast_to(a.reshape(1, -1), (P, a.size))


def kernel(**inputs):
    import concourse.bacc as _bacc
    from concourse.bass_utils import run_bass_kernel_spmd as _run

    inp = {k: np.ascontiguousarray(v) for k, v in inputs.items()}
    nc = _bacc.Bacc("TRN2", target_bir_lowering=False, num_devices=1)

    def dram(name, shape, kind="ExternalInput"):
        return nc.dram_tensor(name, shape, F32, kind=kind).ap()

    args = [
        dram("weights", (NSLAB, P, 1024)), dram("x_t", (8, P, SEQ)), dram("mem_t", (8, P, NMEM)),
        dram("consts", (P, NCONST)), dram("params", (P, NPARAM)), dram("table", (32, 8)),
        dram("buckets", (33, 640)), dram("out_t", (8, P, SEQ), "ExternalOutput"),
    ]
    order = hybrid_then_mixer_program(nc, *args)

    mats = matrices(inp)
    weights = np.zeros((NSLAB, P, 8, P), np.float32)
    for n, (mat, mt, kt) in enumerate(order):
        weights[n // 8, :, n % 8, :] = mats[mat][kt * P:(kt + 1) * P, mt * P:(mt + 1) * P]
    sinks = inp["swa_sinks"].reshape(DEPTH, 2, 4).transpose(0, 2, 1)
    params = np.concatenate([
        cols(inp["mem_ln_g"]), cols(inp["mem_ln_b"]), cols(inp["ln_g"]), cols(inp["ln_b"]),
        cols(inp["dn_conv_w"]), cols(inp["dn_norm_w"]), over_rows(sinks), over_rows(inp["dn_a_log"]),
        over_rows(inp["dn_dt_bias"]), cols(inp["norm_mix_g_2"]), cols(inp["norm_ffn_g_2"]),
        cols(inp["norm_final_g_2"]), over_rows(inp["fox_b_f_2"]), cols(inp["conv_w_2"]), cols(inp["conv_b_2"]),
    ], axis=1)
    arrays = {
        "weights": weights.reshape(NSLAB, P, 1024),
        "x_t": np.ascontiguousarray(inp["x"][0].T).reshape(8, P, SEQ),
        "mem_t": np.ascontiguousarray(inp["mem"][0].T).reshape(8, P, NMEM),
        "consts": np.concatenate(list(const_tables().values()), axis=1),
        "params": np.ascontiguousarray(params),
        "table": inp["t5_bias_2"],
        "buckets": bucket_rows(),
    }
    r = _run(nc, [arrays], core_ids=[0])
    got = r.results[0]["out_t"]
    return np.ascontiguousarray(got.reshape(DM, SEQ).T).reshape(1, SEQ, DM)
```

```python
import math
from contextlib import ExitStack

import numpy as np
import concourse.bass as bass
from concourse import mybir

F32 = mybir.dt.float32
F32R = mybir.dt.float32r
ALU = mybir.AluOpType
ACT = mybir.ActivationFunctionType
AX = mybir.AxisListType

P = 128
SEQ = 512
NT = SEQ // P
DM = 1024
DT = DM // P
FF = 2816
FT = FF // P
DEPTH = 2
NMEM = 256
ALPHA = (2 * DEPTH) ** 0.25
LN_EPS = 1e-5
RMS_EPS = 1e-6
NEG = -1e30
FILL = -3.0e38
TAKEN = -3.3e38

T5_BUCKETS = 32
T5_MAX_DIST = 128

NSLAB = 561
NRAW = 3
NSPLIT = 3
AHEAD = NSPLIT - 1
ROUND_AT = 2
REST_AT = 5
PAGES = 76
N_SB, N_MB, N_FX, N_DS = 2.4, 1.9, 2.3, 1.8



CONSTS = {}


def const_tables():
    p = np.arange(P)[:, None]
    c = np.arange(P)[None, :]
    t = {
        "ident": (p == c).astype(np.float32),
        "ones": np.ones((P, P), np.float32),
        "mean": np.full((P, P), 1.0 / DM, np.float32),
        "upto": (p <= c).astype(np.float32),
        "before": np.where(c < p, 0.0, NEG).astype(np.float32),
        "since": np.where(c >= p, 0.0, NEG).astype(np.float32),
        "causal": np.where(c <= p, 0.0, NEG).astype(np.float32),
        "later": (c > p).astype(np.float32),
        "ntri": np.where(p > c, -1.0, 0.0).astype(np.float32),
        "nones": np.full((P, P), -1.0, np.float32),
        "nblock8": np.where(p // 8 == c // 8, -1.0, 0.0).astype(np.float32),
    }
    for b in (8, 16, 32, 64):
        t[f"low{b}"] = ((c // b % 2 == 1) & (p // b == c // b - 1)).astype(np.float32)
    kk = np.arange(2 * P)[None, :]
    t["band"] = np.where((kk > p) & (kk <= p + P), 0.0, NEG).astype(np.float32)
    return t


def bucket_rows():
    d = 511 - np.arange(640)
    n = np.maximum(d, 0)
    nf = np.maximum(n, 1).astype(np.float32)
    half = T5_BUCKETS // 2
    large = half + (np.log(nf / half) / math.log(T5_MAX_DIST / half) * (T5_BUCKETS - half)).astype(np.int32)
    bucket = np.where(n < half, n, np.minimum(large, T5_BUCKETS - 1))
    out = np.zeros((33, 640), np.float32)
    out[np.where(d >= 0, bucket, 32), np.arange(640)] = 1.0
    return out


def layout(entries):
    at, out = 0, {}
    for name, n in entries:
        out[name] = (at, n)
        at += n
    return out, at


CONST_AT, NCONST = layout([(k, v.shape[1]) for k, v in const_tables().items()])
PARAM_AT, NPARAM = layout([
    ("mem_ln_g", 8), ("mem_ln_b", 8), ("ln_g", 48), ("ln_b", 48), ("conv", 96), ("dn_norm", 2),
    ("sinks", 16), ("a_log", 8), ("dt_bias", 8), ("norm_mix", 8), ("norm_ffn", 8), ("norm_final", 8),
    ("fox", 4), ("conv2", 132), ("conv2_b", 44),
])



class Line:

    def __init__(self, sem):
        self.sem, self.n, self.seen, self.ops = sem, 0, {}, []

    def wait(self, *tokens):
        for t in tokens:
            if t is None:
                continue
            if isinstance(t, list):
                self.wait(*t)
            elif self.seen.get(id(t[0]), 0) < t[1]:
                self.seen[id(t[0])] = t[1]
                self.ops.append(("wait", t[0], t[1]))

    def __call__(self, fn, *tokens, mark=True):
        self.wait(*tokens)
        if mark:
            self.n += 1
            self.ops.append(("run", fn, self.sem, 1))
            return (self.sem, self.n)
        self.ops.append(("run", fn, None, 0))
        return None

    def dma(self, dst, src, sem, value, *tokens):
        self.wait(*tokens)
        self.ops.append(("run", lambda e: e.dma_start(dst, src), sem, 16))
        return (sem, value)

    def emit(self, e):
        for op in self.ops:
            if op[0] == "wait":
                e.wait_ge(op[1], op[2])
            else:
                i = op[1](e)
                if op[2] is not None:
                    i.then_inc(op[2], op[3])


class Stock:

    def __init__(self, items):
        self.free = [(x, []) for x in items]

    def take(self):
        return self.free.pop(0)

    def give(self, x, *tokens):
        self.free.append((x, [t for t in tokens if t is not None]))


class Act:

    def __init__(self, tiles=None):
        self.tiles = tiles
        self.hi, self.lo, self.tok, self.pages = [], [], [], []


def go(gen):
    while True:
        try:
            next(gen)
        except StopIteration as s:
            return s.value


def finished(work):
    while not all(w.done for w in work):
        for w in work:
            if not w.done:
                w.step()
    return [w.value for w in work]


class Later:

    def __init__(self, gen):
        self.gen, self.value, self.done = gen, None, False

    def step(self):
        try:
            next(self.gen)
        except StopIteration as s:
            self.value, self.done = s.value, True


def feed(norm, gens, meanwhile=None):
    norm, work = Later(norm), [Later(g) for g in gens]
    norm.step()
    if meanwhile:
        meanwhile()
    while not norm.done:
        norm.step()
        for w in work:
            w.step()
    return finished(work)


class Background:

    def __init__(self):
        self.queue = []

    def add(self, gen):
        w = Later(gen)
        self.queue.append(w)
        return w

    def steps(self, n):
        while n > 0 and self.queue:
            self.queue[0].step()
            n -= 1
            if self.queue[0].done:
                self.queue.pop(0)

    def get(self, w):
        while not w.done:
            self.steps(1)
        return w.value

    def beside(self, gen, every):
        n = 0
        while True:
            try:
                next(gen)
            except StopIteration as s:
                return s.value
            n += 1
            if n % every == 0:
                self.steps(1)

    def weave(self, gens, n, longer=None):
        gens, owed = list(gens), 0.0
        while gens:
            if longer is not None and not longer.done:
                longer.step()
            for g in list(gens):
                try:
                    k = next(g)
                except StopIteration:
                    gens.remove(g)
                    continue
                owed += n if k is None else k
                self.steps(int(owed))
                owed -= int(owed)



def hybrid_then_mixer_program(nc, w, x_t, mem_t, consts, params, table, buckets, out):
    order = []
    ctx = ExitStack()
    with ctx:
        def sb(name, shape, dt=F32):
            return ctx.enter_context(nc.sbuf_tensor(name, shape, dt))

        def sem(name):
            return ctx.enter_context(nc.semaphore(name))

        raw = sb("raw", [P, NRAW, 1024])
        w_hi = sb("w_hi", [P, NSPLIT, 1024], F32R)
        w_lo = sb("w_lo", [P, NSPLIT, 1024], F32R)
        cst = sb("cst", [P, NCONST])
        par = sb("par", [P, NPARAM])
        alb = sb("alb", [P, 48])
        small = sb("small", [P, 2048])
        tab = sb("tab", [33, 8])
        page_f, page_r = [], []
        for i in range(PAGES):
            with nc.sbuf_tensor(f"page_r{i}", [P, 512], F32R) as r:
                page_r.append(r)
            page_f.append(sb(f"page_f{i}", [P, 512]))
        banks = [ctx.enter_context(nc.psum_tensor(f"bank{i}", [P, 512], F32)) for i in range(8)]
        scratch = nc.dram_tensor("bias_rows", (8, P, 640), F32, kind="Internal").ap()

        pe, act, dve, pool = Line(sem("s_pe")), Line(sem("s_act")), Line(sem("s_dve")), Line(sem("s_pool"))
        sp = Line(None)
        s_raw = [sem(f"s_raw{i}") for i in range(NRAW)]
        s_cst, s_par, s_tab = sem("s_cst"), sem("s_par"), sem("s_tab")
        s_x = [sem(f"s_x{i}") for i in range(8)]
        s_oh, s_out = sem("s_oh"), sem("s_out")
        s_bw = [sem(f"s_bw{i}") for i in range(8)]
        s_tb = [sem(f"s_tb{i}") for i in range(8)]

        ps = Stock(range(8))
        pg = Stock(range(PAGES))
        stat_at = [0]

        def stat(n):
            a = stat_at[0]
            stat_at[0] += n
            assert a + n <= 2048
            return small[:, a:a + n]

        def pf(i, n=512):
            return page_f[i][:, 0:n]

        def pr(i, n=512):
            return page_r[i][:, 0:n]

        def C(name):
            a, n = CONST_AT[name]
            return cst[:, a:a + n]

        def col(name, i):
            a, _ = PARAM_AT[name]
            return par[:, a + i:a + i + 1]


        def mm(o, l, r, start, stop, *tok, mark=False):
            return pe(lambda e: e.matmul(o, l, r, start=start, stop=stop), *tok, mark=mark)

        def tr(o, i, *tok, mark=False):
            idn = C("ident")
            return pe(lambda e: e.transpose(o, i, idn), *tok, mark=mark)

        def fn(o, i, f, *tok, bias=None, scale=1.0, acc=None):
            kw = {}
            if bias is not None:
                kw["bias"] = bias
            if acc is not None:
                kw["accum_out"] = acc
            return act(lambda e: e.activation(o, i, f, scale=scale, **kw), *tok)

        def tt(o, a, b, op, *tok, on=dve):
            return on(lambda e: e.tensor_tensor(o, a, b, op), *tok)

        def ts(o, a, s1, s2, op0, op1, *tok, on=dve):
            if op1 is None:
                return on(lambda e: e.tensor_scalar(o, a, s1, None, op0), *tok)
            return on(lambda e: e.tensor_scalar(o, a, s1, s2, op0, op1), *tok)

        def stt(o, a, s, b, op0, op1, *tok):
            return dve(lambda e: e.scalar_tensor_tensor(out=o, in0=a, scalar=s, in1=b, op0=op0, op1=op1), *tok)

        def rmax(o, a, *tok):
            return dve(lambda e: e.tensor_reduce(o, a, AX.X, ALU.max), *tok)

        def recip(o, a, *tok):
            return dve(lambda e: e.reciprocal(o, a), *tok)

        cb = stat(5)
        t_cb = []
        for i, v in enumerate((LN_EPS, RMS_EPS, 128 * RMS_EPS, 1.0, 4 * RMS_EPS)):
            t_cb.append(dve(lambda e, i=i, v=v: e.memset(cb[:, i:i + 1], v)))
        EPS_LN, EPS_RMS, EPS_Q, ONE, EPS_4 = (cb[:, i:i + 1] for i in range(5))
        act.wait(t_cb[-1])
        dull = stat(1)

        def load_constants():
            t_cst = sp.dma(cst[:, :], consts, s_cst, 16)
            t_par = sp.dma(par[:, :], params, s_par, 16)
            yield
            act.wait(t_cst, t_par)
            dve.wait(t_cst, t_par)
            pe.wait(t_cst)
            a, n = PARAM_AT["ln_b"]
            act.wait(ts(alb[:, :], par[:, a:a + n], ALPHA, None, ALU.mult, None))

        t_hi, t_lo, freed, t_raw = {}, {}, {}, {}
        state = {"block": 0, "raw": 0, "round": 0, "rest": 0}

        def load_slab(s):
            t_raw[s] = sp.dma(raw[:, s % NRAW, :], w[s], s_raw[s % NRAW], 16 * (s // NRAW + 1),
                              t_hi.get(s - NRAW), t_lo.get(s - NRAW))

        def round_slab(s):
            t_hi[s] = fn(w_hi[:, s % NSPLIT, :], raw[:, s % NRAW, :], ACT.Copy, t_raw[s], freed.get(s - NSPLIT))

        def rest_slab(s):
            k = s % NSPLIT
            t_lo[s] = tt(w_lo[:, k, :], raw[:, s % NRAW, :], w_hi[:, k, :].bitcast(F32), ALU.subtract,
                         t_hi[s], freed.get(s - NSPLIT))

        def rounded(s):
            while state["round"] <= min(s, NSLAB - 1):
                while state["raw"] <= min(state["rest"] + NRAW - 1, NSLAB - 1):
                    load_slab(state["raw"])
                    state["raw"] += 1
                round_slab(state["round"])
                state["round"] += 1

        def rested(s):
            while state["rest"] <= min(s, NSLAB - 1):
                rounded(state["rest"])
                rest_slab(state["rest"])
                state["rest"] += 1

        def block(key):
            i = state["block"]
            state["block"] += 1
            order.append(key)
            s, j = divmod(i, 8)
            if j == 0:
                rested(s + AHEAD - 1)
            if j == ROUND_AT:
                rounded(s + AHEAD)
            if j == REST_AT:
                rested(s + AHEAD)
            c = slice(j * P, j * P + P)
            return w_hi[:, s % NSPLIT, c], w_lo[:, s % NSPLIT, c], [t_hi[s], t_lo[s]], s, j

        bg = Background()

        def product(mat, mt, X, n=512):
            b, bf = ps.take()
            kts = X.tiles or len(X.hi)
            for kt in range(kts):
                wh, wl, wt, s, j = block((mat, mt, kt))
                o = banks[b][:, 0:n]
                mm(o, wh, X.hi[kt], kt == 0, False, bf, wt, X.tok[kt])
                mm(o, wh, X.lo[kt], False, False)
                t = mm(o, wl, X.hi[kt], False, kt == kts - 1, mark=(j == 7 or kt == kts - 1))
                if j == 7:
                    freed[s] = t
                yield
            return b, t

        def gemm_t(mat, mt, X, n=512):
            return go(product(mat, mt, X, n))

        def drop(X, *tok):
            for p in X.pages:
                pg.give(p, *tok)
            X.pages = []

        def split_pair(src, *tok, n=512):
            h, hf = pg.take()
            l, lf = pg.take()
            t1 = fn(pr(h, n), src, ACT.Copy, hf, *tok)
            t2 = tt(pr(l, n), src, pr(h, n).bitcast(F32), ALU.subtract, lf, t1)
            return h, l, [t1, t2]

        def join(X, parts, n=512):
            h, l, t = parts
            X.hi.append(pr(h, n))
            X.lo.append(pr(l, n))
            X.tok.append(t)
            X.pages += [h, l]
            return t

        def split_into(X, src, *tok, n=512):
            return join(X, split_pair(src, *tok, n=n), n)

        def joined(O):
            X = Act()
            for i in sorted(O):
                join(X, O[i])
            return X

        R = [pg.take()[0] for _ in range(8)]
        Rt = [None] * 8

        def first_load(X, alpha):
            for m in range(8):
                t = sp.dma(pf(R[m]), x_t[m], s_x[m], 16)
                if m == 0:
                    rounded(NRAW - 1)
                t2 = split_into(X, pf(R[m]), t)
                Rt[m] = fn(pf(R[m]), pf(R[m]), ACT.Copy, t2, scale=alpha)
                yield

        def add_up(b, t, m, scale):
            Rt[m] = stt(pf(R[m]), banks[b][:, :], scale, pf(R[m]), ALU.mult, ALU.add, t, Rt[m])
            ps.give(b, Rt[m])

        def normalised(X, tiles, centred, r, tr_, g, bcol, keep=None, n=512):
            def tail(m):
                h, l = X.pages[2 * m], X.pages[2 * m + 1]
                src = pf(tiles[m], n)
                t2 = stt(pr(l, n), src, bcol(m), pr(h, n).bitcast(F32), ALU.add, ALU.subtract, lfs[m], X.tok[m])
                X.tok[m] = [X.tok[m], t2]
                if keep is not None:
                    k, bb = keep(m)
                    Rt[m] = fn(src, src, ACT.Identity, t2, bias=bb, scale=k)
                else:
                    pg.give(tiles[m], t2, X.tok[m][0])

            lfs = []
            td = [centred(0), centred(1)]
            for m in range(8):
                if m > 1:
                    td.append(centred(m))
                h, hf = pg.take()
                l, lf = pg.take()
                lfs.append(lf)
                src = pf(tiles[m], n)
                t1 = stt(src, src, g(m), pf(r, n), ALU.mult, ALU.mult, tr_, td[m])
                t1 = fn(pr(h, n), src, ACT.Identity, t1, hf, bias=bcol(m))
                X.hi.append(pr(h, n))
                X.lo.append(pr(l, n))
                X.tok.append(t1)
                X.pages += [h, l]
                if m >= 1:
                    tail(m - 1)
                yield
            tail(7)
            pg.give(r, X.tok[7][1])

        def layer_norm(tiles, toks, g, bcol, n):
            s, sf = pg.take()
            ta = tt(pf(s, n), pf(tiles[0], n), pf(tiles[1], n), ALU.add, sf, toks[0], toks[1])
            for m in range(2, 8):
                ta = tt(pf(s, n), pf(s, n), pf(tiles[m], n), ALU.add, ta, toks[m])
            for _ in range(6):
                yield
            b, bf = ps.take()
            tm = mm(banks[b][:, 0:n], C("mean"), pf(s, n), True, True, bf, ta, mark=True)
            pg.give(s, tm)
            yield
            td, sq = [], []
            for m in range(8):
                td.append(tt(pf(tiles[m], n), pf(tiles[m], n), banks[b][:, 0:n], ALU.subtract, tm, toks[m]))
                q, qf = pg.take()
                sq.append((q, fn(pf(q, n), pf(tiles[m], n), ACT.Square, td[m], qf)))
                yield
            ps.give(b, td[-1])
            v, vf = ps.take()
            for m, (q, t) in enumerate(sq):
                t = mm(banks[v][:, 0:n], C("mean"), pf(q, n), m == 0, m == 7, vf, t, mark=True)
                pg.give(q, t)
                yield
            r, rf = pg.take()
            t = inverse_root(pf(r, n), banks[v][:, 0:n], EPS_LN, 1.0, t, rf)
            ps.give(v, t)
            X = Act()
            yield from normalised(X, tiles, lambda m: td[m], r, t, g, bcol, n=n)
            for _ in range(4):
                yield
            return X

        def inverse_root(o, i, eps, scale, *tok):
            t = fn(o, i, ACT.Ln, *tok, bias=eps, scale=scale)
            return fn(o, o, ACT.Exp, t, scale=-0.5)

        class Squares:

            def __init__(self, summed=True):
                self.summed = summed
                self.v, self.vf = ps.take()
                self.sq = {}

            def tile(self, m):
                q, qf = pg.take()
                self.sq[m] = (q, fn(pf(q), pf(R[m]), ACT.Square, Rt[m], qf))
                if m == 6:
                    fn(dull, ONE, ACT.Ln)

            def behind(self, m):
                for k in sorted(self.sq):
                    q, t = self.sq.pop(k)
                    if not self.summed:
                        self.t = mm(banks[self.v][:, :], C("mean"), pf(q), k == 0, k == 7, self.vf, t, mark=True)
                        pg.give(q, self.t)
                    elif k == 0:
                        self.sum, self.tsum = q, t
                    elif k < 7:
                        self.tsum = tt(pf(self.sum), pf(self.sum), pf(q), ALU.add, self.tsum, t)
                        pg.give(q, self.tsum)
                    else:
                        o = banks[self.v][:, :]
                        t2 = mm(o, C("mean"), pf(self.sum), True, False, self.vf, self.tsum, mark=True)
                        self.t = mm(o, C("mean"), pf(q), False, True, t, mark=True)
                        pg.give(self.sum, t2)
                        pg.give(q, self.t)

            def rstd(self):
                r, rf = pg.take()
                t = inverse_root(pf(r), banks[self.v][:, :], EPS_RMS, 1.0, self.t, rf)
                ps.give(self.v, t)
                return r, t

        class Spread(Squares):

            def tile(self, m):
                if m == 0:
                    self.s, self.sf = pg.take()
                elif m == 1:
                    self.ts = tt(pf(self.s), pf(R[0]), pf(R[1]), ALU.add, self.sf, Rt[0], Rt[1])
                else:
                    self.ts = tt(pf(self.s), pf(self.s), pf(R[m]), ALU.add, self.ts, Rt[m])
                if m > 3:
                    super().tile(m)

            def behind(self, m):
                if m == 3:
                    b, bf = ps.take()
                    t = mm(banks[b][:, :], C("mean"), pf(self.s), True, True, bf, self.ts, mark=True)
                    c, cf = pg.take()
                    tc = fn(pf(c), banks[b][:, :], ACT.Copy, t, cf, scale=2.0)
                    ps.give(b, tc)
                    for k in (4, 0, 1, 2, 3, 5, 6, 7):
                        Rt[k] = tt(pf(R[k]), pf(R[k]), pf(c), ALU.subtract, tc, Rt[k])
                        if k < 4:
                            super().tile(k)
                            if k == 1:
                                self.ts = tt(pf(self.s), pf(R[0]), pf(R[1]), ALU.add, t, Rt[0], Rt[1])
                            elif k > 1:
                                self.ts = tt(pf(self.s), pf(self.s), pf(R[k]), ALU.add, self.ts, Rt[k])
                    pg.give(c, Rt[7])
                elif m > 3:
                    super().behind(m)

            def result(self):
                b, bf = ps.take()
                tm = mm(banks[b][:, :], C("mean"), pf(self.s), True, True, bf, self.ts, mark=True)
                pg.give(self.s, tm)
                r, rf = pg.take()
                t = fn(pf(r), banks[b][:, :], ACT.Square, tm, rf)
                t = tt(pf(r), banks[self.v][:, :], pf(r), ALU.subtract, self.t, t)
                ps.give(self.v, t)
                t = inverse_root(pf(r), pf(r), EPS_LN, 1.0, t)

                def centred(m):
                    Rt[m] = tt(pf(R[m]), pf(R[m]), banks[b][:, :], ALU.subtract, tm, Rt[m])
                    if m == 7:
                        ps.give(b, Rt[m])
                    return Rt[m]
                return centred, r, t

        def residual_norm(X, stats, k, keep):
            centred, r, tr_ = stats.result()
            g, bc_ = (lambda m: col("ln_g", k * 8 + m)), (lambda m: col("ln_b", k * 8 + m))
            kept = lambda m: (keep, bc_(m) if keep == 1.0 else alb[:, k * 8 + m:k * 8 + m + 1])
            yield from normalised(X, R, centred, r, tr_, g, bc_, keep=kept)

        def last_norm(stats, k):
            centred, r, t = stats.result()
            td = [centred(0), centred(1)]
            after = Squares(summed=False)
            for m in range(8):
                if m > 1:
                    td.append(centred(m))
                t1 = stt(pf(R[m]), pf(R[m]), col("ln_g", k * 8 + m), pf(r), ALU.mult, ALU.mult, t, td[m])
                Rt[m] = fn(pf(R[m]), pf(R[m]), ACT.Identity, t1, bias=col("ln_b", k * 8 + m))
                after.tile(m)
                bg.steps(1)
                after.behind(m)
            pg.give(r, t1)
            return after

        def update(mat, H, scale, stats):
            for m in range(8):
                b, t = gemm_t(mat, m, H)
                if m:
                    stats.behind(m - 1)
                add_up(b, t, m, scale)
                stats.tile(m)
            drop(H, t)
            stats.behind(7)
            return stats

        def rms_norm(X, name, stats):
            r, t = stats.rstd()

            def rest(p, h, th):
                l, lf = pg.take()
                t2 = tt(pr(l), pf(p), pr(h).bitcast(F32), ALU.subtract, lf, th)
                join(X, (h, l, [th, t2]))
                pg.give(p, t2)

            before = None
            for m in range(8):
                p, pfree = pg.take()
                h, hf = pg.take()
                t1 = stt(pf(p), pf(R[m]), col(name, m), pf(r), ALU.mult, ALU.mult, t, Rt[m], pfree)
                th = fn(pr(h), pf(p), ACT.Copy, hf, t1)
                if before:
                    rest(*before)
                before = (p, h, th)
                yield
            rest(*before)
            pg.give(r, t1)

        def ffn(source, X, up, down, scale):
            H = Act()
            first = feed(source, [product(up, m, X) for m in (0, FT, 1, FT + 1)])
            for j in range(FT):
                if j < 2:
                    (b1, tg), (bu, tu) = first[2 * j:2 * j + 2]
                else:
                    (b1, tg), (bu, tu) = (bg.beside(product(up, m, X), 1) for m in (j, FT + j))
                s, sf = pg.take()
                t1 = fn(pf(s), banks[b1][:, :], ACT.Silu, tg, sf)
                ps.give(b1, t1)
                t2 = tt(pf(s), pf(s), banks[bu][:, :], ALU.mult, t1, tu)
                ps.give(bu, t2)
                if j == FT - 1:
                    drop(X, tu)
                t3 = split_into(H, pf(s), t2)
                pg.give(s, *t3)
            return update(down, H, scale, Spread())

        def project(mat, mt, X, n=512):
            b, t = yield from product(mat, mt, X, n)
            p, f = pg.take()
            t2 = fn(pf(p, n), banks[b][:, 0:n], ACT.Copy, t, f)
            ps.give(b, t2)
            return p, t2

        def project_n(mat, mt, X, cols=P, tiles=NT):
            q, t = yield from project(mat, mt, X, tiles * P)
            b, bf = ps.take()
            for i in range(tiles):
                t = tr(banks[b][:, i * P:(i + 1) * P], pf(q)[:, i * P:(i + 1) * P], bf, t, mark=True)
            p, f = pg.take()
            src = banks[b][:, 0:tiles * P].rearrange("p (i c) -> p i c", i=tiles)[:, :, 0:cols]
            dst = pf(p, tiles * cols).rearrange("p (i c) -> p i c", i=tiles)
            t2 = fn(dst, src, ACT.Copy, t, f)
            ps.give(b, t2)
            pg.give(q, t)
            return p, t2

        class Merge:

            def __init__(self, X, gate, branch):
                self.X, self.gate, self.branch, self.M, self.Y = X, gate, branch, {}, Act()

            def add(self, n, O, final=False):
                for m in range(8):
                    b, t = yield from product(self.gate, n * 8 + m, self.X)
                    g, f = pg.take()
                    tg = fn(pf(g), banks[b][:, :], ACT.Tanh, t, f, scale=0.5)
                    ps.give(b, tg)
                    b, t = yield from product(self.branch(n), m, O)
                    t2 = stt(pf(g), pf(g), 1.0, banks[b][:, :], ALU.add, ALU.mult, t, tg)
                    ps.give(b, t2)
                    if m not in self.M:
                        self.M[m] = (g, t2)
                    else:
                        p, tp = self.M[m]
                        t3 = tt(pf(p), pf(p), pf(g), ALU.add, t2, tp)
                        pg.give(g, t3)
                        self.M[m] = (p, t3)
                    if final and m:
                        self.part(m - 1)
                drop(O, t)

            def part(self, m):
                p, t = self.M[m]
                h, hf = pg.take()
                t1 = fn(pr(h), pf(p), ACT.Copy, hf, t, scale=0.5)
                l, lf = pg.take()
                t2 = stt(pr(l), pf(p), 0.5, pr(h).bitcast(F32), ALU.mult, ALU.subtract, lf, t1)
                join(self.Y, (h, l, [t1, t2]))
                pg.give(p, t2)

            def result(self):
                self.part(7)
                return self.Y

        def weights_and_values(Ps, tP, L, vs, ob, i, of, last):
            qs_ = []
            for a, p in enumerate(Ps):
                b, bf = ps.take()
                nk = L // P
                for kb in range(nk):
                    t = tr(banks[b][:, kb * P:(kb + 1) * P], p[0][:, kb * P:(kb + 1) * P],
                           bf, tP[a], mark=(kb == nk - 1))
                q, qf = pg.take()
                t2 = fn(pf(q, L), banks[b][:, 0:L], ACT.Copy, t, qf)
                ps.give(b, t2)
                if p[1] is not None:
                    pg.give(p[1], t)
                qs_.append((q, t2))
            yield
            for a, (q, t2) in enumerate(qs_):
                for kb in range(nk):
                    v, tv, rows = vs(a, kb)
                    t3 = mm(banks[ob[a]][rows, i * P:(i + 1) * P], v, pf(q)[:, kb * P:(kb + 1) * P],
                            kb == 0, kb == nk - 1, t2, tv, of[a] if i == 0 else None, mark=(kb == nk - 1))
                pg.give(q, t3)
                last[a] = t3

        def softmax_rows(rows, L):
            st = []
            for p, t, sink in rows:
                x = stat(5)
                t = rmax(x[:, 0:1], pf(p, L), t)
                if sink is not None:
                    t = tt(x[:, 0:1], x[:, 0:1], sink, ALU.max, t)
                st.append((x, ts(x[:, 1:2], x[:, 0:1], -1.0, None, ALU.mult, None, t)))
            yield
            te = []
            for (x, t), (p, _, sink) in zip(st, rows):
                t2 = fn(pf(p, L), pf(p, L), ACT.Exp, t, bias=x[:, 1:2], acc=x[:, 2:3])
                if sink is not None:
                    t2 = fn(x[:, 4:5], sink, ACT.Exp, bias=x[:, 1:2])
                te.append(t2)
            yield
            out_ = []
            for (x, _), t2, (p, _, sink) in zip(st, te, rows):
                if sink is not None:
                    t2 = tt(x[:, 2:3], x[:, 2:3], x[:, 4:5], ALU.add, t2)
                t2 = recip(x[:, 3:4], x[:, 2:3], t2)
                out_.append(ts(pf(p, L), pf(p, L), x[:, 3:4], None, ALU.mult, None, t2))
            yield
            return out_

        s_m = [sem(f"s_m{i}") for i in range(8)]
        X = Act(DT)
        source = first_load(X, ALPHA)

        mem_k, mem_v = {}, {}

        def prepare_memory():
            yield from load_constants()
            mt_, mtok = [], []
            for m in range(8):
                p, f = pg.take()
                mt_.append(p)
                mtok.append(sp.dma(pf(p, NMEM), mem_t[m], s_m[m], 16, f))
            yield
            MX = yield from layer_norm(mt_, mtok, lambda m: col("mem_ln_g", m), lambda m: col("mem_ln_b", m), NMEM)
            yield
            for l in range(DEPTH):
                for kv, store in ((0, mem_k), (4, mem_v)):
                    store[l] = []
                    for h2 in range(2):
                        p, f = pg.take()
                        for a in range(2):
                            half = pf(p)[:, a * NMEM:(a + 1) * NMEM]
                            b, t = yield from product(("w_mem_kv", l), kv + 2 * h2 + a, MX, NMEM)
                            if kv == 0:
                                t2 = fn(half, banks[b][:, 0:NMEM], ACT.Copy, t, f)
                                ps.give(b, t2)
                                continue
                            q, qf = pg.take()
                            t2 = fn(pf(q, NMEM), banks[b][:, 0:NMEM], ACT.Copy, t, qf)
                            ps.give(b, t2)
                            yield
                            b, bf = ps.take()
                            for i in range(2):
                                t3 = tr(banks[b][:, i * P:(i + 1) * P], pf(q)[:, i * P:(i + 1) * P], bf, t2,
                                        mark=True)
                            pg.give(q, t3)
                            t2 = fn(half, banks[b][:, 0:NMEM], ACT.Copy, t3, f)
                            ps.give(b, t2)
                            yield
                        store[l].append((p, t2))
            drop(MX, t)

        def cross_head(l, h, q, O):
            sc = P ** -0.5
            ob, of = ps.take()
            kp, tk = mem_k[l][h // 2]
            vp, tv = mem_v[l][h // 2]
            half = slice(h % 2 * 256, h % 2 * 256 + 256)
            q, tq = q
            last = [None]
            for i in range(NT):
                b, bf = ps.take()
                s_ = banks[b][:, 0:256]
                t = mm(s_, pf(q)[:, i * P:(i + 1) * P], pf(kp)[:, half], True, True, bf, tq, tk, mark=True)
                st = stat(4)
                p, f = pg.take()
                t = rmax(st[:, 0:1], s_, t)
                t = ts(st[:, 1:2], st[:, 0:1], -sc, None, ALU.mult, None, t)
                yield
                t = fn(pf(p, 256), s_, ACT.Exp, t, f, bias=st[:, 1:2], scale=sc, acc=st[:, 2:3])
                ps.give(b, t)
                yield
                t = recip(st[:, 3:4], st[:, 2:3], t)
                t = ts(pf(p, 256), pf(p, 256), st[:, 3:4], None, ALU.mult, None, t)
                yield
                yield from weights_and_values(
                    [(pf(p, 256), p)], [t], 256,
                    lambda a, kb: (pf(vp)[:, half][:, kb * P:(kb + 1) * P], tv, slice(0, P)),
                    [ob], i, [of], last)
                yield
            pg.give(q, last[0])
            O[h] = split_pair(banks[ob][:, :], last[0])
            ps.give(ob, *O[h][2])

        def window_pair(l, j, q, k, v, O):
            sc = 64 ** -0.5
            (q, tq), (k, tk), (v, tv) = q, k, v
            ob, of = ps.take()
            last = [None, None]
            for n in range(NT):
                k0 = max(n - 1, 0) * P
                L = (n + 1) * P - k0
                tp, pgs = [], []
                for a in range(2):
                    b, bf = ps.take()
                    rows = slice(64 * a, 64 * a + 64)
                    t = mm(banks[b][:, 0:L], pf(q)[rows, n * P:(n + 1) * P], pf(k)[rows, k0:k0 + L],
                           True, True, bf, tq, tk, mark=True)
                    p, f = pg.take()
                    t = stt(pf(p, L), banks[b][:, 0:L], sc, C("band")[:, 2 * P - L:2 * P],
                            ALU.mult, ALU.add, t, f)
                    ps.give(b, t)
                    tp.append((p, t, col("sinks", l * 8 + 2 * j + a)))
                    pgs.append((pf(p, L), p))
                yield
                tp = yield from softmax_rows(tp, L)
                yield from weights_and_values(
                    pgs, tp, L,
                    lambda a, kb: (pf(v)[:, (k0 // P + kb) * P + 64 * a:(k0 // P + kb) * P + 64 * a + 64],
                                   tv, slice(64 * a, 64 * a + 64)),
                    [ob, ob], n, [of, of], last)
                yield
            pg.give(q, *last)
            O[j] = split_pair(banks[ob][:, :], *last)
            ps.give(ob, *O[j][2])

        def row_sums(gcols, tg, idx, prefix=False):
            b, bf = ps.take()
            s, sf = pg.take()
            tl = []
            for i in range(NT):
                g = gcols[:, idx(i):idx(i) + 1]
                tl.append(ts(pf(s)[:, i * P:(i + 1) * P], C("ones"), g, None, ALU.mult, None, sf, tg))
            for i in range(NT):
                o = banks[b][:, i * P:(i + 1) * P]
                pre = range(i) if prefix else ()
                t = mm(o, pf(s)[:, i * P:(i + 1) * P], C("upto"), True, not pre, bf, tl[i], mark=True)
                for j in pre:
                    t = mm(o, pf(s)[:, j * P:(j + 1) * P], C("ones"), False, j == i - 1, mark=True)
            pg.give(s, t)
            return b, t

        def softplus_of(v, n, scratch_cols, *tok):
            t = fn(scratch_cols, v, ACT.Abs, *tok)
            t = fn(scratch_cols, scratch_cols, ACT.Exp, t, scale=-1.0)
            yield
            t = fn(scratch_cols, scratch_cols, ACT.Ln, t, bias=ONE)
            return stt(v, v, 0.0, scratch_cols, ALU.max, ALU.add, t)

        def delta_branch(l, source, X, later):
            def conv(m):
                b, t = yield from product(("w_in", l), m, X)
                return short_conv(m, b, t)

            def short_conv(m, b, t):
                p, f = pg.take()
                w_ = lambda j: col("conv", (l * 4 + j) * 12 + m)
                t = fn(pf(p), banks[b][:, :], ACT.Copy, t, f, scale=w_(3))
                for sh in range(1, 4):
                    t = stt(pf(p)[:, sh:], banks[b][:, 0:SEQ - sh], w_(3 - sh), pf(p)[:, sh:],
                            ALU.mult, ALU.add, t)
                ps.give(b, t)
                z, f = pg.take()
                t = fn(pf(z), pf(p), ACT.Tanh, t, f, scale=0.5)
                return p, z, t

            (ba, t_ba), *convs = feed(source, [project_n(("w_in", l), 12, X, 8)] + [conv(m) for m in (0, 4, 8)])
            be, hbe, g, gc, ngc, eg, beg = (stat(16) for _ in range(7))
            D = {}

            def decays():
                ba3 = pf(ba, 32).rearrange("p (i c) -> p i c", c=8)
                ea, w1 = stat(4), stat(16)
                be3, g3 = be.rearrange("p (i h) -> p i h", h=4), g.rearrange("p (i h) -> p i h", h=4)
                t_be = fn(be3, ba3[:, :, 0:4], ACT.Tanh, t_ba, scale=0.5)
                for h in range(4):
                    tg = ts(g3[:, :, h:h + 1], ba3[:, :, 4 + h:5 + h], col("dt_bias", 4 * l + h), None,
                            ALU.add, None, t_ba)
                pg.give(ba, t_be, tg)
                a0 = PARAM_AT["a_log"][0] + 4 * l
                te = fn(ea, par[:, a0:a0 + 4], ACT.Exp)
                tg = yield from softplus_of(g, 16, w1, tg)
                t = ts(hbe, be, 0.25, 0.25, ALU.mult, ALU.add, t_be)
                D["be"] = t_be = ts(be, be, 0.5, 0.5, ALU.mult, ALU.add, t)
                D["hbe"] = t_be
                te = ts(ea, ea, -1.0, None, ALU.mult, None, te)
                for h in range(4):
                    tg = ts(g3[:, :, h:h + 1], g3[:, :, h:h + 1], ea[:, h:h + 1], None, ALU.mult, None, tg, te)
                D["g"] = tg
                yield
                b, bf = ps.take()
                t = mm(banks[b][:, 0:16], C("upto"), g, True, True, bf, tg, mark=True)
                D["gc"] = fn(gc, banks[b][:, 0:16], ACT.Copy, t)
                t_eg = fn(eg, banks[b][:, 0:16], ACT.Exp)
                ps.give(b, t_eg)
                D["ngc"] = ts(ngc, gc, -1.0, None, ALU.mult, None, D["gc"])
                D["beg"] = tt(beg, be, eg, ALU.mult, t_eg, t_be)

            def unit_length(pair):
                if pair == (0, 4):
                    yield
                v = []
                for m in pair:
                    p, t = qkv[m]
                    q, qf = pg.take()
                    t = fn(pf(q), pf(p), ACT.Square, t, qf)
                    v.append((m, p, q, t))
                yield
                for n_, (m, p, q, t) in enumerate(v):
                    b, bf = ps.take()
                    t = mm(banks[b][:, :], C("ones"), pf(q), True, True, bf, t, mark=True)
                    c, eps = (P * 0.25, EPS_Q) if m < 4 else (0.25, EPS_RMS)
                    t = fn(pf(q), banks[b][:, :], ACT.Ln, t, bias=eps, scale=c)
                    ps.give(b, t)
                    v[n_] = (m, p, q, t)
                yield
                for n_, (m, p, q, t) in enumerate(v):
                    v[n_] = (m, p, q, fn(pf(q), pf(q), ACT.Exp, t, scale=-0.5))
                for m, p, q, t in v:
                    t = stt(pf(p), pf(p), 0.5, pf(q), ALU.mult, ALU.mult, t)
                    pg.give(q, t)
                    qkv[m] = (p, t)

            qkv, waiting = {}, []

            def double_silu():
                while waiting:
                    m, (p, z, t) = waiting.pop(0)
                    t = stt(pf(p), pf(z), 1.0, pf(p), ALU.add, ALU.mult, t)
                    pg.give(z, t)
                    qkv[m] = (p, t)

            waiting += zip((0, 4, 8), convs)
            double_silu()
            tasks = [decays(), unit_length((0, 4))]

            def tend():
                for w in list(tasks):
                    try:
                        next(w)
                    except StopIteration:
                        tasks.remove(w)

            for m in (1, 5, 2, 6, 3, 7, 9, 10, 11):
                b, t = gemm_t(("w_in", l), m, X)
                double_silu()
                tend()
                if m in (2, 3, 9):
                    h = min(m, 4) - 1
                    tasks.append(unit_length((h, h + 4)))
                waiting.append((m, short_conv(m, b, t)))
            double_silu()
            later()
            tend()
            bg.steps(14)
            while tasks:
                bg.steps(4)
                tend()
            tg, t_gc, t_ngc, t_be, t_hbe, t_beg = (D[k] for k in ("g", "gc", "ngc", "be", "hbe", "beg"))

            ot = {}

            def four(f, *tok):
                b, bf = ps.take()
                for i in range(NT):
                    prods = f(i)
                    for n_, (x, y) in enumerate(prods):
                        t = mm(banks[b][:, i * P:(i + 1) * P], x, y, n_ == 0, n_ == len(prods) - 1,
                               bf, *tok, mark=(i == NT - 1 and n_ == len(prods) - 1))
                return b, t

            def T(p, i):
                return pf(p)[:, i * P:(i + 1) * P]

            def v4(ap):
                return ap.rearrange("p (i c) -> p i c", i=4)

            def bc(c):
                return C(c).rearrange("p (o c) -> p o c", o=1).broadcast_to([P, 4, P])

            def percol(s16, h):
                return s16.rearrange("p (i h) -> p i h", h=4)[:, :, h:h + 1].broadcast_to([P, 4, P])

            def head(h):
                q, tq = qkv[h]
                k, tk = qkv[4 + h]
                vv, tv = qkv[8 + h]
                gb, tgb = row_sums(g, tg, lambda i: 4 * i + h)
                d1, f1 = pg.take()
                d2, f2 = pg.take()
                e_, f3 = pg.take()
                G4 = v4(banks[gb][:, :])
                t1 = tt(v4(pf(d1)), bc("before"), G4, ALU.subtract, tgb, f1)
                t2 = tt(v4(pf(d2)), G4, bc("since"), ALU.add, tgb, f2)
                gl = stat(4)
                tgl = dve(lambda e, gl=gl, G4=G4: e.tensor_copy(gl, G4[:, :, P - 1:P]), tgb)
                t3 = fn(pf(e_), banks[gb][:, :], ACT.Exp, tgb, f3, tgl, t2)
                ps.give(gb, t3)
                ktl, egl = stat(4), stat(4)
                for i in range(NT):
                    c = 4 * i + h
                    td1 = fn(T(d1, i), T(d1, i), ACT.Exp, t1, bias=gc[:, c:c + 1])
                    td2 = fn(T(d2, i), T(d2, i), ACT.Exp, t2, t_ngc, bias=ngc[:, c:c + 1])
                    tkt = fn(ktl[:, i:i + 1], gl[:, i:i + 1], ACT.Exp, tgl, bias=ngc[:, c:c + 1])
                tegl = fn(egl, gl, ACT.Exp)
                yield
                b, bf = ps.take()
                for i in range(NT):
                    t = tr(banks[b][:, i * P:(i + 1) * P], T(k, i), bf, tk, mark=(i == 3))
                kbe, f1 = pg.take()
                tke, f2 = pg.take()
                vb, f3 = pg.take()
                t4 = tt(v4(pf(kbe)), v4(banks[b][:, :]), percol(beg, h), ALU.mult, t, f1, t_beg)
                kt3 = ktl.rearrange("p (i o) -> p i o", o=1).broadcast_to([P, 4, P])
                t5 = tt(v4(pf(tke)), v4(banks[b][:, :]), kt3, ALU.mult, f2, tkt)
                ps.give(b, t5)
                b, bf = ps.take()
                for i in range(NT):
                    t = tr(banks[b][:, i * P:(i + 1) * P], T(vv, i), bf, tv, mark=(i == 3))
                t6 = tt(v4(pf(vb)), v4(banks[b][:, :]), percol(hbe, h), ALU.mult, t, f3, t_hbe)
                ps.give(b, t6)
                pg.give(vv, t)
                yield
                b, t = four(lambda i: [(T(k, i), T(k, i))])
                t = tt(pf(d1), pf(d1), banks[b][:, :], ALU.mult, t, td1)
                ps.give(b, t)
                tA = tt(v4(pf(d1)), v4(pf(d1)), percol(be, h), ALU.mult, t)
                b, t = four(lambda i: [(T(k, i), T(q, i))], tq, tk)
                tQ = tt(pf(d2), pf(d2), banks[b][:, :], ALU.mult, t, td2)
                ps.give(b, tQ)
                pg.give(k, t)
                tqd = tt(pf(q), pf(q), pf(e_), ALU.mult, t, t3)
                pg.give(e_, tqd)
                yield
                b, bf = ps.take()
                for i in range(NT):
                    t = tr(banks[b][:, i * P:(i + 1) * P], T(d1, i), bf, tA, mark=(i == 3))
                at, f = pg.take()
                tAT = fn(pf(at), banks[b][:, :], ACT.Copy, t, f)
                ps.give(b, tAT)
                n1, f1 = pg.take()
                n1t, f2 = pg.take()
                ta = tt(v4(pf(n1)), v4(pf(d1)), bc("nblock8"), ALU.mult, tA, f1)
                pg.give(d1, ta, tAT)
                tb = tt(v4(pf(n1t)), v4(pf(at)), bc("nblock8"), ALU.mult, tAT, f2)
                x, f3 = pg.take()
                xt, f4 = pg.take()
                tx = tt(v4(pf(x)), v4(pf(n1)), bc("ident"), ALU.add, ta, f3)
                txt = tt(v4(pf(xt)), v4(pf(n1t)), bc("ident"), ALU.add, tb, f4)
                yield
                tn = [ta, tb]
                for lev in range(2):
                    b1, u1 = four(lambda i: [(T(n1t, i), T(n1, i))], tn)
                    if lev == 0:
                        b2, u2 = four(lambda i: [(T(n1, i), T(n1t, i))])
                        tb = dve(lambda e, b2=b2, n1t=n1t: e.tensor_copy(pf(n1t), banks[b2][:, :]), u2, u1, txt)
                        ps.give(b2, tb)
                    ta = fn(pf(n1), banks[b1][:, :], ACT.Copy, u1, u2, tx)
                    ps.give(b1, ta)
                    yield
                    tn = [ta, tb]
                    b1, u1 = four(lambda i: [(T(xt, i), T(n1, i))], tn, txt)
                    b2, u2 = four(lambda i: [(T(n1, i), T(xt, i))])
                    tx = tt(pf(x), pf(x), banks[b1][:, :], ALU.add, u1, tx)
                    txt = tt(pf(xt), pf(xt), banks[b2][:, :], ALU.add, u2, txt)
                    ps.give(b1, tx)
                    ps.give(b2, txt)
                    if lev == 0:
                        yield
                low, prod = n1, n1t
                tlast = u2
                t = tt(v4(pf(low)), v4(pf(at)), bc("low8"), ALU.mult, tlast, tAT)
                yield
                for size in (8, 16, 32, 64):
                    b1, u1 = four(lambda i: [(T(low, i), T(x, i))], t, tx)
                    tp = fn(pf(prod), banks[b1][:, :], ACT.Copy, u1, tlast)
                    ps.give(b1, tp)
                    if size < 64:
                        t = tt(v4(pf(low)), v4(pf(at)), bc(f"low{2 * size}"), ALU.mult, u1)
                    yield
                    b2, u2 = four(lambda i: [(T(prod, i), T(xt, i))], tp, txt)
                    if size < 64:
                        b1, u1 = four(lambda i: [(T(xt, i), T(prod, i))])
                        tx = tt(pf(x), pf(x), banks[b1][:, :], ALU.subtract, u1, tx)
                        ps.give(b1, tx)
                        u2 = u1
                    txt = tt(pf(xt), pf(xt), banks[b2][:, :], ALU.subtract, u2, txt)
                    ps.give(b2, txt)
                    tlast = u2
                    yield
                pg.give(n1t, tlast)
                pg.give(at, tlast)
                pg.give(x, tlast)
                wt, f = n1, None
                b, t = four(lambda i: [(T(kbe, i), T(xt, i))], t4, txt)
                twt = fn(pf(wt), banks[b][:, :], ACT.Copy, t, tlast, scale=-1.0)
                ps.give(b, twt)
                pg.give(kbe, t)
                yield
                S, f = pg.take()
                vn, f2 = pg.take()
                ob, of = ps.take()
                tS = None
                for i in range(NT):
                    b, bf = ps.take()
                    o = banks[b][:, 0:P]
                    t = mm(o, T(xt, i), T(vb, i), True, i == 0, bf, txt, t6, mark=True)
                    if i:
                        t = mm(o, T(wt, i), pf(S, P), False, True, twt, tS, mark=True)
                    tv_ = fn(T(vn, i), o, ACT.Copy, t, f2)
                    ps.give(b, tv_)
                    yield
                    oo = banks[ob][:, i * P:(i + 1) * P]
                    if i:
                        mm(oo, pf(S, P), T(q, i), True, False, of, tqd, tS)
                    to = mm(oo, T(vn, i), T(d2, i), i == 0, True, of, tv_, tQ, mark=True)
                    if i < NT - 1:
                        b, bf = ps.take()
                        o = banks[b][:, 0:P]
                        t = mm(o, T(tke, i), T(vn, i), True, True, bf, t5, mark=True)
                        if i == 0:
                            tS = dve(lambda e, o=o, S=S: e.tensor_copy(pf(S, P), o), t, f)
                        else:
                            tS = stt(pf(S, P), pf(S, P), egl[:, i:i + 1], o, ALU.mult, ALU.add, t, to, tegl)
                        ps.give(b, tS)
                        yield
                for z in (S, vn, xt, wt, vb, tke, d2, q):
                    pg.give(z, to, tS)
                o_, f = pg.take()
                t = fn(pf(o_), banks[ob][:, :], ACT.Copy, to, f)
                ps.give(ob, t)
                ot[h] = (o_, t)

            bg.weave([head(0), head(1)], 1)
            bg.weave([head(2), head(3)], 1)

            def finish():
                O, sq = {}, {}
                for h in range(4):
                    o_, t = ot[h]
                    q, qf = pg.take()
                    sq[h] = (q, fn(pf(q), pf(o_), ACT.Square, t, qf))
                yield
                for h in range(4):
                    q, t = sq[h]
                    b, bf = ps.take()
                    t = mm(banks[b][:, :], C("ones"), pf(q), True, True, bf, t, mark=True)
                    sq[h] = (q, fn(pf(q), banks[b][:, :], ACT.Ln, t, bias=EPS_4, scale=4.0 / P))
                    ps.give(b, sq[h][1])
                yield
                for h in range(4):
                    q, t = sq[h]
                    sq[h] = (q, fn(pf(q), pf(q), ACT.Exp, t, scale=-0.5))
                for h in range(4):
                    (o_, t), (q, tq) = ot[h], sq[h]
                    t2 = stt(pf(o_), pf(o_), col("dn_norm", l), pf(q), ALU.mult, ALU.mult, tq)
                    pg.give(q, t2)
                    b, t = yield from product(("w_in", l), 13 + h, X)
                    z, f = pg.take()
                    t3 = fn(pf(z), banks[b][:, :], ACT.Tanh, t, f, scale=0.5)
                    t3 = stt(pf(z), pf(z), 1.0, banks[b][:, :], ALU.add, ALU.mult, t3)
                    ps.give(b, t3)
                    t = tt(pf(o_), pf(o_), pf(z), ALU.mult, t2, t3)
                    pg.give(z, t)
                    O[h] = split_pair(pf(o_), t)
                    pg.give(o_, *O[h][2])
                return joined(O)

            return finish

        t_bw = []

        def bias_rows():
            t = dve(lambda e: e.memset(tab[:, :], NEG))
            t_tab = sp.dma(tab[0:32, :], table, s_tab, 16, t)
            oh0, f0 = pg.take()
            oh1, f1 = pg.take()
            t_oh = sp.dma(pf(oh0)[0:33, :], buckets[:, 0:512], s_oh, 16, f0)
            t_oh = sp.dma(pf(oh1)[0:33, 0:128], buckets[:, 512:640], s_oh, 32, f1)
            yield
            for h in range(8):
                th, f = pg.take()
                t1 = ts(pf(th)[0:33, 0:P], C("ones")[0:33, :], tab[:, h:h + 1], None, ALU.mult, None, f, t, t_tab)
                yield
                b, bf = ps.take()
                b2, bf2 = ps.take()
                mm(banks[b][:, :], pf(th)[0:33, 0:P], pf(oh0)[0:33, :], True, True, bf, bf2, t1, t_oh)
                t1 = mm(banks[b2][:, 0:P], pf(th)[0:33, 0:P], pf(oh1)[0:33, 0:P], True, True, mark=True)
                pg.give(th, t1)
                bb, f2 = pg.take()
                bb2, f3 = pg.take()
                t2 = fn(pf(bb), banks[b][:, :], ACT.Copy, t1, f2)
                t3 = fn(pf(bb2, P), banks[b2][:, 0:P], ACT.Copy, t1, f3)
                ps.give(b, t2)
                ps.give(b2, t3)
                yield
                sp.dma(scratch[h, :, 0:512], pf(bb), s_bw[h], 16, t2)
                t_bw.append(sp.dma(scratch[h, :, 512:640], pf(bb2, P), s_bw[h], 32, t3))
                pg.give(bb, t_bw[h])
                pg.give(bb2, t_bw[h])
            pg.give(oh0, t1)
            pg.give(oh1, t1)

        for l in range(DEPTH):
            if l == 0:
                mem = bg.add(prepare_memory())
                st = ffn(source, X, ("ffn1_gu", l), ("ffn1_down", l), 0.5)
                bg.get(mem)
            else:
                st = ffn(source, X, ("ffn1_gu", l), ("ffn1_down", l), 0.5)
            X = Act(DT)
            source = residual_norm(X, st, 3 * l, ALPHA)
            mg = Merge(X, ("gates", l), lambda n: ("w_branch", l, n))
            ahead_ = {}

            def attention_projections():
                for h in range(4):
                    ahead_["x", h] = bg.add(project(("w_in", l), 23 + h, X))
                for j in range(4):
                    ahead_["s", j] = bg.add(project(("w_in", l), 17 + j, X))
                ahead_["k"] = bg.add(project(("w_in", l), 21, X))
                ahead_["v"] = bg.add(project_n(("w_in", l), 22, X))

            finish = delta_branch(l, source, X, attention_projections)
            got = {k: bg.get(v) for k, v in ahead_.items()}

            def first_branch():
                O = yield from finish()
                yield from mg.add(0, O)

            merge0 = bg.add(first_branch())
            OX, OS = {}, {}

            def crosses(h0):
                for h in (h0, h0 + 1):
                    yield from cross_head(l, h, got["x", h], OX)

            def windows(j0):
                for j in (j0, j0 + 1):
                    yield from window_pair(l, j, got["s", j], got["k"], got["v"], OS)

            bg.weave([crosses(0), windows(0), crosses(2), windows(2)], 1)
            for p, t in mem_k[l] + mem_v[l] + [got["k"], got["v"]]:
                pg.give(p, (pe.sem, pe.n))
            bg.get(merge0)
            go(mg.add(2, joined(OX)))
            go(mg.add(1, joined(OS), final=True))
            drop(X, (pe.sem, pe.n))
            Y = mg.result()
            st = update(("w_out", l), Y, 1.0, Spread(summed=False))
            X = Act(DT)
            source = residual_norm(X, st, 3 * l + 1, ALPHA)
            st = ffn(source, X, ("ffn2_gu", l), ("ffn2_down", l), 0.5)
            if l < DEPTH - 1:
                X = Act(DT)
                source = residual_norm(X, st, 3 * l + 2, ALPHA)

        rows = bg.add(bias_rows())
        X = Act(DT)
        source = rms_norm(X, "norm_mix", last_norm(st, 3 * DEPTH - 1))

        def bias_tiles(hs):
            out_ = {}
            for h in hs:
                p, f = pg.take()
                src = bass.AP(tensor=scratch.tensor, offset=h * 640 * P + 127, ap=[[639, P], [1, 512]])
                out_[h] = (p, sp.dma(pf(p), src, s_tb[h], 16, t_bw[h], f))
            return out_

        sc = 64 ** -0.5
        mg = Merge(X, "w_gate_2", lambda n: ("w_branch_2", n))

        def stick_breaking(jt, q, k, v, O):
            (q, tq), (k, tk), (v, tv) = q, k, v
            ob, of = ps.take()
            last = []
            for a in range(2):
                rows = slice(64 * a, 64 * a + 64)
                zp, ap_, tz, ta_ = [], [], [], []
                for i in range(NT):
                    W = SEQ - i * P
                    b, bf = ps.take()
                    t = mm(banks[b][:, 0:W], pf(k)[rows, i * P:(i + 1) * P], pf(q)[rows, i * P:SEQ],
                           True, True, bf, tq, tk, mark=True)
                    z, fz = pg.take()
                    s, fs = pg.take()
                    t1 = ts(pf(z, W), banks[b][:, 0:W], sc, None, ALU.mult, None, t, fz)
                    ps.give(b, t1)
                    t = fn(pf(s, W), pf(z, W), ACT.Abs, t1, fs)
                    ta_.append(fn(pf(s, W), pf(s, W), ACT.Exp, t, scale=-1.0))
                    zp.append(z)
                    ap_.append(s)
                    yield
                for i in range(NT):
                    W = SEQ - i * P
                    ta_[i] = fn(pf(ap_[i], W), pf(ap_[i], W), ACT.Ln, ta_[i], bias=ONE)
                yield
                for i in range(NT):
                    W, z, s = SEQ - i * P, zp[i], ap_[i]
                    t = stt(pf(s, W), pf(z, W), 0.0, pf(s, W), ALU.max, ALU.add, ta_[i])
                    t1 = tt(pf(z, W), pf(z, W), pf(s, W), ALU.subtract, t)
                    ta_[i] = tt(pf(s, P), pf(s, P), C("later"), ALU.mult, t1)
                    tz.append(t1)
                    yield 2
                for i in range(NT):
                    W = SEQ - i * P
                    b, bf = ps.take()
                    t = mm(banks[b][:, 0:W], C("ntri"), pf(ap_[i], W), True, i == NT - 1, bf, ta_, mark=True)
                    for j in range(i + 1, NT):
                        t = mm(banks[b][:, (j - i) * P:W], C("nones"), pf(ap_[j], SEQ - j * P),
                               False, j == NT - 1, mark=True)
                    t = tt(pf(zp[i], W), pf(zp[i], W), banks[b][:, 0:W], ALU.add, t, tz[i])
                    ps.give(b, t)
                    t = fn(pf(zp[i], W), pf(zp[i], W), ACT.Exp, t)
                    tz[i] = tt(pf(zp[i], P), pf(zp[i], P), C("later"), ALU.mult, t)
                    yield
                for i in range(NT):
                    W = SEQ - i * P
                    t = mm(banks[ob][rows, i * P:SEQ], pf(v)[:, i * P + 64 * a:i * P + 64 * a + 64],
                           pf(zp[i], W), i == 0, i == NT - 1, of, tz[i], tv, mark=True)
                for i in range(NT):
                    pg.give(zp[i], t)
                    pg.give(ap_[i], t)
                last.append(t)
                yield
            O[jt] = split_pair(banks[ob][:, :], last)
            ps.give(ob, *O[jt][2])
            for p in (q, k, v):
                pg.give(p, *last)

        def causal_softmax(jt, q, k, vof, bias, O):
            (q, tq), (k, tk) = q, k
            ob, of = ps.take()
            last = [None, None]
            for i in range(NT):
                L = (i + 1) * P
                tp, pgs = [], []
                for a in range(2):
                    rows = slice(64 * a, 64 * a + 64)
                    b, bf = ps.take()
                    t = mm(banks[b][:, 0:L], pf(q)[rows, i * P:(i + 1) * P], pf(k)[rows, 0:L],
                           True, True, bf, tq, tk, mark=True)
                    p, f = pg.take()
                    adds, after = bias(2 * jt + a, i, L)
                    t = stt(pf(p, L), banks[b][:, 0:L], sc, adds[0][0], ALU.mult, ALU.add, t, f, adds[0][1])
                    ps.give(b, t)
                    for ap_, tok in adds[1:]:
                        t = tt(pf(p, L), pf(p, L), ap_, ALU.add, t, tok)
                    after(t)
                    tp.append((p, t, None))
                    pgs.append((pf(p, L), p))
                yield
                tp = yield from softmax_rows(tp, L)
                yield from weights_and_values(pgs, tp, L, lambda a, kb: vof(2 * jt + a, kb),
                                              [ob, ob], i, [of, of], last)
                yield
            O[jt] = split_pair(banks[ob][:, :], *last)
            ps.give(ob, *O[jt][2])
            pg.give(q, *last)

        def proj(m):
            return project("w_in_2", m, X)

        (nar, t_nar), *ix = feed(source, [project_n("w_in_2", 23, X)] + [proj(m) for m in (20, 21, 22)],
                                 lambda: bg.steps(6))

        def narrow(i, c0, n):
            return pf(nar)[:, i * P + c0:i * P + c0 + n]

        ixq, (ixk, t_ixk) = ix[:2], ix[2]
        pen = [None]

        def best_keys():
            for i in range(1, NT):
                L = (i + 1) * P
                s, fs = pg.take()
                for h in range(8):
                    rows = slice(32 * (h % 4), 32 * (h % 4) + 32)
                    q, tq = ixq[h // 4]
                    b, bf = ps.take()
                    t = mm(banks[b][:, 0:L], pf(q)[rows, i * P:(i + 1) * P], pf(ixk)[rows, 0:L],
                           True, True, bf, tq, t_ixk, mark=True)
                    r, fr = pg.take()
                    tr1 = fn(pf(r, L), banks[b][:, 0:L], ACT.Relu, t, fr)
                    ps.give(b, tr1)
                    wc = narrow(i, 68 + h, 1)
                    if h == 0:
                        t2 = ts(pf(s, L), pf(r, L), wc, 0.0, ALU.mult, ALU.add, tr1, fs, t_nar)
                    else:
                        t2 = stt(pf(s, L), pf(r, L), wc, pf(s, L), ALU.mult, ALU.add, tr1, t2)
                    pg.give(r, t2)
                    if h % 2:
                        yield
                d = pf(s)[:, L - P:L]
                t2 = tt(d, d, C("causal"), ALU.add, t2)
                t8 = stat(8)
                for r_ in range(16):
                    t3 = dve(lambda e, s=s, L=L, t8=t8: e.max(t8, pf(s, L)), t2)
                    t2 = dve(lambda e, s=s, L=L, t8=t8: e.match_replace(pf(s, L), t8, pf(s, L), TAKEN), t3)
                    yield
                t2 = ts(pf(s, L), pf(s, L), TAKEN, NEG, ALU.not_equal, ALU.mult, t2)
                pen.append((s, t2))
            for p in [x[0] for x in ixq] + [ixk]:
                pg.give(p, t)

        sq = [go(proj(m)) for m in (0, 1)]
        sk = [go(proj(m)) for m in (2, 3)]
        sv = [go(project_n("w_in_2", m, X)) for m in (4, 5)]
        OSB = {}
        mq = [bg.add(proj(m)) for m in (6, 7)]
        mk = [bg.add(proj(m)) for m in (8, 9)]
        mv = [bg.add(project_n("w_in_2", m, X)) for m in (10, 11)]
        fq = [bg.add(proj(m)) for m in (12, 13)]
        fk = [bg.add(proj(m)) for m in (14, 15)]
        fv = [bg.add(project_n("w_in_2", m, X)) for m in (16, 17)]
        keys = Later(best_keys())
        bg.weave([stick_breaking(0, sq[0], sk[0], sv[0], OSB), stick_breaking(1, sq[1], sk[1], sv[1], OSB)], N_SB, keys)
        mq, mk, mv, fq, fk, fv = ([bg.get(x) for x in y] for y in (mq, mk, mv, fq, fk, fv))
        dq = [bg.add(proj(m)) for m in (18, 19)]
        dk = bg.add(proj(24))
        merges = [bg.add(mg.add(0, joined(OSB)))]
        tbs = bias_tiles(range(4))

        def v_of(vs):
            def f(h, kb):
                v, tv = vs[h // 2]
                a = h % 2
                return pf(v)[:, kb * P + 64 * a:kb * P + 64 * a + 64], tv, slice(64 * a, 64 * a + 64)
            return f

        def t5(tbs, h0):
            def f(h, i, L):
                p, t = tbs[h0 + h]
                return [(pf(p)[:, 384 - P * i:384 - P * i + L], t)], lambda t: None
            return f

        fl, w1, cc = stat(16), stat(16), stat(16)
        fl3 = fl.rearrange("p (i h) -> p i h", h=4)
        for i in range(NT):
            a0 = PARAM_AT["fox"][0]
            t = tt(fl3[:, i, :], narrow(i, 64, 4), par[:, a0:a0 + 4], ALU.add, t_nar)
        t = ts(fl, fl, -1.0, None, ALU.mult, None, t)
        t = go(softplus_of(fl, 16, w1, t))
        b, bf = ps.take()
        for i in range(NT):
            o = banks[b][:, 4 * i:4 * i + 4]
            tc = mm(o, C("upto"), fl[:, 4 * i:4 * i + 4], True, i == 0, bf, t, mark=True)
            for j in range(i):
                tc = mm(o, C("ones"), fl[:, 4 * j:4 * j + 4], False, j == i - 1, mark=True)
        t_cc = fn(cc, banks[b][:, 0:16], ACT.Copy, tc, scale=-1.0)
        ps.give(b, t_cc)
        crow = []
        for h in range(4):
            b, tb = row_sums(fl, t, lambda i: 4 * i + h, prefix=True)
            p, f = pg.take()
            tb = fn(pf(p), banks[b][:, :], ACT.Copy, tb, f)
            ps.give(b, tb)
            crow.append((p, tb))
            bg.steps(4)

        def fox(h, i, L):
            p, t = crow[h]
            q, f = pg.take()
            t = ts(pf(q, L), pf(p, L), cc[:, 4 * i + h:4 * i + h + 1], None, ALU.add, None, t, t_cc, f)
            d = pf(q)[:, L - P:L]
            t = tt(d, d, C("causal"), ALU.add, t)
            return [(pf(q, L), t)], lambda t: pg.give(q, t)

        def dsa(tbs):
            def f(h, i, L):
                adds, _ = t5(tbs, 4)(h, i, L)
                if i:
                    adds.append((pf(pen[i][0], L), pen[i][1]))
                return adds, lambda t: None
            return f

        OMB, OFX, ODS = {}, {}, {}

        bg.weave([causal_softmax(jt, mq[jt], mk[jt], v_of(mv), t5(tbs, 0), OMB) for jt in range(2)], N_MB, keys)
        for p, _ in mk + mv + list(tbs.values()):
            pg.give(p, (pe.sem, pe.n), (dve.sem, dve.n))
        merges.append(bg.add(mg.add(1, joined(OMB))))
        bg.weave([causal_softmax(jt, fq[jt], fk[jt], v_of(fv), fox, OFX) for jt in range(2)], N_FX, keys)
        for p, _ in fk + fv + crow:
            pg.give(p, (pe.sem, pe.n), (dve.sem, dve.n))
        merges.append(bg.add(mg.add(2, joined(OFX))))
        while not keys.done:
            keys.step()
            bg.steps(2)
        tbs = bias_tiles(range(4, 8))
        dq, dk = [bg.get(x) for x in dq], bg.get(dk)
        f_ = dsa(tbs)
        vd = lambda h, kb: (narrow(kb, 0, 64), t_nar, slice(64 * (h % 2), 64 * (h % 2) + 64))
        bg.weave([causal_softmax(jt, dq[jt], dk, vd, f_, ODS) for jt in range(2)], N_DS)
        for p, _ in [dk] + pen[1:] + list(tbs.values()):
            pg.give(p, (pe.sem, pe.n), (dve.sem, dve.n))
        pg.give(nar, (pe.sem, pe.n), (dve.sem, dve.n))
        for m_ in merges:
            bg.get(m_)
        go(mg.add(3, joined(ODS), final=True))
        drop(X, (pe.sem, pe.n))
        Y = mg.result()
        st = update("w_out_2", Y, 1.0, Squares())

        X = Act(DT)
        source = rms_norm(X, "norm_ffn", st)
        H = Act()
        first = dict(zip((0, FT, 1, FT + 1), feed(source, [product("w_up_2", m, X) for m in (0, FT, 1, FT + 1)])))
        for j in range(FT):
            parts = []
            for m in (j, FT + j):
                b, t = first.get(m) or gemm_t("w_up_2", m, X)
                p, f = pg.take()
                w_ = lambda jj: col("conv2", jj * 2 * FT + m)
                t = fn(pf(p), banks[b][:, :], ACT.Identity, t, f, scale=w_(2), bias=col("conv2_b", m))
                for sh in (1, 2):
                    t = stt(pf(p)[:, sh:], banks[b][:, 0:SEQ - sh], w_(2 - sh), pf(p)[:, sh:],
                            ALU.mult, ALU.add, t)
                ps.give(b, t)
                parts.append((p, t))
            if j == FT - 1:
                drop(X, (pe.sem, pe.n))
            (g_, tg), (u_, tu) = parts
            t = fn(pf(g_), pf(g_), ACT.Gelu, tg)
            t = tt(pf(g_), pf(g_), pf(u_), ALU.mult, t, tu)
            pg.give(u_, t)
            t = split_into(H, pf(g_), t)
            pg.give(g_, *t)
        r, t = update("w_down_2", H, 1.0, Squares()).rstd()
        for m in range(8):
            t1 = stt(pf(R[m]), pf(R[m]), col("norm_final", m), pf(r), ALU.mult, ALU.mult, t, Rt[m])
            t_out = sp.dma(out[m], pf(R[m]), s_out, 16 * (m + 1), t1)
        sp.wait(t_out)

        assert state["block"] <= 8 * NSLAB and state["block"] > 8 * (NSLAB - 1), state

        block_ = ctx.enter_context(nc.Block())
        for name, line in (("sync", sp), ("tensor", pe), ("scalar", act), ("vector", dve), ("gpsimd", pool)):
            if line.ops:
                on_engine(block_, name)(line.emit)
    return order


def on_engine(block_, name):
    return {"sync": block_.sync, "tensor": block_.tensor, "scalar": block_.scalar,
            "vector": block_.vector, "gpsimd": block_.gpsimd}[name]



def pad_cols(a, n):
    return np.concatenate([a, np.zeros((a.shape[0], n - a.shape[1]), a.dtype)], axis=1)


def matrices(inp):
    m = {}
    pairs = np.concatenate([np.r_[64 * j:64 * j + 64, 64 * (j + 4):64 * (j + 4) + 64] for j in range(4)])
    for l in range(DEPTH):
        m[("ffn1_gu", l)] = inp["ffn1_w_gu"][l]
        m[("ffn2_gu", l)] = inp["ffn2_w_gu"][l]
        m[("ffn1_down", l)] = inp["ffn1_w_down"][l]
        m[("ffn2_down", l)] = inp["ffn2_w_down"][l]
        w = inp["w_in"][l]
        m[("w_in", l)] = np.concatenate([
            w[:, 0:1536], pad_cols(w[:, 1536:1544], P), w[:, 1544:2056], w[:, 2056:2568][:, pairs],
            w[:, 2568:2824], w[:, 2824:3336]], axis=1)
        m[("gates", l)] = w[:, 3336:6408]
        m[("w_mem_kv", l)] = inp["w_mem_kv"][l]
        for n in range(3):
            b = inp["w_branch"][l, n]
            m[("w_branch", l, n)] = b[pairs] if n == 1 else b
        m[("w_out", l)] = inp["w_out"][l]
    w = inp["w_in_2"][0]
    sb, mb, fx, ds = w[:, 0:768], w[:, 768:1536], w[:, 1536:2308], w[:, 2308:]
    m["w_in_2"] = np.concatenate([
        sb, mb, fx[:, 0:768], ds[:, 0:256], ds[:, 384:640],
        ds[:, 640:672], ds[:, 640:672], ds[:, 640:672], ds[:, 640:672],
        pad_cols(np.concatenate([ds[:, 320:384], fx[:, 768:772], ds[:, 672:680]], axis=1), P),
        ds[:, 256:320], ds[:, 256:320]], axis=1)
    m["w_gate_2"] = np.concatenate([inp["w_gate_2"][0, n] for n in range(4)], axis=1)
    for n in range(4):
        m[("w_branch_2", n)] = inp["w_branch_2"][0, n]
    m["w_out_2"] = inp["w_out_2"][0]
    m["w_up_2"] = inp["w_up_2"][0]
    m["w_down_2"] = inp["w_down_2"][0]
    return m


def cols(a):
    return np.ascontiguousarray(a.reshape(-1, P).T)


def over_rows(a):
    return np.broadcast_to(a.reshape(1, -1), (P, a.size))


def kernel(**inputs):
    import concourse.bacc as _bacc
    from concourse.bass_utils import run_bass_kernel_spmd as _run

    inp = {k: np.ascontiguousarray(v) for k, v in inputs.items()}
    nc = _bacc.Bacc("TRN2", target_bir_lowering=False, num_devices=1)

    def dram(name, shape, kind="ExternalInput"):
        return nc.dram_tensor(name, shape, F32, kind=kind).ap()

    args = [
        dram("weights", (NSLAB, P, 1024)), dram("x_t", (8, P, SEQ)), dram("mem_t", (8, P, NMEM)),
        dram("consts", (P, NCONST)), dram("params", (P, NPARAM)), dram("table", (32, 8)),
        dram("buckets", (33, 640)), dram("out_t", (8, P, SEQ), "ExternalOutput"),
    ]
    order = hybrid_then_mixer_program(nc, *args)

    mats = matrices(inp)
    weights = np.zeros((NSLAB, P, 8, P), np.float32)
    for n, (mat, mt, kt) in enumerate(order):
        weights[n // 8, :, n % 8, :] = mats[mat][kt * P:(kt + 1) * P, mt * P:(mt + 1) * P]
    sinks = inp["swa_sinks"].reshape(DEPTH, 2, 4).transpose(0, 2, 1)
    params = np.concatenate([
        cols(inp["mem_ln_g"]), cols(inp["mem_ln_b"]), cols(inp["ln_g"]), cols(inp["ln_b"]),
        cols(inp["dn_conv_w"]), cols(inp["dn_norm_w"]), over_rows(sinks), over_rows(inp["dn_a_log"]),
        over_rows(inp["dn_dt_bias"]), cols(inp["norm_mix_g_2"]), cols(inp["norm_ffn_g_2"]),
        cols(inp["norm_final_g_2"]), over_rows(inp["fox_b_f_2"]), cols(inp["conv_w_2"]), cols(inp["conv_b_2"]),
    ], axis=1)
    arrays = {
        "weights": weights.reshape(NSLAB, P, 1024),
        "x_t": np.ascontiguousarray(inp["x"][0].T).reshape(8, P, SEQ),
        "mem_t": np.ascontiguousarray(inp["mem"][0].T).reshape(8, P, NMEM),
        "consts": np.concatenate(list(const_tables().values()), axis=1),
        "params": np.ascontiguousarray(params),
        "table": inp["t5_bias_2"],
        "buckets": bucket_rows(),
    }
    r = _run(nc, [arrays], core_ids=[0])
    got = r.results[0]["out_t"]
    return np.ascontiguousarray(got.reshape(DM, SEQ).T).reshape(1, SEQ, DM)
```
